# Optimizing a Trainium2 kernel written in Bass

```python
import jax, jax.numpy as jnp
from jax import lax
import numpy as np

D_MODEL = 1024
BATCH = 1
SEQ = 256
DEPTH = 2
DEC_BATCH = 1
DEC_SEQ = 256
PAST_LEN = 128

GRID_W = 64
N_MIXERS = 2
N_RWKV = (DEPTH + 1) // 2
N_ATTN = DEPTH // 2
RW_HEAD = 64
RW_HEADS = D_MODEL // RW_HEAD
LORA_W = 64
LORA_A = 64
LORA_V = 32
LORA_G = 128
GN_EPS = 64e-5
AT_HEAD = 128
AT_QH = D_MODEL // AT_HEAD
AT_KVH = 2
AT_GROUP = AT_QH // AT_KVH
Q_BLOCK = 128
ROPE_THETA = 10000.0
D_FF = 2816
NORM_EPS = 1e-6
F32 = jnp.float32

kernel_name = 'hybrid_rwkv7_axial_gqa_encoder'

def _rmsnorm(x, g, eps=NORM_EPS):
    xf = x.astype(F32)
    y = xf * lax.rsqrt(jnp.mean(xf * xf, axis=-1, keepdims=True) + eps)
    return (y * g.astype(F32)).astype(x.dtype)

def _shift_prev(z):
    return jnp.pad(z[:, :-1], ((0, 0), (1, 0), (0, 0)))

def _shift_next(z):
    return jnp.pad(z[:, 1:], ((0, 0), (0, 1), (0, 0)))

def _wkv_scan(r, w, k, v, a, b, reverse):
    Bn, T, H, N = r.shape
    xs = tuple(jnp.moveaxis(z, 1, 0) for z in (r, w, k, v, a, b))

    def step(S, inp):
        r_t, w_t, k_t, v_t, a_t, b_t = inp
        sa = jnp.einsum('bhij,bhj->bhi', S, a_t)
        S = S * w_t[:, :, None, :] + sa[..., None] * b_t[:, :, None, :] + v_t[..., None] * k_t[:, :, None, :]
        return S, jnp.einsum('bhij,bhj->bhi', S, r_t)

    S0 = jnp.zeros((Bn, H, N, N), F32)
    _, ys = lax.scan(step, S0, xs, reverse=reverse)
    return jnp.moveaxis(ys, 0, 1)

def _rwkv_mixer(h, v_first, mu, w_rkv, w0, wA, wB, a0, aA, aB, gA, gB, k_k, k_a, r_k, lnx, w_o, vres):
    Bn, T, D = h.shape
    H, N = RW_HEADS, RW_HEAD
    xx = 0.5 * (_shift_prev(h) + _shift_next(h)) - h
    xr, xw, xk, xv, xa, xg = (h + xx * mu[i] for i in range(6))
    rkv = jnp.einsum('nbtd,nde->nbte', jnp.stack([xr, xk, xv]), w_rkv)
    r, k, v = rkv[0], rkv[1], rkv[2]
    if vres is None:
        v_first = v
    else:
        v0, vA, vB = vres
        v = v + (v_first - v) * jax.nn.sigmoid(v0 + (xv @ vA) @ vB)
    w_log = w0[:, None, None, :] + jnp.einsum('nbtr,nrd->nbtd', jnp.tanh(jnp.einsum('btd,ndr->nbtr', xw, wA)), wB)
    w_log = -jax.nn.softplus(-w_log.astype(F32)) - 0.5
    decay = jnp.exp(-jnp.exp(w_log))
    a = jax.nn.sigmoid(a0[:, None, None, :] + jnp.einsum('nbtr,nrd->nbtd', jnp.einsum('btd,ndr->nbtr', xa, aA), aB))
    g = jax.nn.sigmoid(xg @ gA) @ gB
    kk = (k * k_k).reshape(Bn, T, H, N).astype(F32)
    kk = kk / jnp.maximum(jnp.sqrt(jnp.sum(kk * kk, axis=-1, keepdims=True)), 1e-12)
    kd = k[None] * (1 + (a - 1) * k_a)

    def hv(z):
        return z.reshape(z.shape[:-1] + (H, N)).astype(F32)

    r4, v4, a4, kd4, dec4 = hv(r), hv(v), hv(a), hv(kd), hv(decay)
    y = (_wkv_scan(r4, dec4[0], kd4[0], v4, -kk, kk * a4[0], reverse=False)
         + _wkv_scan(r4, dec4[1], kd4[1], v4, -kk, kk * a4[1], reverse=True))
    mean = jnp.mean(y, axis=-1, keepdims=True)
    var = jnp.mean(jnp.square(y - mean), axis=-1, keepdims=True)
    yn = (y - mean) * lax.rsqrt(var + GN_EPS)
    yn = yn * lnx[0].astype(F32).reshape(H, N) + lnx[1].astype(F32).reshape(H, N)
    bonus = jnp.sum(r4 * (kd4[0] + kd4[1]) * r_k.astype(F32), axis=-1, keepdims=True) * v4
    o = (yn + bonus).reshape(Bn, T, D).astype(h.dtype) * g
    return o @ w_o, v_first

def _axial_rope(T):
    rows = T // GRID_W
    row, col = jnp.meshgrid(jnp.arange(rows), jnp.arange(GRID_W), indexing='ij')
    row = row.reshape(-1).astype(F32)
    col = col.reshape(-1).astype(F32)
    n_pair = AT_HEAD // 4
    inv = ROPE_THETA ** (-jnp.arange(n_pair, dtype=F32) / n_pair)
    ang = jnp.concatenate([row[:, None] * inv, col[:, None] * inv], axis=-1)
    return jnp.cos(ang), jnp.sin(ang)

def _apply_rope(x, cos, sin):
    xf = x.astype(F32).reshape(x.shape[:-1] + (-1, 2))
    x0, x1 = xf[..., 0], xf[..., 1]
    c = cos[None, :, None, :]
    s = sin[None, :, None, :]
    out = jnp.stack([x0 * c - x1 * s, x0 * s + x1 * c], axis=-1).reshape(x.shape)
    return out.astype(x.dtype)

def _gqa_mixer(h, w_qkv, qk_g, w_o, cos, sin):
    Bn, T, D = h.shape
    nq, nk = AT_QH * AT_HEAD, AT_KVH * AT_HEAD
    qkv = h @ w_qkv
    q = qkv[..., :nq].reshape(Bn, T, AT_QH, AT_HEAD)
    k = qkv[..., nq:nq + nk].reshape(Bn, T, AT_KVH, AT_HEAD)
    v = qkv[..., nq + nk:].reshape(Bn, T, AT_KVH, AT_HEAD)
    q = _apply_rope(_rmsnorm(q, qk_g[0]), cos, sin)
    k = _apply_rope(_rmsnorm(k, qk_g[1]), cos, sin)
    scale = AT_HEAD ** -0.5
    qb = q.reshape(Bn, T // Q_BLOCK, Q_BLOCK, AT_KVH, AT_GROUP, AT_HEAD).transpose(1, 0, 2, 3, 4, 5)

    def block(qi):
        s = jnp.einsum('bqhgd,bkhd->bhgqk', qi, k).astype(F32) * scale
        p = jax.nn.softmax(s, axis=-1).astype(v.dtype)
        return jnp.einsum('bhgqk,bkhd->bqhgd', p, v)

    o = lax.map(block, qb)
    o = o.transpose(1, 0, 2, 3, 4, 5).reshape(Bn, T, D)
    return o @ w_o

def _conv_ffn(h, w_up, conv_w, conv_b, w_down):
    u, gv = jnp.split(h @ w_up, 2, axis=-1)
    u = conv_w[0] * _shift_prev(u) + conv_w[1] * u + conv_w[2] * _shift_next(u) + conv_b
    return (jax.nn.silu(u) * gv) @ w_down

def _trunk(x, c, P):
    cos, sin = _axial_rope(x.shape[1])
    sc = jax.nn.silu(c)
    v_first = None
    for l in range(DEPTH):
        mod = sc @ P['ada_w'][l] + P['ada_b'][l]
        sh_m, sc_m, g_m, sh_f, sc_f, g_f = (m[:, None, :] for m in jnp.split(mod, 6, axis=-1))
        ng = P['norm_g'][l]
        h = _rmsnorm(x, ng[0]) * (1 + sc_m) + sh_m
        j = l // N_MIXERS
        if l % N_MIXERS == 0:
            vres = None if j == 0 else (P['rw_v0'][j - 1], P['rw_vA'][j - 1], P['rw_vB'][j - 1])
            out, v_first = _rwkv_mixer(h, v_first, P['rw_mu'][j], P['rw_rkv'][j], P['rw_w0'][j], P['rw_wA'][j],
                                       P['rw_wB'][j], P['rw_a0'][j], P['rw_aA'][j], P['rw_aB'][j], P['rw_gA'][j],
                                       P['rw_gB'][j], P['rw_kk'][j], P['rw_ka'][j], P['rw_rk'][j], P['rw_lnx'][j],
                                       P['rw_o'][j], vres)
        else:
            out = _gqa_mixer(h, P['at_qkv'][j], P['at_qk_g'][j], P['at_o'][j], cos, sin)
        x = x + g_m * _rmsnorm(out, ng[1])
        h = _rmsnorm(x, ng[2]) * (1 + sc_f) + sh_f
        f = _conv_ffn(h, P['ffn_up'][l], P['ffn_conv_w'][l], P['ffn_conv_b'][l], P['ffn_down'][l])
        x = x + g_f * _rmsnorm(f, ng[3])
    return x

def setup_inputs(seed: int = 0) -> dict:
    key = jax.random.key(seed)
    ks = iter(jax.random.split(key, 48))
    D, F, H, N = D_MODEL, D_FF, RW_HEADS, RW_HEAD
    NR, NA = N_RWKV, N_ATTN

    def nrm(shape, scale):
        return jax.random.normal(next(ks), shape, F32) * scale

    def uni(shape, lo, hi):
        return jax.random.uniform(next(ks), shape, F32, lo, hi)

    qkv_w = (AT_QH + 2 * AT_KVH) * AT_HEAD
    return {
        'x_prompt': nrm((BATCH, SEQ, D), 1.0),
        'x_sample': nrm((DEC_BATCH, DEC_SEQ, D), 1.0),
        'c_prompt': nrm((BATCH, D), 1.0),
        'c_sample': nrm((DEC_BATCH, D), 1.0),
        'ada_w': nrm((DEPTH, D, 6 * D), 0.5 * D ** -0.5),
        'ada_b': nrm((DEPTH, 6 * D), 0.02),
        'norm_g': 1.0 + nrm((DEPTH, 4, D), 0.02),
        'rw_mu': uni((NR, 6, D), 0.0, 1.0),
        'rw_rkv': nrm((NR, 3, D, D), D ** -0.5),
        'rw_w0': uni((NR, 2, D), -6.0, -1.0),
        'rw_wA': nrm((NR, 2, D, LORA_W), D ** -0.5),
        'rw_wB': nrm((NR, 2, LORA_W, D), 0.1 * LORA_W ** -0.5),
        'rw_a0': nrm((NR, 2, D), 0.1),
        'rw_aA': nrm((NR, 2, D, LORA_A), D ** -0.5),
        'rw_aB': nrm((NR, 2, LORA_A, D), 0.1 * LORA_A ** -0.5),
        'rw_gA': nrm((NR, D, LORA_G), D ** -0.5),
        'rw_gB': nrm((NR, LORA_G, D), LORA_G ** -0.5),
        'rw_kk': 0.85 + nrm((NR, D), 0.02),
        'rw_ka': 1.0 + nrm((NR, D), 0.02),
        'rw_rk': nrm((NR, H, N), 0.1),
        'rw_lnx': jnp.stack([1.0 + nrm((NR, D), 0.02), nrm((NR, D), 0.02)], axis=1),
        'rw_o': nrm((NR, D, D), D ** -0.5),
        'rw_v0': nrm((NR - 1, D), 0.1),
        'rw_vA': nrm((NR - 1, D, LORA_V), D ** -0.5),
        'rw_vB': nrm((NR - 1, LORA_V, D), LORA_V ** -0.5),
        'at_qkv': nrm((NA, D, qkv_w), D ** -0.5),
        'at_qk_g': 1.0 + nrm((NA, 2, AT_HEAD), 0.02),
        'at_o': nrm((NA, D, D), D ** -0.5),
        'ffn_up': nrm((DEPTH, D, 2 * F), D ** -0.5),
        'ffn_conv_w': nrm((DEPTH, 3, F), 3 ** -0.5),
        'ffn_conv_b': nrm((DEPTH, F), 0.02),
        'ffn_down': nrm((DEPTH, F, D), F ** -0.5),
    }

def reference(x_prompt, x_sample, c_prompt, c_sample, ada_w, ada_b, norm_g, rw_mu, rw_rkv, rw_w0, rw_wA, rw_wB,
              rw_a0, rw_aA, rw_aB, rw_gA, rw_gB, rw_kk, rw_ka, rw_rk, rw_lnx, rw_o, rw_v0, rw_vA, rw_vB,
              at_qkv, at_qk_g, at_o, ffn_up, ffn_conv_w, ffn_conv_b, ffn_down):
    P = dict(ada_w=ada_w, ada_b=ada_b, norm_g=norm_g, rw_mu=rw_mu, rw_rkv=rw_rkv, rw_w0=rw_w0, rw_wA=rw_wA,
             rw_wB=rw_wB, rw_a0=rw_a0, rw_aA=rw_aA, rw_aB=rw_aB, rw_gA=rw_gA, rw_gB=rw_gB, rw_kk=rw_kk,
             rw_ka=rw_ka, rw_rk=rw_rk, rw_lnx=rw_lnx, rw_o=rw_o, rw_v0=rw_v0, rw_vA=rw_vA, rw_vB=rw_vB,
             at_qkv=at_qkv, at_qk_g=at_qk_g, at_o=at_o, ffn_up=ffn_up, ffn_conv_w=ffn_conv_w,
             ffn_conv_b=ffn_conv_b, ffn_down=ffn_down)
    y_prompt = _trunk(x_prompt, c_prompt, P)
    y_sample = _trunk(x_sample, c_sample, P)
    return (y_prompt, y_sample)


_drawn_inputs = setup_inputs


def setup_inputs(seed=0):
    import zlib

    import numpy as np

    out = dict(_drawn_inputs(seed))
    spreads = {}
    factors = {'norm_g': 2.855,
     'rw_wA': 38.657,
     'rw_wB': 37.186,
     'rw_a0': 4.645,
     'rw_aA': 4.864,
     'rw_aB': 4.948,
     'rw_kk': 38.84,
     'rw_ka': 4.883,
     'at_qk_g': 8.0,
     'ffn_conv_b': 7.969}
    for name, (base, spread) in spreads.items():
        noise = np.random.default_rng([zlib.crc32(name.encode()), seed]).standard_normal(out[name].shape)
        drawn = base * np.exp(spread * noise) if base else spread * noise
        out[name] = __import__('jax').numpy.asarray(drawn.astype(out[name].dtype))
    for name, factor in factors.items():
        out[name] = (out[name] * factor).astype(out[name].dtype)
    return out
```

```python
from contextlib import ExitStack

import numpy as np

import concourse.bass as bass
from concourse import mybir

F32 = mybir.dt.float32
ALU = mybir.AluOpType
ACT = mybir.ActivationFunctionType
AX_X = mybir.AxisListType.X

P = 128
D = 1024
KT = D // P
NSEQ = 2
SEQ = 256
TOK = NSEQ * SEQ
DEPTH = 2
D_FF = 2816
FT = D_FF // P
HEAD = 64
NDIR = 2
C = 64
NCH = TOK // C
CPS = SEQ // C
LEVELS = 5
QH, KVH, AH = 8, 2, 128
GRID_W = 64
ROPE_THETA = 10000.0
NORM_EPS = 1e-6
GN_EPS = 64e-5
DECAY = float(np.exp(-0.5))

C_ADAB = 0
C_NORM = C_ADAB + DEPTH * 48
C_MU = C_NORM + DEPTH * 4 * KT
C_PAIR = C_MU + 6 * KT
NPP = 9
C_QKG = C_PAIR + KT * NPP
C_FFN = C_QKG + 2
NPARAM = C_FFN + DEPTH * FT * 4

K_ONES = 0
K_BLK = K_ONES + P
K_ID = K_BLK + P
K_GM = K_ID + P
K_NT = K_GM + NDIR * P
K_M1 = K_NT + NDIR * C
K_LV = K_M1 + NDIR * C
K_RES = K_LV + NDIR * LEVELS * C
K_COS = K_RES + TOK
K_SIN = K_COS + SEQ
K_EPS = K_SIN + SEQ
NCONST = K_EPS + 2


def constants():
    t = np.zeros((P, NCONST), np.float32)
    t[:, K_ONES:K_ONES + P] = 1.0 / D
    head = np.arange(P) // HEAD
    t[:, K_BLK:K_BLK + P] = (head[:, None] == head[None, :]) / HEAD
    t[:, K_ID:K_ID + P] = np.eye(P)
    i = np.arange(C)
    for n in range(NDIR):
        before = (i[:, None] < i[None, :]) if n == 0 else (i[:, None] > i[None, :])
        upto = before | (i[:, None] == i[None, :])
        gm = np.concatenate([before, upto], 1)
        t[:, K_GM + n * P:K_GM + (n + 1) * P] = np.concatenate([gm, gm], 0)
        t[:, K_NT + n * C:K_NT + (n + 1) * C] = np.tile(before.T, (2, 1))
        same = lambda b: (i[:, None] // b) == (i[None, :] // b)
        t[:, K_M1 + n * C:K_M1 + (n + 1) * C] = np.tile((before.T & same(2)) | np.eye(C, dtype=bool), (2, 1))
        for l in range(LEVELS):
            b = 2 ** (l + 1)
            m = (before & same(2 * b) & ~same(b)) | np.eye(C, dtype=bool)
            o = K_LV + (n * LEVELS + l) * C
            t[:, o:o + C] = np.tile(m, (2, 1))
    t[:, K_RES:K_RES + TOK] = (np.arange(TOK) % C != 0)
    tok = np.arange(SEQ)
    npair = AH // 4
    inv = ROPE_THETA ** (-np.arange(npair, dtype=np.float32) / npair)
    ang = np.concatenate([(tok // GRID_W)[:, None] * inv, (tok % GRID_W)[:, None] * inv], -1).astype(np.float32)
    t[:, K_COS:K_COS + SEQ] = np.tile(np.cos(ang).T, (2, 1))
    t[:, K_SIN:K_SIN + SEQ] = np.concatenate([np.sin(ang).T, -np.sin(ang).T], 0)
    t[:, K_EPS] = NORM_EPS
    t[:, K_EPS + 1] = GN_EPS
    return t


def encoder_trunk(nc, xT, cT, params, consts, ada_w, lora_a, pair_w, rw_o, at_kv, at_q, at_o,
                  ffn_up, ffn_down, yT):
    ctx = ExitStack()
    with ctx:
        sb = lambda name, shape: ctx.enter_context(nc.sbuf_tensor(name, shape, F32))
        sem = lambda name: ctx.enter_context(nc.semaphore(name))

        x_res = sb("x_res", [P, KT, TOK])
        h_pad = sb("h_pad", [P, KT, NSEQ, SEQ + 2])
        big = sb("big", [P, 3 * KT * TOK])
        o_res = sb("o_res", [P, KT, TOK])
        SLOT = 27 * P
        ring = sb("ring", [P, 2, SLOT])
        pt = sb("pt", [P, NPARAM])
        ct = sb("ct", [P, NCONST])
        mod = sb("mod", [P, DEPTH * 6 * KT, NSEQ])
        gs = sb("gs", [P, KT, NSEQ])
        csil = sb("csil", [P, KT, NSEQ])
        derived = sb("derived", [P, KT, 2])
        pcur = sb("pcur", [P, NPP + 2])
        fcur = sb("fcur", [P, 2, 4])
        lora = sb("lora", [P, 3, TOK])
        scan = sb("scan", [P, 15 * 1024])
        sx = sb("sx", [P, 2, NDIR, NSEQ, P])
        pend = sb("pend", [P, NDIR, NCH])
        ps = ctx.enter_context(nc.psum_tensor("ps", [P, 8, 512], F32))

        xr, xk, xv = (big[:, n * KT * TOK:(n + 1) * KT * TOK].rearrange("p (k t) -> p k t", k=KT) for n in range(3))
        mix_out = xr
        act_ff = big[:, 0:FT * TOK].rearrange("p (k t) -> p k t", k=FT)
        h_in = h_pad[:, :, :, 1:SEQ + 1]

        off = [0]

        def part(n):
            off[0] += n
            return scan[:, off[0] - n:off[0]]

        kb = part(2048).rearrange("p (n c s) -> p n c s", n=NDIR, c=NCH)
        ar = part(2048).rearrange("p (n c s) -> p n c s", n=NDIR, c=NCH)
        gm_flat = part(4096)
        gm = gm_flat.rearrange("p (n h c s) -> p n h c s", n=NDIR, h=2, c=NCH)
        wv = part(1024).rearrange("p (c i) -> p c i", c=NCH)
        nt = part(2048).rearrange("p (n c s) -> p n c s", n=NDIR, c=NCH)
        mt = part(2048).rearrange("p (n c s) -> p n c s", n=NDIR, c=NCH)
        mc_flat = part(1024)
        mc = mc_flat.rearrange("p (n c s) -> p n c s", n=NDIR, c=NCH)
        xc_flat = part(1024)
        xc = xc_flat.rearrange("p (n c s) -> p n c s", n=NDIR, c=NCH)
        x0s = xc_flat[0:C, 0:2 * NSEQ * P].rearrange("p (n q i) -> p n q i", n=NDIR, q=NSEQ)
        stmp = mc_flat[:, 0:2 * NSEQ * C].rearrange("p (n q i) -> p n q i", n=NDIR, q=NSEQ)
        ht = h_pad[:, :, :, :].rearrange("p k q t -> p (k q t)")[:, 0:8 * TOK]
        mf = ht[0:C, 0:4 * TOK].rearrange("p (n c h t) -> p n c h t", n=NDIR, c=NCH, h=2)
        t_k, t_r, t_v, t_nkk, t_g, t_bon, t_a0, t_a1 = (ht[:, n * TOK:(n + 1) * TOK] for n in range(8))
        t_a = (t_a0, t_a1)
        (s_w0, s_w1, s_l, s_inc, s_exc, s_e1, s_e2, s_e3) = (gm_flat[:, n * TOK:(n + 1) * TOK] for n in range(8))
        s_w = (s_w0, s_w1)
        t_kd = (xc_flat[:, 0:TOK], xc_flat[:, TOK:])
        t_b, t_sq = mc_flat[:, 0:TOK], mc_flat[:, TOK:]
        sq2 = (gm_flat[:, 0:TOK], gm_flat[:, TOK:2 * TOK])
        tmp2 = (gm_flat[:, 2 * TOK:3 * TOK], gm_flat[:, 3 * TOK:4 * TOK])
        rs = gm_flat[:, 4 * TOK:5 * TOK]
        xx, hsum = gm_flat[:, 5 * TOK:6 * TOK], gm_flat[:, 6 * TOK:7 * TOK]
        mixb = kb.rearrange("p n c s -> p (n c s)")
        mix4 = tuple(mixb[:, n * TOK:(n + 1) * TOK] for n in range(4))
        FU = NSEQ * (SEQ + 2)
        arf = ar.rearrange("p n c s -> p (n c s)")
        u_pad = tuple(arf[:, n * FU:(n + 1) * FU].rearrange("p (q t) -> p q t", q=NSEQ) for n in range(2))
        conv = (mixb[:, 0:TOK], mixb[:, TOK:2 * TOK])
        silu = (mixb[:, 2 * TOK:3 * TOK], mixb[:, 3 * TOK:])
        boff = [KT * TOK]

        def bpart(n):
            boff[0] += n
            return big[:, boff[0] - n:boff[0]]

        kh = bpart(KVH * TOK).rearrange("p (g t) -> p g t", g=KVH)
        vh = bpart(KVH * TOK).rearrange("p (g b d) -> p g b d", g=KVH, b=4)
        qh = tuple(bpart(TOK) for _ in range(2))
        raw = tuple(bpart(TOK) for _ in range(2))
        rot = tuple(bpart(TOK) for _ in range(2))
        swp = tuple(bpart(TOK) for _ in range(2))
        asq = tuple(bpart(TOK) for _ in range(2))
        ars = tuple(bpart(TOK) for _ in range(2))
        prob = mixb[:, 0:4 * SEQ].rearrange("p (b k) -> p b k", b=4)
        prT = mixb[:, 4 * SEQ:8 * SEQ].rearrange("p (q b t) -> p q b t", q=2, b=2)
        stat = arf[:, 0:16]
        cosb = ct[:, K_COS:K_COS + SEQ].unsqueeze(1).broadcast_to([P, NSEQ, SEQ])
        sinb = ct[:, K_SIN:K_SIN + SEQ].unsqueeze(1).broadcast_to([P, NSEQ, SEQ])

        ones = ct[:, K_ONES:K_ONES + P]
        blk = ct[:, K_BLK:K_BLK + P]
        ident = ct[:, K_ID:K_ID + P]
        seqs = lambda ap: ap.rearrange("p (q t) -> p q t", q=NSEQ)
        chunks = lambda ap: ap.rearrange("p (c t) -> p c t", c=NCH)
        pc = lambda n: pcur[:, n:n + 1]
        halves = ((0, C), (C, P))

        loaded = sem("loaded")
        phase_end = sem("phase_end")
        block_in = [sem(f"block_in{s}") for s in range(2)]
        block_done = [sem(f"block_done{s}") for s in range(2)]
        taken = [sem(f"taken{s}") for s in range(2)]
        act_own, dve_own, pool_own = sem("act_own"), sem("dve_own"), sem("pool_own")
        sq_ready, sq_used = sem("sq_ready"), sem("sq_used")
        root, rstd, scaled, scaled_used = sem("root"), sem("rstd"), sem("scaled"), sem("scaled_used")
        mixed, mixed_used = sem("mixed"), sem("mixed_used")
        u_ready, conv_ready, silu_ready = sem("u_ready"), sem("conv_ready"), sem("silu_ready")
        fcols, pcols = sem("fcols"), sem("pcols")
        centred = sem("centred")
        projected, evac, pair_end = sem("projected"), sem("evac"), sem("pair_end")
        head_sum, norm_root = sem("head_sum"), sem("norm_root")
        scan_in, cum, expd = sem("scan_in"), sem("cum"), sem("expd")
        bon_in = sem("bon_in")
        gram, gram_in, sys, sys_in, ident_in = sem("gram"), sem("gram_in"), sem("sys"), sem("sys_in"), sem("ident_in")
        tr, tr_in, tr_in2 = sem("tr"), sem("tr_in"), sem("tr_in2")
        xmm = [sem(f"xmm{n}") for n in range(2)]
        xev = [sem(f"xev{n}") for n in range(2)]
        mmm = [sem(f"mmm{n}") for n in range(2)]
        mev = [sem(f"mev{n}") for n in range(2)]
        tmm = [sem(f"tmm{n}") for n in range(2)]
        tev = [sem(f"tev{n}") for n in range(2)]
        fmm = [sem(f"fmm{n}") for n in range(2)]
        fev = [sem(f"fev{n}") for n in range(2)]
        x0_mm = [sem(f"x0_mm{n}") for n in range(2)]
        x0_ev = [sem(f"x0_ev{n}") for n in range(2)]
        u_mm = [sem(f"u_mm{n}") for n in range(2)]
        u_ev = [sem(f"u_ev{n}") for n in range(2)]
        s_mm = [sem(f"s_mm{n}") for n in range(2)]
        s_ev = [sem(f"s_ev{n}") for n in range(2)]
        y_mm, y_cp, y_in = sem("y_mm"), sem("y_cp"), sem("y_in")
        mean_mm, dev_sq, var_mm, var_root = sem("mean_mm"), sem("dev_sq"), sem("var_mm"), sem("var_root")
        a_pj, a_ev, a_ss, a_rt, a_q = sem("a_pj"), sem("a_ev"), sem("a_ss"), sem("a_rt"), sem("a_q")
        a_sc, a_mx, a_ex, a_p, a_tr, a_te, a_pv, a_o = (sem(n) for n in (
            "a_sc", "a_mx", "a_ex", "a_p", "a_tr", "a_te", "a_pv", "a_o"))
        v_tr = sem("v_tr")
        pe_tick, act_tick, dve_tick = sem("pe_tick"), sem("act_tick"), sem("dve_tick")
        stored = sem("stored")

        block = ctx.enter_context(nc.Block())

        class Own:

            def __init__(self, eng, own):
                self.eng, self.own, self.n = eng, own, 0

            def __call__(self, ins):
                ins.then_inc(self.own, 1)
                self.n += 1
                return self.n

            def wait(self, n=None):
                if self.n:
                    self.eng.wait_ge(self.own, self.n if n is None else n)

            def loop_start(self):
                self.base = self.n

            def loop_end(self):
                self.wait()
                if self.n > self.base:
                    self.eng.sem_inc(self.own, self.base - self.n)
                    self.n = self.base

        class Phases:
            def __init__(self, eng):
                self.eng, self.n = eng, 0

            def end(self):
                self.n += 1
                self.eng.drain().then_inc(phase_end, 1)
                self.eng.wait_ge(phase_end, 4 * self.n)

        class Slots:

            def __init__(self):
                self.n, self.took = [0, 0], 0

            def add(self, n, took=0):
                self.n = [x + n for x in self.n]
                self.took += took

        @block.sync
        def _(sp):
            slots = Slots()

            def fill(s, i, dst, src):
                sp.wait_ge(block_done[s], slots.n[s] + i)
                sp.dma_start(dst, src).then_inc(block_in[s], 16)

            def fill_first(s, dst, src):
                if slots.n[s]:
                    sp.wait_ge(block_done[s], slots.n[s])
                sp.dma_start(dst, src).then_inc(block_in[s], 16)
                slots.n[s] += 1

            def two(s):
                return ring[:, s, 0:2 * D].rearrange("p (m k) -> p m k", m=2)

            sp.dma_start(ct[:], consts).then_inc(loaded, 16)
            sp.dma_start(csil[:], cT).then_inc(loaded, 16)
            sp.dma_start(pt[:], params).then_inc(loaded, 16)
            sp.dma_start(x_res[:], xT).then_inc(loaded, 16)
            with sp.Fori(0, DEPTH * 12) as i:
                for s in range(2):
                    fill(s, i, two(s), ada_w[i, s].rearrange("m p k -> p m k"))
            slots.add(DEPTH * 12)

            def square(w):
                with sp.Fori(0, 2) as i:
                    for s in range(2):
                        fill(s, i, two(s), w[i, s].rearrange("m p k -> p m k"))
                slots.add(2)

            def mlp(l):
                with sp.Fori(0, FT // 2) as i:
                    for s in range(2):
                        fill(s, i, ring[:, s, 0:2 * D], ffn_up[l, i, s])
                slots.add(FT // 2)
                with sp.Fori(0, KT // 2) as i:
                    for s in range(2):
                        fill(s, i, ring[:, s, 0:D_FF], ffn_down[l, i, s])
                slots.add(KT // 2)

            fill_first(1, ring[:, 1, 0:3 * D], lora_a)
            with sp.Fori(0, KT) as i:
                fill(0, i, ring[:, 0, :], pair_w[i])
            slots.n[0] += KT
            square(rw_o)
            mlp(0)
            for s in range(2):
                fill_first(s, two(s), at_kv[s].rearrange("m p k -> p m k"))
            with sp.Fori(0, QH // 2) as i:
                for s in range(2):
                    fill(s, i, ring[:, s, 0:D], at_q[i, s])
            slots.add(QH // 2)
            square(at_o)
            mlp(1)
            sp.wait_ge(scaled_used, 8 * KT)
            sp.dma_start(yT, x_res[:]).then_inc(stored, 16)
            sp.wait_ge(stored, 16)

        @block.tensor
        def _(pe):
            mm, tp = nc.tensor.matmul, nc.tensor.transpose
            slots = Slots()
            phase = Phases(pe)
            norms = [0]

            def arrived(s, i=0):
                pe.wait_ge(block_in[s], 16 * (slots.n[s] + 1) + 16 * i)

            def product(bank, w, rhs, n=KT):
                for k in range(n):
                    last = mm(bank, w[:, k * P:(k + 1) * P], rhs[:, k], start=(k == 0), stop=(k == n - 1))
                return last

            def norm_sums():
                base = norms[0] * KT
                for k in range(KT):
                    pe.wait_ge(sq_ready, base + k + 1)
                    mm(ps[:, 0, :], ones, sq2[k % 2], start=(k == 0), stop=(k == KT - 1)).then_inc(sq_used, 1)
                norms[0] += 1

            def square(src):
                with pe.Fori(0, 2) as i:
                    for s in range(2):
                        arrived(s, i)
                        pe.wait_ge(taken[s], slots.took + i)
                        for m in range(2):
                            last = product(ps[:, 2 * s + m, :], ring[:, s, m * D:(m + 1) * D], src)
                        last.then_inc(block_done[s], 1)
                slots.add(2, 2)

            def mlp():
                with pe.Fori(0, FT // 2) as i:
                    for s in range(2):
                        arrived(s, i)
                        pe.wait_ge(taken[s], slots.took + i)
                        for m in range(2):
                            last = product(ps[:, 2 * s + m, :], ring[:, s, m * D:(m + 1) * D], h_in)
                        last.then_inc(block_done[s], 1)
                slots.add(FT // 2, FT // 2)
                for s in range(2):
                    pe.wait_ge(taken[s], slots.took)
                with pe.Fori(0, KT // 2) as i:
                    for s in range(2):
                        arrived(s, i)
                        pe.wait_ge(taken[s], slots.took + i)
                        product(ps[:, 4 + s, :], ring[:, s, 0:D_FF], act_ff, FT).then_inc(block_done[s], 1)
                slots.add(KT // 2, KT // 2)

            pe.wait_ge(loaded, 64)
            phase.end()
            with pe.Fori(0, DEPTH * 12) as i:
                for s in range(2):
                    arrived(s, i)
                    pe.wait_ge(taken[s], i)
                    for m in range(2):
                        for k in range(KT):
                            o = m * KT + k
                            last = mm(ps[:, s, 2 * m:2 * m + 2], ring[:, s, o * P:(o + 1) * P], csil[:, k, :],
                                      start=(k == 0), stop=(k == KT - 1))
                    last.then_inc(block_done[s], 1)
            slots.add(DEPTH * 12, DEPTH * 12)
            phase.end()
            norm_sums()
            phase.end()
            arrived(1)
            for k in range(KT):
                for n in range(3):
                    pe.wait_ge(mixed, k * 3 + n + 1)
                    last = mm(ps[:, 1 + n, :], ring[:, 1, (n * KT + k) * P:(n * KT + k + 1) * P],
                              mix4[(k * 3 + n) % 4], start=(k == 0), stop=(k == KT - 1))
                    last.then_inc(block_done[1] if k == KT - 1 and n == 2 else mixed_used, 1)
            slots.n[1] += 1
            phase.end()

            with pe.Fori(0, KT) as p:
                arrived(0, p)
                pe.wait_ge(pair_end, p)
                w = ring[:, 0, :]
                for n, src in enumerate((xr, xk, xv)):
                    product(ps[:, n, :], w[:, n * D:(n + 1) * D], src).then_inc(projected, 1)
                for lo_n in range(2):
                    for n, (lo, hi) in enumerate(halves):
                        mm(ps[:, 3 + 2 * lo_n + n, :], w[lo:hi, (24 + lo_n) * P:(25 + lo_n) * P],
                           lora[lo:hi, lo_n, :], start=True, stop=True).then_inc(projected, 1)
                mm(ps[:, 7, :], w[:, 26 * P:27 * P], lora[:, 2, :], start=True, stop=True).then_inc(block_done[0], 1)
                pe.wait_ge(evac, 9 * p + 9)
                mm(ps[:, 1, :], blk, t_sq, start=True, stop=True).then_inc(head_sum, 1)
                pe.wait_ge(bon_in, 2 * p + 1)
                mm(ps[:, 2, :], blk, t_sq, start=True, stop=True).then_inc(head_sum, 1)
                for n in range(NDIR):
                    for c in range(NCH):
                        for lo, hi in halves:
                            last = mm(ps[lo:hi, 3 + n, c * C:(c + 1) * C], ar[lo:hi, n, c, 0:C], kb[lo:hi, n, c, C:P],
                                      start=True, stop=True)
                    last.then_inc(sys, 1)
                for g in range(8):
                    n, h, q = g // 4, (g // 2) % 2, g % 2
                    bank = (0, 5, 6, 7)[g % 4]
                    if g >= 4:
                        pe.wait_ge(gram_in, 8 * p + g - 3)
                    lo, hi = halves[h]
                    for c in range(4):
                        last = mm(ps[:, bank, c * P:(c + 1) * P], kb[lo:hi, n, 4 * q + c, :], ar[lo:hi, n, 4 * q + c, :],
                                  start=True, stop=True)
                    last.then_inc(gram, 1)
                pe.wait_ge(norm_root, p + 1)
                pe.wait_ge(bon_in, 2 * p + 2)
                for g in range(6):
                    bank = (1, 0, 5, 6, 7, 2)[g]
                    if 1 <= g <= 4:
                        pe.wait_ge(gram_in, 8 * p + 4 + g)
                        pe.sem_inc(pe_tick, 1)
                    for c in range(4):
                        if g < 4:
                            last = tp(ps[:, bank, c * P:(c + 1) * P], kb[:, g // 2, 4 * (g % 2) + c, :], ident)
                        else:
                            cc = 4 * (g - 4) + c
                            last = tp(ps[0:C, bank, c * P:(c + 1) * P], t_v[:, cc * C:(cc + 1) * C], ident)
                    last.then_inc(tr, 1)
                pe.wait_ge(tr_in, 6 * p + 6)
                for n in range(NDIR):
                    pe.wait_ge(ident_in, 2 * p + n + 1)
                    for c in range(NCH):
                        last = tp(ps[:, 2 * n + c // 4, (c % 4) * P:(c % 4 + 1) * P], mt[:, n, c, :], ident)
                    last.then_inc(tmm[n], 1)
                for l in range(LEVELS):
                    for n in range(NDIR):
                        pe.wait_ge(mev[n], LEVELS * p + l + 1)
                        for c in range(NCH):
                            last = mm(ps[:, 4 + n, c * C:(c + 1) * C], nt[:, n, c, :], mc[:, n, c, :], start=True, stop=True)
                        last.then_inc(xmm[n], 1)
                    for n in range(NDIR):
                        pe.wait_ge(tev[n], (LEVELS - 1) * p + l)
                        pe.wait_ge(xev[n], LEVELS * p + l + 1)
                        if l < LEVELS - 1:
                            for c in range(NCH):
                                last = mm(ps[:, 6 + n, c * C:(c + 1) * C], mt[:, n, c, :], xc[:, n, c, :], start=True, stop=True)
                            last.then_inc(mmm[n], 1)
                        else:
                            pe.sem_inc(pe_tick, 1)
                            for c in range(NCH):
                                for h, (lo, hi) in enumerate(halves):
                                    last = mm(ps[0:C, 2 * n + h, c * C:(c + 1) * C], mt[lo:hi, n, c, lo:hi], xc[lo:hi, n, c, :],
                                              start=True, stop=True)
                            last.then_inc(fmm[n], 1)
                    if l < LEVELS - 1:
                        for n in range(NDIR):
                            pe.wait_ge(mev[n], LEVELS * p + l + 2)
                            pe.sem_inc(pe_tick, 1)
                            for c in range(NCH):
                                last = tp(ps[0:C, 2 * n + c // 4, (c % 4) * P:(c % 4 + 1) * P], mc[:, n, c, :], ident)
                            last.then_inc(tmm[n], 1)
                for j in range(CPS):
                    cs = [[q * CPS + (j if n == 0 else CPS - 1 - j) for q in range(NSEQ)] for n in range(NDIR)]
                    st = sx[:, j % 2]
                    for n in range(NDIR):
                        if j == 0:
                            pe.wait_ge(fev[n], p + 1)
                        else:
                            pe.wait_ge(s_ev[n], (CPS - 1) * p + j)
                        pe.sem_inc(pe_tick, 1)
                        for q in range(NSEQ):
                            c, o = cs[n][q], q * P
                            if j > 0:
                                mm(ps[0:C, 4 + n, o:o + P], ar[:, n, c, 0:C], st[:, n, q, :], start=True, stop=False)
                            for h in range(2):
                                last = mm(ps[0:C, 4 + n, o + h * C:o + (h + 1) * C], gm[0:C, n, h, c, 0:C],
                                          wv[0:C, c, h * C:(h + 1) * C], start=(j == 0), stop=(j == 0 or h == 1))
                        last.then_inc(x0_mm[n], 1)
                    for n in range(NDIR):
                        pe.wait_ge(x0_ev[n], CPS * p + j + 1)
                        pe.sem_inc(pe_tick, 1)
                        for q in range(NSEQ):
                            for h in range(2):
                                o = 256 + q * P + h * C
                                last = mm(ps[C:P, 4 + n, o:o + C], mf[:, n, cs[n][q], h, :],
                                          x0s[:, n, q, h * C:(h + 1) * C], start=True, stop=True)
                        last.then_inc(u_mm[n], 1)
                    for n in range(NDIR):
                        pe.wait_ge(u_ev[n], CPS * p + j + 1)
                        if j < CPS - 1:
                            for q in range(NSEQ):
                                last = mm(ps[:, 6 + n, q * P:(q + 1) * P], kb[:, n, cs[n][q], :], wv[:, cs[n][q], :],
                                          start=True, stop=True)
                            last.then_inc(s_mm[n], 1)
                        for q in range(NSEQ):
                            c = cs[n][q]
                            if j > 0:
                                mm(ps[:, n, c * C:(c + 1) * C], st[:, n, q, :], ar[:, n, c, C:P], start=True, stop=False)
                            for h, (lo, hi) in enumerate(halves):
                                last = mm(ps[lo:hi, n, c * C:(c + 1) * C], wv[:, c, lo:hi], gm[:, n, h, c, C:P],
                                          start=(j == 0), stop=True)
                        last.then_inc(y_mm, 1)
                pe.wait_ge(y_in, p + 1)
                mm(ps[:, 2, :], blk, t_a0, start=True, stop=True).then_inc(mean_mm, 1)
                pe.wait_ge(dev_sq, p + 1)
                mm(ps[:, 3, :], blk, t_sq, start=True, stop=True).then_inc(var_mm, 1)
            slots.n[0] += KT
            phase.end()
            square(o_res)
            phase.end()
            norm_sums()
            phase.end()
            norm_sums()
            phase.end()
            mlp()
            phase.end()
            norm_sums()
            phase.end()
            norm_sums()
            phase.end()

            for s in range(2):
                arrived(s)
                for m in range(2):
                    last = product(ps[:, 6 * s + m, :], ring[:, s, m * D:(m + 1) * D], h_in)
                last.then_inc(block_done[s], 1)
            slots.add(1, 1)
            for x in range(KVH):
                pe.wait_ge(a_ev, x + 1)
                mm(ps[:, 2 + x, :], ones, asq[x], start=True, stop=True).then_inc(a_ss, 1)
            for g in range(KVH):
                pe.wait_ge(v_tr, g + 1)
                for b in range(4):
                    last = tp(ps[:, 4 + g, b * P:(b + 1) * P], raw[g][:, b * P:(b + 1) * P], ident)
                last.then_inc(a_tr, 1)
            for s in range(2):
                pe.wait_ge(taken[s], slots.took)
            for g in range(KVH):
                with pe.Fori(0, 2) as i:
                    for s in range(2):
                        arrived(s, i)
                        pe.wait_ge(a_q, KVH + 4 * g + 2 * i)
                        product(ps[:, s, :], ring[:, s, 0:D], h_in).then_inc(block_done[s], 1)
                    for s in range(2):
                        pe.wait_ge(a_ev, KVH + 4 * g + 2 * i + s + 1)
                        mm(ps[:, 2 + s, :], ones, asq[s], start=True, stop=True).then_inc(a_ss, 1)
                    for s in range(2):
                        n = 4 * g + 2 * i + s
                        pe.wait_ge(a_q, KVH + 1 + n)
                        pe.wait_ge(a_o, n)
                        for q in range(NSEQ):
                            for b in range(2):
                                o = q * SEQ + b * P
                                last = mm(ps[:, 4 + q, b * SEQ:(b + 1) * SEQ], qh[s][:, o:o + P],
                                          kh[:, g, q * SEQ:(q + 1) * SEQ], start=True, stop=True)
                        last.then_inc(a_sc, 1)
                        pe.wait_ge(a_p, n + 1)
                        for q in range(NSEQ):
                            for k in range(2):
                                for b in range(2):
                                    o = (k * 2 + b) * P
                                    last = tp(ps[:, 6 + q, o:o + P], prob[:, 2 * q + b, k * P:(k + 1) * P], ident)
                        last.then_inc(a_tr, 1)
                        pe.wait_ge(a_te, n + 1)
                        for q in range(NSEQ):
                            for k in range(2):
                                last = mm(ps[:, 4, q * SEQ:(q + 1) * SEQ], vh[:, g, 2 * q + k, :], prT[:, q, k, :],
                                          start=(k == 0), stop=(k == 1))
                        last.then_inc(a_pv, 1)
                slots.add(2)
            phase.end()
            square(o_res)
            phase.end()
            norm_sums()
            phase.end()
            norm_sums()
            phase.end()
            mlp()
            phase.end()
            norm_sums()
            phase.end()

        @block.scalar
        def _(act):
            A = nc.scalar.activation
            slots = Slots()
            phase = Phases(act)
            norms = [0]
            gq, gk = pt[:, C_QKG:C_QKG + 1], pt[:, C_QKG + 1:C_QKG + 2]

            def norm_squares(src):
                base = norms[0] * KT
                for k in range(KT):
                    if base + k >= 2:
                        act.wait_ge(sq_used, base + k - 1)
                    A(sq2[k % 2], src[:, k, :], ACT.Square).then_inc(sq_ready, 1)
                act.wait_ge(sq_used, base + KT)
                A(rs, ps[:, 0, :], ACT.Sqrt, bias=ct[:, K_EPS:K_EPS + 1]).then_inc(root, 1)
                norms[0] += 1

            def norm_affine(l, shift):
                base = (norms[0] - 1) * KT
                for k in range(KT):
                    act.wait_ge(scaled, base + k + 1)
                    for q in range(NSEQ):
                        last = A(h_in[:, k, q, :], tmp2[k % 2][:, q * SEQ:(q + 1) * SEQ], ACT.Identity,
                                 scale=gs[:, k, q:q + 1], bias=mod[:, (6 * l + shift) * KT + k, q:q + 1])
                    last.then_inc(scaled_used, 1)

            def square():
                with act.Fori(0, 2) as i:
                    for s in range(2):
                        act.wait_ge(block_done[s], slots.n[s] + i + 1)
                        act.sem_inc(act_tick, 1)
                        A(mix_out[:, bass.ds(4 * i + 2 * s, 2), :], ps[:, 2 * s:2 * s + 2, :],
                          ACT.Copy).then_inc(taken[s], 1)
                slots.add(2)

            def mlp(l):
                with act.Fori(0, FT // 2) as i:
                    for s in range(2):
                        act.wait_ge(block_done[s], slots.n[s] + i + 1)
                        act.wait_ge(fcols, l * FT + 2 * i + s + 1)
                        act.wait_ge(taken[s], slots.took + i)
                        A(u_pad[s][:, :, 1:SEQ + 1], seqs(ps[:, 2 * s, :]), ACT.Copy)
                        A(conv[s], ps[:, 2 * s, :], ACT.Identity, scale=fcur[:, s, 1:2],
                          bias=fcur[:, s, 3:4]).then_inc(u_ready, 1)
                    for s in range(2):
                        act.wait_ge(conv_ready, l * FT + 2 * i + s + 1)
                        A(silu[s], conv[s], ACT.Silu).then_inc(silu_ready, 1)
                slots.add(FT // 2, FT // 2)
                with act.Fori(0, KT // 2) as i:
                    for s in range(2):
                        act.wait_ge(block_done[s], slots.n[s] + i + 1)
                        act.sem_inc(act_tick, 1)
                        A(o_res[:, 2 * i + s, :], ps[:, 4 + s, :], ACT.Copy).then_inc(taken[s], 1)
                slots.add(KT // 2, KT // 2)

            act.wait_ge(loaded, 64)
            A(csil[:], csil[:], ACT.Silu)
            phase.end()
            slots.add(DEPTH * 12, DEPTH * 12)
            phase.end()
            norm_squares(x_res)
            norm_affine(0, 0)
            phase.end()
            slots.n[1] += 1
            act.wait_ge(block_done[1], slots.n[1])
            A(lora[:, 0, :], ps[:, 1, :], ACT.Tanh)
            A(lora[:, 1, :], ps[:, 2, :], ACT.Copy)
            A(lora[:, 2, :], ps[:, 3, :], ACT.Sigmoid)
            phase.end()

            with act.Fori(0, KT) as p:
                act.wait_ge(projected, 7 * p + 2)
                act.wait_ge(pcols, p + 1)
                A(t_k, ps[:, 1, :], ACT.Copy).then_inc(evac, 1)
                A(t_sq, ps[:, 1, :], ACT.Square, scale=pc(4)).then_inc(evac, 1)
                A(t_r, ps[:, 0, :], ACT.Copy).then_inc(evac, 1)
                act.wait_ge(projected, 7 * p + 7)
                A(t_v, ps[:, 2, :], ACT.Copy).then_inc(evac, 1)
                for n in range(NDIR):
                    A(s_w[n], ps[:, 3 + n, :], ACT.Sigmoid, bias=pc(n)).then_inc(evac, 1)
                for n in range(NDIR):
                    A(t_a[n], ps[:, 5 + n, :], ACT.Sigmoid, bias=pc(2 + n)).then_inc(evac, 1)
                act.wait_ge(block_done[0], slots.n[0] + p + 1)
                A(t_g, ps[:, 7, :], ACT.Copy).then_inc(evac, 1)
                act.wait_ge(head_sum, 2 * p + 1)
                A(t_b, ps[:, 1, :], ACT.Sqrt, scale=float(HEAD)).then_inc(norm_root, 1)
                for n in range(NDIR):
                    act.wait_ge(cum, 2 * p + n + 1)
                    A(s_e1, s_exc, ACT.Exp, scale=-DECAY)
                    A(s_e2, s_inc, ACT.Exp, scale=DECAY)
                    A(s_e3, s_inc, ACT.Exp, scale=-DECAY).then_inc(expd, 1)
                for g in range(6):
                    act.wait_ge(tr, 6 * p + g + 1)
                    bank = (1, 0, 5, 6, 7, 2)[g]
                    dst = kb[:, g // 2, 4 * (g % 2):4 * (g % 2) + 4, :] if g < 4 else wv[0:C, 4 * (g - 4):4 * (g - 3), :]
                    src = ps[:, bank, :] if g < 4 else ps[0:C, bank, :]
                    A(dst, src.rearrange("p (c s) -> p c s", c=4), ACT.Copy).then_inc(tr_in, 1)
                pairs = [ps[:, 2 * n:2 * n + 2, :].rearrange("p b (c s) -> p (b c) s", s=P) for n in range(NDIR)]
                for n in range(NDIR):
                    act.wait_ge(tmm[n], LEVELS * p + 1)
                    A(mc[0:C, n, :, :], pairs[n][0:C, :, 0:C], ACT.Copy)
                    A(mc[C:P, n, :, :], pairs[n][C:P, :, C:P], ACT.Copy).then_inc(mev[n], 1)
                for l in range(LEVELS - 1):
                    for n in range(NDIR):
                        act.wait_ge(mmm[n], (LEVELS - 1) * p + l + 1)
                        A(mc[:, n, :, :], chunks(ps[:, 6 + n, :]), ACT.Copy).then_inc(mev[n], 1)
                    act.wait_ge(tmm[0], LEVELS * p + l + 2)
                    A(mt[0:C, 0, :, 0:C], pairs[0][0:C, :, 0:C], ACT.Copy)
                    A(mt[C:P, 0, :, C:P], pairs[0][0:C, :, C:P], ACT.Copy).then_inc(tev[0], 1)
                for n in range(NDIR):
                    act.wait_ge(fmm[n], p + 1)
                    for h in range(2):
                        last = A(mf[:, n, :, h, :], chunks(ps[0:C, 2 * n + h, :]), ACT.Copy)
                    last.then_inc(fev[n], 1)
                for j in range(CPS):
                    for n in range(NDIR):
                        act.wait_ge(x0_mm[n], CPS * p + j + 1)
                        A(x0s[:, n, :, :], ps[0:C, 4 + n, 0:2 * P].rearrange("p (q i) -> p q i", q=NSEQ),
                          ACT.Copy).then_inc(x0_ev[n], 1)
                act.wait_ge(y_mm, 2 * CPS * (p + 1))
                A(t_a1, ps[:, 0, :], ACT.Copy).then_inc(y_cp, 1)
                act.wait_ge(centred, p + 1)
                A(t_sq, t_a1, ACT.Square).then_inc(dev_sq, 1)
                act.wait_ge(var_mm, p + 1)
                A(t_b, ps[:, 3, :], ACT.Sqrt, bias=ct[:, K_EPS + 1:K_EPS + 2]).then_inc(var_root, 1)
            slots.n[0] += KT
            phase.end()
            square()
            slots.took += 2
            phase.end()
            norm_squares(mix_out)
            phase.end()
            norm_squares(x_res)
            norm_affine(0, 3)
            phase.end()
            mlp(0)
            phase.end()
            norm_squares(o_res)
            phase.end()
            norm_squares(x_res)
            norm_affine(1, 0)
            phase.end()
            slots.add(1, 1)
            act.wait_ge(block_done[0], slots.n[0])
            for x in range(KVH):
                A(raw[x], ps[:, x, :], ACT.Identity, scale=gk)
                A(asq[x], ps[:, x, :], ACT.Square).then_inc(a_ev, 1)
            for x in range(KVH):
                act.wait_ge(a_ss, x + 1)
                A(ars[x], ps[:, 2 + x, :], ACT.Sqrt, scale=float(D // AH), bias=ct[:, K_EPS:K_EPS + 1]).then_inc(a_rt, 1)
            act.wait_ge(block_done[1], slots.n[1])
            act.wait_ge(a_q, KVH)
            for g in range(KVH):
                A(raw[g], ps[:, 6 + g, :], ACT.Copy).then_inc(v_tr, 1)
            for g in range(KVH):
                act.wait_ge(a_tr, g + 1)
                A(vh[:, g, :, :], ps[:, 4 + g, :].rearrange("p (b d) -> p b d", b=4), ACT.Copy).then_inc(taken[g], 1)
            for g in range(KVH):
                with act.Fori(0, 2) as i:
                    for s in range(2):
                        act.wait_ge(block_done[s], slots.n[s] + i + 1)
                        A(raw[s], ps[:, s, :], ACT.Identity, scale=gq)
                        A(asq[s], ps[:, s, :], ACT.Square).then_inc(a_ev, 1)
                    for s in range(2):
                        act.wait_ge(a_ss, KVH + 4 * g + 2 * i + s + 1)
                        A(ars[s], ps[:, 2 + s, :], ACT.Sqrt, scale=float(D // AH),
                          bias=ct[:, K_EPS:K_EPS + 1]).then_inc(a_rt, 1)
                    for s in range(2):
                        n = 4 * g + 2 * i + s
                        act.wait_ge(a_mx, n + 1)
                        act.wait_ge(a_tr, KVH + n)
                        for b in range(4):
                            last = A(prob[:, b, :], ps[:, 4 + b // 2, (b % 2) * SEQ:(b % 2 + 1) * SEQ], ACT.Exp,
                                     scale=float(AH) ** -0.5, bias=stat[:, 4 + b:5 + b], accum_out=stat[:, 8 + b:9 + b])
                        last.then_inc(a_ex, 1)
                        act.wait_ge(a_tr, KVH + n + 1)
                        act.wait_ge(a_pv, n)
                        for q in range(NSEQ):
                            last = A(prT[:, q, :, :], ps[:, 6 + q, :].rearrange("p (k t) -> p k t", k=2), ACT.Copy)
                        last.then_inc(a_te, 1)
                slots.add(2)
            phase.end()
            square()
            slots.took += 2
            phase.end()
            norm_squares(mix_out)
            phase.end()
            norm_squares(x_res)
            norm_affine(1, 3)
            phase.end()
            mlp(1)
            phase.end()
            norm_squares(o_res)
            phase.end()

        @block.vector
        def _(dve):
            own = Own(dve, dve_own)
            phase = Phases(dve)
            V = nc.vector
            norms = [0]

            def gains(l, norm, part_, pre):
                g = pt[:, C_NORM + (4 * l + norm) * KT:C_NORM + (4 * l + norm + 1) * KT].unsqueeze(2).broadcast_to([P, KT, NSEQ])
                m = mod[:, (6 * l + part_) * KT:(6 * l + part_ + 1) * KT, :]
                own.wait()
                own(V.scalar_tensor_tensor(gs[:], m, 1.0 if pre else 0.0, g, ALU.add, ALU.mult))

            def inverse_root():
                dve.wait_ge(root, norms[0] + 1)
                return V.reciprocal(rs, rs)

            def pre_norm(l, norm, scale_part):
                gains(l, norm, scale_part, True)
                own.wait()
                own(inverse_root())
                own.wait()
                base = norms[0] * KT
                for k in range(KT):
                    if base + k >= 2:
                        dve.wait_ge(scaled_used, base + k - 1)
                    own.wait()
                    V.tensor_tensor(tmp2[k % 2], x_res[:, k, :], rs, ALU.mult).then_inc(scaled, 1)
                norms[0] += 1

            def post_norm(l, norm, gate_part):
                gains(l, norm, gate_part, False)
                own.wait()
                inverse_root().then_inc(rstd, 1)
                base = norms[0] * KT
                for k in range(KT):
                    dve.wait_ge(scaled, base + k + 1)
                    for q in range(NSEQ):
                        xs = x_res[:, k, q * SEQ:(q + 1) * SEQ]
                        own.wait()
                        last = V.scalar_tensor_tensor(xs, tmp2[k % 2][:, q * SEQ:(q + 1) * SEQ], gs[:, k, q:q + 1], xs,
                                                      ALU.mult, ALU.add)
                    last.then_inc(scaled_used, 1)
                norms[0] += 1

            def mlp(l):
                own.loop_start()
                with dve.Fori(0, FT // 2) as i:
                    for s in range(2):
                        own.wait()
                        V.tensor_copy(fcur[:, s, :], pt[:, bass.ds(C_FFN + 4 * (l * FT + s) + 8 * i, 4)]).then_inc(fcols, 1)
                    for s in range(2):
                        dve.wait_ge(u_ready, l * FT + 2 * i + s + 1)
                        own.wait()
                        own(V.scalar_tensor_tensor(seqs(conv[s]), u_pad[s][:, :, 0:SEQ], fcur[:, s, 0:1], seqs(conv[s]),
                                                   ALU.mult, ALU.add))
                        own.wait()
                        V.scalar_tensor_tensor(seqs(conv[s]), u_pad[s][:, :, 2:SEQ + 2], fcur[:, s, 2:3], seqs(conv[s]),
                                               ALU.mult, ALU.add).then_inc(conv_ready, 1)
                    for s in range(2):
                        dve.wait_ge(silu_ready, l * FT + 2 * i + s + 1)
                        own.wait()
                        V.tensor_tensor(act_ff[:, 2 * i + s, :], silu[s], ps[:, 2 * s + 1, :], ALU.mult).then_inc(taken[s], 1)
                    own.loop_end()

            dve.wait_ge(loaded, 64)
            pair_tab = pt[:, C_PAIR:C_PAIR + KT * NPP].rearrange("p (k n) -> p k n", n=NPP)
            own.wait()
            own(V.tensor_scalar(derived[:, :, 0:1], pair_tab[:, :, 4:5], -1.0, None, ALU.mult))
            own.wait()
            own(V.tensor_scalar(derived[:, :, 1:2], pair_tab[:, :, 5:6], -1.0, 1.0, ALU.mult, ALU.add))
            phase.end()
            with dve.Fori(0, DEPTH * 12) as i:
                for s in range(2):
                    dve.wait_ge(block_done[s], i + 1)
                    b = pt[:, bass.ds(C_ADAB + 2 * s + 4 * i, 2)].unsqueeze(2).broadcast_to([P, 2, NSEQ])
                    own.wait()
                    V.tensor_tensor(mod[:, bass.ds(4 * i + 2 * s, 2), :], ps[:, s, 0:4].rearrange("p (m q) -> p m q", m=2), b,
                                    ALU.add).then_inc(taken[s], 1)
            phase.end()
            pre_norm(0, 0, 1)
            phase.end()
            n_ring = 0
            for k in range(KT):
                hk = h_pad[:, k]
                own.wait()
                own(V.tensor_tensor(seqs(hsum), hk[:, :, 0:SEQ], hk[:, :, 2:SEQ + 2], ALU.add))
                own.wait()
                own(V.scalar_tensor_tensor(seqs(xx), seqs(hsum), 0.5, h_in[:, k], ALU.mult, ALU.subtract))
                own.wait()
                mu = lambda n: pt[:, C_MU + n * KT + k:C_MU + n * KT + k + 1]
                for n in (1, 4, 5):
                    if n_ring >= 4:
                        dve.wait_ge(mixed_used, n_ring - 3)
                    own.wait()
                    V.scalar_tensor_tensor(seqs(mix4[n_ring % 4]), seqs(xx), mu(n), h_in[:, k], ALU.mult,
                                           ALU.add).then_inc(mixed, 1)
                    n_ring += 1
                for n, dst in ((0, xr), (2, xk), (3, xv)):
                    own.wait()
                    own(V.scalar_tensor_tensor(seqs(dst[:, k, :]), seqs(xx), mu(n), h_in[:, k], ALU.mult, ALU.add))
            own.wait()
            phase.end()

            own.loop_start()
            with dve.Fori(0, KT) as p:
                own.wait()
                own(V.tensor_copy(pcur[:, 0:NPP], pt[:, bass.ds(C_PAIR + NPP * p, NPP)]))
                own.wait()
                V.tensor_copy(pcur[:, NPP:NPP + 2], derived[:, bass.ds(p, 1), :].squeeze(1)).then_inc(pcols, 1)
                dve.wait_ge(norm_root, p + 1)
                own.wait()
                own(V.tensor_scalar_max(t_b, t_b, 1e-12))
                own.wait()
                own(V.reciprocal(t_b, t_b))
                own.wait()
                own(V.scalar_tensor_tensor(t_nkk, t_k, pc(NPP), t_b, ALU.mult, ALU.mult))
                own.wait()
                res = ct[:, K_RES:K_RES + TOK]
                for n in range(NDIR):
                    if n == 0:
                        own.wait()
                        own(V.tensor_tensor_scan(s_inc, res, s_w[0], 0.0, ALU.mult, ALU.add))
                        own.wait()
                        V.tensor_tensor(s_exc, s_inc, s_w[0], ALU.subtract).then_inc(cum, 1)
                    else:
                        own.wait()
                        own(V.tensor_tensor_scan(s_l, res, s_w[1], 0.0, ALU.mult, ALU.add))
                        own.wait()
                        tot = chunks(s_l)[:, :, C - 1:C].broadcast_to([P, NCH, C])
                        own.wait()
                        own(V.tensor_tensor(chunks(s_exc), tot, chunks(s_l), ALU.subtract))
                        own.wait()
                        V.tensor_tensor(s_inc, s_exc, s_w[1], ALU.add).then_inc(cum, 1)
                    own.wait()
                    own(V.scalar_tensor_tensor(t_b, t_nkk, -1.0, t_a[n], ALU.mult, ALU.mult))
                    own.wait()
                    own(V.tensor_scalar(t_a[n], t_a[n], pc(5), pc(NPP + 1), ALU.mult, ALU.add))
                    own.wait()
                    own(V.tensor_tensor(t_kd[n], t_a[n], t_k, ALU.mult))
                    own.wait()
                    dve.wait_ge(expd, 2 * p + n + 1)
                    own.wait()
                    own(V.tensor_tensor(kb[:, n, :, 0:C], chunks(t_kd[n]), chunks(s_e2), ALU.mult))
                    own.wait()
                    own(V.tensor_tensor(kb[:, n, :, C:P], chunks(t_b), chunks(s_e2), ALU.mult))
                    own.wait()
                    own(V.tensor_tensor(ar[:, n, :, 0:C], chunks(t_nkk), chunks(s_e1), ALU.mult))
                    own.wait()
                    own(V.tensor_tensor(ar[:, n, :, C:P], chunks(t_r), chunks(s_e3), ALU.mult))
                    e = C - 1 if n == 0 else 0
                    own.wait()
                    own(V.tensor_copy(pend[:, n, :], chunks(s_e3)[:, :, e]))
                own.wait()
                own(V.tensor_tensor(t_b, t_kd[0], t_kd[1], ALU.add))
                own.wait()
                V.scalar_tensor_tensor(t_sq, t_r, pc(6), t_b, ALU.mult, ALU.mult).then_inc(bon_in, 1)
                dve.wait_ge(head_sum, 2 * p + 2)
                own.wait()
                V.scalar_tensor_tensor(t_bon, ps[:, 2, :], float(HEAD), t_v, ALU.mult, ALU.mult).then_inc(bon_in, 1)
                for n in range(NDIR):
                    dve.wait_ge(sys, 2 * p + n + 1)
                    msk = ct[:, K_NT + n * C:K_NT + (n + 1) * C].unsqueeze(1).broadcast_to([P, NCH, C])
                    for h, (lo, hi) in enumerate(halves):
                        own.wait()
                        last = V.tensor_tensor(nt[lo:hi, n, :, lo:hi], chunks(ps[lo:hi, 3 + n, :]), msk[lo:hi], ALU.mult)
                    last.then_inc(sys_in, 1)
                for g in range(8):
                    dve.wait_ge(gram, 8 * p + g + 1)
                    n, h, q = g // 4, (g // 2) % 2, g % 2
                    bank = (0, 5, 6, 7)[g % 4]
                    msk = ct[:, K_GM + n * P:K_GM + (n + 1) * P].unsqueeze(1).broadcast_to([P, 4, P])
                    own.wait()
                    V.tensor_tensor(gm[:, n, h, 4 * q:4 * q + 4, :], ps[:, bank, :].rearrange("p (c s) -> p c s", c=4), msk,
                                    ALU.mult).then_inc(gram_in, 1)
                pairs = [ps[:, 2 * n:2 * n + 2, :].rearrange("p b (c s) -> p (b c) s", s=P) for n in range(NDIR)]
                for l in range(LEVELS):
                    for n in range(NDIR):
                        dve.wait_ge(xmm[n], LEVELS * p + l + 1)
                        o = K_LV + (n * LEVELS + l) * C
                        msk = ct[:, o:o + C].unsqueeze(1).broadcast_to([P, NCH, C])
                        own.wait()
                        V.tensor_tensor(xc[:, n, :, :], chunks(ps[:, 4 + n, :]), msk, ALU.mult).then_inc(xev[n], 1)
                    if l < LEVELS - 1:
                        dve.wait_ge(tmm[1], LEVELS * p + l + 2)
                        V.tensor_copy(mt[0:C, 1, :, 0:C], pairs[1][0:C, :, 0:C])
                        V.tensor_copy(mt[C:P, 1, :, C:P], pairs[1][0:C, :, C:P]).then_inc(tev[1], 1)
                pend4 = pend[:, :, :].rearrange("p n (q c) -> p n q c", q=NSEQ)
                wv4 = wv.rearrange("p (q c) i -> p q c i", q=NSEQ)
                for j in range(CPS):
                    for n in range(NDIR):
                        dve.wait_ge(u_mm[n], CPS * p + j + 1)
                        c = j if n == 0 else CPS - 1 - j
                        own.wait()
                        V.tensor_copy(wv4[C:P, :, c, :], ps[C:P, 4 + n, 256:512].rearrange("p (q i) -> p q i", q=NSEQ)).then_inc(u_ev[n], 1)
                    if j < CPS - 1:
                        for n in range(NDIR):
                            c = j if n == 0 else CPS - 1 - j
                            dve.wait_ge(s_mm[n], (CPS - 1) * p + j + 1)
                            for h, (lo, hi) in enumerate(halves):
                                sm = ps[lo:hi, 6 + n, 0:2 * P].rearrange("p (q i) -> p q i", q=NSEQ)[:, :, lo:hi]
                                if j > 0:
                                    own.wait()
                                    own(V.tensor_tensor(stmp[lo:hi, n, :, :], sm, sx[lo:hi, j % 2, n, :, lo:hi], ALU.add))
                            if j > 0:
                                own.wait()
                            for h, (lo, hi) in enumerate(halves):
                                sm = ps[lo:hi, 6 + n, 0:2 * P].rearrange("p (q i) -> p q i", q=NSEQ)[:, :, lo:hi]
                                src = stmp[lo:hi, n, :, :] if j > 0 else sm
                                own.wait()
                                last = V.tensor_tensor(sx[lo:hi, (j + 1) % 2, n, :, lo:hi], src,
                                                       pend4[lo:hi, n, :, c:c + 1].broadcast_to([C, NSEQ, C]), ALU.mult)
                            last.then_inc(s_ev[n], 1)
                dve.wait_ge(y_cp, p + 1)
                own.wait()
                V.tensor_tensor(t_a0, ps[:, 1, :], t_a1, ALU.add).then_inc(y_in, 1)
                dve.wait_ge(mean_mm, p + 1)
                own.wait()
                V.tensor_tensor(t_a1, t_a0, ps[:, 2, :], ALU.subtract).then_inc(centred, 1)
                dve.wait_ge(var_root, p + 1)
                own.wait()
                own(V.reciprocal(t_b, t_b))
                own.wait()
                own(V.tensor_tensor(t_a0, t_a1, t_b, ALU.mult))
                own.wait()
                own(V.tensor_scalar(t_a0, t_a0, pc(7), pc(8), ALU.mult, ALU.add))
                own.wait()
                own(V.tensor_tensor(t_a0, t_a0, t_bon, ALU.add))
                own.wait()
                V.tensor_tensor(o_res[:, p, :], t_a0, t_g, ALU.mult).then_inc(pair_end, 1)
                own.loop_end()
            phase.end()
            phase.end()
            post_norm(0, 1, 2)
            phase.end()
            pre_norm(0, 2, 4)
            phase.end()
            mlp(0)
            phase.end()
            post_norm(0, 3, 5)
            phase.end()
            pre_norm(1, 0, 1)
            phase.end()

            def rotate(x, dst, n):
                dve.wait_ge(a_ev, n + 1)
                own.wait()
                own(V.tensor_tensor(seqs(swp[x])[0:C], seqs(raw[x])[C:P], sinb[C:P], ALU.mult))
                own.wait()
                own(V.tensor_tensor(seqs(swp[x])[C:P], seqs(raw[x])[0:C], sinb[0:C], ALU.mult))
                own.wait()
                own(V.tensor_tensor(seqs(rot[x]), seqs(raw[x]), cosb, ALU.mult))
                own.wait()
                own(V.tensor_tensor(rot[x], rot[x], swp[x], ALU.add))
                dve.wait_ge(a_rt, n + 1)
                own.wait()
                own(V.reciprocal(ars[x], ars[x]))
                own.wait()
                V.tensor_tensor(dst, rot[x], ars[x], ALU.mult).then_inc(a_q, 1)

            for x in range(KVH):
                rotate(x, kh[:, x, :], x)
            for g in range(KVH):
                own.loop_start()
                with dve.Fori(0, 2) as i:
                    for s in range(2):
                        rotate(s, qh[s], KVH + 4 * g + 2 * i + s)
                    for s in range(2):
                        n = 4 * g + 2 * i + s
                        dve.wait_ge(a_sc, n + 1)
                        own.wait()
                        own(V.reduce_max(stat[:, 0:4], ps[:, 4:6, :].rearrange("p q (b k) -> p (q b) k", k=SEQ), AX_X))
                        own.wait()
                        V.tensor_scalar(stat[:, 4:8], stat[:, 0:4], -float(AH) ** -0.5, None, ALU.mult).then_inc(a_mx, 1)
                        dve.wait_ge(a_ex, n + 1)
                        own.wait()
                        own(V.reciprocal(stat[:, 12:16], stat[:, 8:12]))
                        own.wait()
                        V.tensor_tensor(prob[:], prob[:], stat[:, 12:16].unsqueeze(2).broadcast_to([P, 4, SEQ]),
                                        ALU.mult).then_inc(a_p, 1)
                        dve.wait_ge(a_pv, n + 1)
                        dve.sem_inc(dve_tick, 1)
                        own.wait()
                        V.tensor_copy(o_res[:, 4 * g + 2 * i + s, :], ps[:, 4, :]).then_inc(a_o, 1)
                    own.loop_end()
            phase.end()
            phase.end()
            post_norm(1, 1, 2)
            phase.end()
            pre_norm(1, 2, 4)
            phase.end()
            mlp(1)
            phase.end()
            post_norm(1, 3, 5)
            phase.end()

        @block.gpsimd
        def _(pool):
            phase = Phases(pool)
            own = Own(pool, pool_own)
            G = nc.gpsimd
            norms = [0]
            posts = [0]

            def pads():
                G.memset(h_pad[:, :, :, 0:1], 0.0)
                G.memset(h_pad[:, :, :, SEQ + 1:SEQ + 2], 0.0)
                for s in range(2):
                    G.memset(u_pad[s][:, :, 0:1], 0.0)
                    G.memset(u_pad[s][:, :, SEQ + 1:SEQ + 2], 0.0)
                norms[0] += 1

            def post_norm(src):
                posts[0] += 1
                pool.wait_ge(rstd, posts[0])
                base = norms[0] * KT
                for k in range(KT):
                    if base + k >= 2:
                        pool.wait_ge(scaled_used, base + k - 1)
                    G.tensor_tensor(tmp2[k % 2], src[:, k, :], rs, ALU.mult).then_inc(scaled, 1)
                norms[0] += 1

            G.memset(scan[:, 15 * 1024 - 6144:15 * 1024], 0.0)
            G.memset(sx[:], 0.0)
            phase.end()
            phase.end()
            pads()
            phase.end()
            phase.end()
            own.loop_start()
            with pool.Fori(0, KT) as p:
                for n in range(NDIR):
                    pool.wait_ge(sys_in, 2 * p + n + 1)
                    one = ct[:, K_ID:K_ID + P].unsqueeze(1).broadcast_to([P, NCH, P])
                    own(G.tensor_tensor(nt[:, n], nt[:, n], one, ALU.add))
                    own.wait()
                    m1 = ct[:, K_M1 + n * C:K_M1 + (n + 1) * C].unsqueeze(1).broadcast_to([P, NCH, C])
                    own(G.tensor_tensor(mt[0:C, n, :, 0:C], nt[0:C, n, :, 0:C], m1[0:C], ALU.mult))
                    own.wait()
                    G.tensor_tensor(mt[C:P, n, :, C:P], nt[C:P, n, :, C:P], m1[C:P], ALU.mult).then_inc(ident_in, 1)
                    pool.wait_ge(ident_in, 2 * p + n + 1)
                own.loop_end()
            phase.end()
            phase.end()
            post_norm(mix_out)
            phase.end()
            pads()
            phase.end()
            phase.end()
            post_norm(o_res)
            phase.end()
            pads()
            phase.end()
            phase.end()
            phase.end()
            post_norm(mix_out)
            phase.end()
            pads()
            phase.end()
            phase.end()
            post_norm(o_res)
            phase.end()


def tiles(w):
    k, m = w.shape
    return w.reshape(k // P, P, m // P, P).transpose(2, 1, 0, 3)


def columns(v):
    return v.reshape(-1, P).T


def kernel(x_prompt, x_sample, c_prompt, c_sample, ada_w, ada_b, norm_g, rw_mu, rw_rkv, rw_w0, rw_wA, rw_wB,
           rw_a0, rw_aA, rw_aB, rw_gA, rw_gB, rw_kk, rw_ka, rw_rk, rw_lnx, rw_o, rw_v0, rw_vA, rw_vB,
           at_qkv, at_qk_g, at_o, ffn_up, ffn_conv_w, ffn_conv_b, ffn_down):
    import concourse.bacc as bacc
    from concourse.bass_utils import run_bass_kernel_spmd

    arr = lambda a: np.asarray(a)
    x = np.concatenate([arr(x_prompt), arr(x_sample)], 0)
    xT = x.transpose(2, 0, 1).reshape(KT, P, TOK).transpose(1, 0, 2)
    c = np.concatenate([arr(c_prompt), arr(c_sample)], 0)
    cT = c.T.reshape(KT, P, NSEQ).transpose(1, 0, 2)

    halfway = np.concatenate([np.arange(0, AH, 2), np.arange(1, AH, 2)])
    pair = np.stack([columns(a) for a in (arr(rw_w0)[0, 0], arr(rw_w0)[0, 1], arr(rw_a0)[0, 0], arr(rw_a0)[0, 1],
                                          arr(rw_kk)[0], arr(rw_ka)[0], arr(rw_rk)[0], arr(rw_lnx)[0, 0],
                                          arr(rw_lnx)[0, 1])], -1)
    cw, cb = arr(ffn_conv_w), arr(ffn_conv_b)
    ffc = np.concatenate([np.stack([columns(a) for a in (cw[l, 0], cw[l, 1], cw[l, 2], cb[l])], -1)
                          for l in range(DEPTH)], 1)
    params = np.concatenate([columns(arr(ada_b)), columns(arr(norm_g)), columns(arr(rw_mu)[0]),
                             pair.reshape(P, -1), arr(at_qk_g)[0][:, halfway].T, ffc.reshape(P, -1)], 1)

    aw = np.stack([tiles(arr(ada_w)[l]) for l in range(DEPTH)]).reshape(DEPTH * 12, 2, 2, P, D)
    rkv = [tiles(arr(rw_rkv)[0, n]).reshape(KT, P, D) for n in range(3)]
    second = [arr(w)[0].reshape(P, KT, P).transpose(1, 0, 2) for w in (rw_wB, rw_aB, rw_gB)]
    pair_w = np.concatenate(rkv + second, -1)
    first = [tiles(arr(w)[0].transpose(1, 0, 2).reshape(D, P))[0].reshape(P, D) for w in (rw_wA, rw_aA)]
    lora_a = np.concatenate(first + [tiles(arr(rw_gA)[0])[0].reshape(P, D)], -1)
    wo = tiles(arr(rw_o)[0]).reshape(2, 2, 2, P, D)
    qkv = tiles(arr(at_qkv)[0]).reshape(12, P, D)
    swap = lambda w: w.reshape(w.shape[0], P, KT, P)[..., halfway].reshape(w.shape[0], P, D)
    at_kv = np.stack([swap(qkv[8:10]), qkv[10:12]])
    at_q = swap(qkv[0:8]).reshape(4, 2, P, D)
    ao = tiles(arr(at_o)[0]).reshape(2, 2, 2, P, D)
    up = np.stack([tiles(arr(ffn_up)[l]).reshape(2, FT, P, D).transpose(1, 2, 0, 3).reshape(FT // 2, 2, P, 2 * D)
                   for l in range(DEPTH)])
    down = np.stack([tiles(arr(ffn_down)[l]).reshape(KT // 2, 2, P, D_FF) for l in range(DEPTH)])

    ins = dict(xT=xT, cT=cT, params=params, consts=constants(), ada_w=aw, lora_a=lora_a, pair_w=pair_w, rw_o=wo,
               at_kv=at_kv, at_q=at_q, at_o=ao, ffn_up=up, ffn_down=down)
    nc = bacc.Bacc("TRN2", target_bir_lowering=False, num_devices=1)
    arrays, args = {}, {}
    for name, a in ins.items():
        a = np.ascontiguousarray(a)
        arrays[f"in_{name}"] = a
        args[name] = nc.dram_tensor(f"in_{name}", a.shape, mybir.dt.from_np(a.dtype), kind="ExternalInput").ap()
    yT = nc.dram_tensor("out_y", (P, KT, TOK), F32, kind="ExternalOutput").ap()
    encoder_trunk(nc, yT=yT, **args)
    r = run_bass_kernel_spmd(nc, [arrays], core_ids=[0])
    y = r.results[0]["out_y"].reshape(P, KT, NSEQ, SEQ).transpose(2, 3, 1, 0).reshape(NSEQ, SEQ, D)
    return y[0:1], y[1:2]
```

```python
from contextlib import ExitStack

import numpy as np

import concourse.bass as bass
from concourse import mybir

F32 = mybir.dt.float32
F32R = mybir.dt.float32r
ALU = mybir.AluOpType
ACT = mybir.ActivationFunctionType
AX_X = mybir.AxisListType.X

P = 128
D = 1024
KT = D // P
NSEQ = 2
SEQ = 256
TOK = NSEQ * SEQ
DEPTH = 2
D_FF = 2816
FT = D_FF // P
HEAD = 64
NDIR = 2
C = 64
NCH = TOK // C
CPS = SEQ // C
LEVELS = 5
QH, KVH, AH = 8, 2, 128
GRID_W = 64
ROPE_THETA = 10000.0
NORM_EPS = 1e-6
GN_EPS = 64e-5
DECAY = float(np.exp(-0.5))

C_ADAB = 0
C_NORM = C_ADAB + DEPTH * 48
C_MU = C_NORM + DEPTH * 4 * KT
C_PAIR = C_MU + 6 * KT
NPP = 9
C_QKG = C_PAIR + KT * NPP
C_FFN = C_QKG + 2
NPARAM = C_FFN + DEPTH * FT * 4

K_ONES = 0
K_BLK = K_ONES + P
K_ID = K_BLK + P
K_GM = K_ID + P
K_NT = K_GM + NDIR * P
K_M1 = K_NT + NDIR * C
K_LV = K_M1 + NDIR * C
K_RES = K_LV + NDIR * LEVELS * C
K_COS = K_RES + TOK
K_SIN = K_COS + SEQ
K_EPS = K_SIN + SEQ
NCONST = K_EPS + 2


def constants():
    t = np.zeros((P, NCONST), np.float32)
    t[:, K_ONES:K_ONES + P] = 1.0 / D
    head = np.arange(P) // HEAD
    t[:, K_BLK:K_BLK + P] = (head[:, None] == head[None, :]) / HEAD
    t[:, K_ID:K_ID + P] = np.eye(P)
    i = np.arange(C)
    for n in range(NDIR):
        before = (i[:, None] < i[None, :]) if n == 0 else (i[:, None] > i[None, :])
        upto = before | (i[:, None] == i[None, :])
        gm = np.concatenate([before, upto], 1)
        t[:, K_GM + n * P:K_GM + (n + 1) * P] = np.concatenate([gm, gm], 0)
        t[:, K_NT + n * C:K_NT + (n + 1) * C] = np.tile(before.T, (2, 1))
        same = lambda b: (i[:, None] // b) == (i[None, :] // b)
        t[:, K_M1 + n * C:K_M1 + (n + 1) * C] = np.tile((before.T & same(2)) | np.eye(C, dtype=bool), (2, 1))
        for l in range(LEVELS):
            b = 2 ** (l + 1)
            m = (before & same(2 * b) & ~same(b)) | np.eye(C, dtype=bool)
            o = K_LV + (n * LEVELS + l) * C
            t[:, o:o + C] = np.tile(m, (2, 1))
    t[:, K_RES:K_RES + TOK] = (np.arange(TOK) % C != 0)
    tok = np.arange(SEQ)
    npair = AH // 4
    inv = ROPE_THETA ** (-np.arange(npair, dtype=np.float32) / npair)
    ang = np.concatenate([(tok // GRID_W)[:, None] * inv, (tok % GRID_W)[:, None] * inv], -1).astype(np.float32)
    t[:, K_COS:K_COS + SEQ] = np.tile(np.cos(ang).T, (2, 1))
    t[:, K_SIN:K_SIN + SEQ] = np.concatenate([np.sin(ang).T, -np.sin(ang).T], 0)
    t[:, K_EPS] = NORM_EPS
    t[:, K_EPS + 1] = GN_EPS
    return t


def encoder_trunk(nc, xT, cT, params, consts, ada_w, lora_a, pair_w, gate_w, rw_o, at_kv, at_q, at_o,
                  ffn_up, ffn_down, yT):
    ctx = ExitStack()
    ADA = 3
    ADA_ROUNDS = DEPTH * 6 * D // TOK // ADA
    with ctx:
        sb = lambda name, shape: ctx.enter_context(nc.sbuf_tensor(name, shape, F32))
        sem = lambda name: ctx.enter_context(nc.semaphore(name))

        x_res = sb("x_res", [P, KT, TOK])
        pt = sb("pt", [P, NPARAM])
        ct = sb("ct", [P, NCONST])
        mod = sb("mod", [P, DEPTH * 6 * KT, NSEQ])
        gs = sb("gs", [P, KT, NSEQ])
        csil = sb("csil", [P, KT, NSEQ])
        derived = sb("derived", [P, KT, 2])
        pcur = sb("pcur", [P, NPP + 2])
        fcur = sb("fcur", [P, 2, 4])
        sx = sb("sx", [P, 2, NDIR, NSEQ, P])
        pend = sb("pend", [P, NDIR, NCH])
        pendn = sb("pendn", [P, NDIR, NCH])
        gbt = sb("gbt", [P, P])
        SLOT, PIECE, NRAW = 27 * P, D_FF // 2, 4
        BIG, SCAN = 3 * KT * TOK, 15 * 1024
        AREA = BIG + SCAN + 2 * SLOT + 3 * TOK

        def view(*tensors):
            with ExitStack() as here:
                return [here.enter_context(nc.sbuf_tensor(name, shape, kind)) for name, shape, kind in tensors]

        h_pad, o_res, area = view(
            ("h_pad", [P, KT, NSEQ, SEQ + 2], F32),
            ("o_res", [P, KT, TOK], F32),
            ("area", [P, AREA], F32))
        h_lo_pad, h_hi, ff_hi, ff_lo, ffs, raw_w, split_w = view(
            ("h_lo_pad", [P, KT, NSEQ, SEQ + 2], F32R),
            ("h_hi", [P, KT, TOK], F32R),
            ("ff_hi", [P, FT, TOK], F32R),
            ("ff_lo", [P, FT, TOK], F32R),
            ("ffs", [P, AREA - 2 * FT * TOK - (NRAW + 4) * PIECE], F32),
            ("raw_w", [P, NRAW, PIECE], F32),
            ("split_w", [P, 2, 2, PIECE], F32R))
        o_hi, _, o_lo = view(
            ("o_hi", [P, KT, TOK], F32R),
            ("o_gap", [P, KT * NSEQ * 2], F32),
            ("o_lo", [P, KT, TOK], F32R))

        big = area[:, 0:BIG]
        scan = area[:, BIG:BIG + SCAN]
        ring = area[:, BIG + SCAN:BIG + SCAN + 2 * SLOT].rearrange("p (s k) -> p s k", s=2)
        lora = area[:, BIG + SCAN + 2 * SLOT:].rearrange("p (n t) -> p n t", n=3)
        ps = ctx.enter_context(nc.psum_tensor("ps", [P, 8, 512], F32))

        xr, xk, xv = (big[:, n * KT * TOK:(n + 1) * KT * TOK].rearrange("p (k t) -> p k t", k=KT) for n in range(3))
        mix_out = xr
        h_in = h_pad[:, :, :, 1:SEQ + 1]

        off = [0]

        def part(n):
            off[0] += n
            return scan[:, off[0] - n:off[0]]

        kb = part(2048).rearrange("p (n c s) -> p n c s", n=NDIR, c=NCH)
        ar = part(2048).rearrange("p (n c s) -> p n c s", n=NDIR, c=NCH)
        gm_flat = part(4096)
        gm = gm_flat.rearrange("p (n h c s) -> p n h c s", n=NDIR, h=2, c=NCH)
        wv = part(1024).rearrange("p (c i) -> p c i", c=NCH)
        nt = part(2048).rearrange("p (n c s) -> p n c s", n=NDIR, c=NCH)
        mt = part(2048).rearrange("p (n c s) -> p n c s", n=NDIR, c=NCH)
        mc_flat = part(1024)
        mc = mc_flat.rearrange("p (n c s) -> p n c s", n=NDIR, c=NCH)
        xc_flat = part(1024)
        xc = xc_flat.rearrange("p (n c s) -> p n c s", n=NDIR, c=NCH)
        x0s = xc_flat[0:C, 0:2 * NSEQ * P].rearrange("p (n q i) -> p n q i", n=NDIR, q=NSEQ)
        stmp = mc_flat[:, 0:2 * NSEQ * C].rearrange("p (n q i) -> p n q i", n=NDIR, q=NSEQ)
        ht = h_pad[:, :, :, :].rearrange("p k q t -> p (k q t)")
        xt = x_res[:, :, :].rearrange("p k t -> p (k t)")
        tile = lambda area, n: area[:, n * TOK:(n + 1) * TOK]
        mf = ht[0:C, 0:4 * TOK].rearrange("p (n c h t) -> p n c h t", n=NDIR, c=NCH, h=2)
        c_sq, c_b = tile(ht, 0), tile(ht, 1)
        t_r, t_v, t_nkk, s_e2 = (tile(ht, n) for n in range(4, 8))
        t_a1, t_b1, s_exc, s_inc, t_bonn, t_bon = (tile(ring[:, 1, :], n) for n in range(6))
        kbn = xt[:, 0:2048].rearrange("p (n c s) -> p n c s", n=NDIR, c=NCH)
        arn = xt[:, 2048:4096].rearrange("p (n c s) -> p n c s", n=NDIR, c=NCH)
        t_k, t_sq = tile(xt, 0), tile(xt, 1)
        s_w0, t_a0, t_b0, s_w1 = tile(xt, 2), tile(xt, 3), tile(xt, 6), tile(xt, 7)
        s_l = s_w0
        t_a, t_b, s_w = (t_a0, t_a1), (t_b0, t_b1), (s_w0, s_w1)
        sq2 = (gm_flat[:, 0:TOK], gm_flat[:, TOK:2 * TOK])
        tmp2 = (gm_flat[:, 2 * TOK:3 * TOK], gm_flat[:, 3 * TOK:4 * TOK])
        rs = gm_flat[:, 4 * TOK:5 * TOK]
        xx, hsum = gm_flat[:, 5 * TOK:6 * TOK], gm_flat[:, 6 * TOK:7 * TOK]
        mixb = kb.rearrange("p n c s -> p (n c s)")
        mix4 = tuple(mixb[:, n * TOK:(n + 1) * TOK] for n in range(4))
        arf = ar.rearrange("p n c s -> p (n c s)")
        h_lo = h_lo_pad[:, :, :, 1:SEQ + 1]
        att_hi = ff_hi[:, 0:KT, :]
        FU = NSEQ * (SEQ + 2)
        u_pad = tuple(ffs[:, n * FU:(n + 1) * FU].rearrange("p (q t) -> p q t", q=NSEQ) for n in range(2))
        conv = tuple(ffs[:, 2 * FU + n * TOK:2 * FU + (n + 1) * TOK] for n in range(2))
        boff = [KT * TOK]

        def bpart(n):
            boff[0] += n
            return big[:, boff[0] - n:boff[0]]

        kh = bpart(KVH * TOK).rearrange("p (g t) -> p g t", g=KVH)
        vh = bpart(KVH * TOK).rearrange("p (g b d) -> p g b d", g=KVH, b=4)
        qh = tuple(bpart(TOK) for _ in range(2))
        raw = tuple(bpart(TOK) for _ in range(2))
        rot = tuple(bpart(TOK) for _ in range(2))
        swp = tuple(bpart(TOK) for _ in range(2))
        asq = tuple(bpart(TOK) for _ in range(2))
        ars = tuple(bpart(TOK) for _ in range(2))
        prob = mixb[:, 0:4 * SEQ].rearrange("p (b k) -> p b k", b=4)
        prT = mixb[:, 4 * SEQ:8 * SEQ].rearrange("p (q b t) -> p q b t", q=2, b=2)
        stat = arf[:, 0:16]
        cosb = ct[:, K_COS:K_COS + SEQ].unsqueeze(1).broadcast_to([P, NSEQ, SEQ])
        sinb = ct[:, K_SIN:K_SIN + SEQ].unsqueeze(1).broadcast_to([P, NSEQ, SEQ])

        ones = ct[:, K_ONES:K_ONES + P]
        blk = ct[:, K_BLK:K_BLK + P]
        ident = ct[:, K_ID:K_ID + P]
        seqs = lambda ap: ap.rearrange("p (q t) -> p q t", q=NSEQ)
        ada_blk = tuple(big[:, n * KT * TOK:(n + 1) * KT * TOK].rearrange("p (k m) -> p k m", k=KT) for n in range(ADA))
        ada_rows = tuple(scan[0:NSEQ, n * TOK:(n + 1) * TOK] for n in range(ADA))
        chunks = lambda ap: ap.rearrange("p (c t) -> p c t", c=NCH)
        pc = lambda n: pcur[:, n:n + 1]
        halves = ((0, C), (C, P))

        loaded = sem("loaded")
        phase_end = sem("phase_end")
        block_in = [sem(f"block_in{s}") for s in range(2)]
        block_done = [sem(f"block_done{s}") for s in range(2)]
        taken = [sem(f"taken{s}") for s in range(2)]
        act_own, dve_own, pool_own = sem("act_own"), sem("dve_own"), sem("pool_own")
        sq_ready, sq_used = sem("sq_ready"), sem("sq_used")
        root, rstd, scaled, scaled_used = sem("root"), sem("rstd"), sem("scaled"), sem("scaled_used")
        mixed, mixed_used = sem("mixed"), sem("mixed_used")
        u_ready, conv_ready, silu_ready = sem("u_ready"), sem("conv_ready"), sem("silu_ready")
        ada_in, ada_done = ([sem(f"{name}{s}") for s in range(ADA)] for name in ("ada_in", "ada_done"))
        ada_row, ada_cols, ada_taken = sem("ada_row"), sem("ada_cols"), sem("ada_taken")
        piece_in = [sem(f"piece_in{r}") for r in range(NRAW)]
        w_hi, w_lo, w_used = sem("w_hi"), sem("w_lo"), sem("w_used")
        copied = sem("copied")
        h_ready, h_high, moving = sem("h_ready"), sem("h_high"), sem("moving")
        v_in = sem("v_in")
        fcols, pcols = sem("fcols"), sem("pcols")
        centred = sem("centred")
        projected, evac, pair_end = sem("projected"), sem("evac"), sem("pair_end")
        head_sum, norm_root = sem("head_sum"), sem("norm_root")
        scan_in, cum, expd = sem("scan_in"), sem("cum"), sem("expd")
        bon_in, prep, carried, carried_bon = sem("bon_in"), sem("prep"), sem("carried"), sem("carried_bon")
        kdf, kd_sum, prod, gate_in, gate_mm, gated, x_back = (sem(n) for n in (
            "kdf", "kd_sum", "prod", "gate_in", "gate_mm", "gated", "x_back"))
        scanned, bon_copied = sem("scanned"), sem("bon_copied")
        gram, gram_in, sys, sys_in, ident_in = sem("gram"), sem("gram_in"), sem("sys"), sem("sys_in"), sem("ident_in")
        tr, tr_in, tr_in2 = sem("tr"), sem("tr_in"), sem("tr_in2")
        xmm = [sem(f"xmm{n}") for n in range(2)]
        xev = [sem(f"xev{n}") for n in range(2)]
        mmm = [sem(f"mmm{n}") for n in range(2)]
        mev = [sem(f"mev{n}") for n in range(2)]
        tmm = [sem(f"tmm{n}") for n in range(2)]
        tev = [sem(f"tev{n}") for n in range(2)]
        fmm = [sem(f"fmm{n}") for n in range(2)]
        fev = [sem(f"fev{n}") for n in range(2)]
        x0_mm = [sem(f"x0_mm{n}") for n in range(2)]
        x0_ev = [sem(f"x0_ev{n}") for n in range(2)]
        u_mm = [sem(f"u_mm{n}") for n in range(2)]
        u_ev = [sem(f"u_ev{n}") for n in range(2)]
        s_mm = [sem(f"s_mm{n}") for n in range(2)]
        s_ev = [sem(f"s_ev{n}") for n in range(2)]
        y_mm, y_cp, y_in = sem("y_mm"), sem("y_cp"), sem("y_in")
        mean_mm, dev_sq, var_mm, var_root = sem("mean_mm"), sem("dev_sq"), sem("var_mm"), sem("var_root")
        a_pj, a_ev, a_ss, a_rt, a_q = sem("a_pj"), sem("a_ev"), sem("a_ss"), sem("a_rt"), sem("a_q")
        a_sc, a_mx, a_ex, a_p, a_tr, a_te, a_pv, a_o = (sem(n) for n in (
            "a_sc", "a_mx", "a_ex", "a_p", "a_tr", "a_te", "a_pv", "a_o"))
        v_tr = sem("v_tr")
        pe_tick, act_tick, dve_tick, pool_tick = (sem(n) for n in ("pe_tick", "act_tick", "dve_tick", "pool_tick"))
        stored = sem("stored")

        block = ctx.enter_context(nc.Block())

        class Own:

            def __init__(self, eng, own):
                self.eng, self.own, self.n = eng, own, 0

            def __call__(self, ins):
                ins.then_inc(self.own, 1)
                self.n += 1
                return self.n

            def wait(self, n=None):
                if self.n:
                    self.eng.wait_ge(self.own, self.n if n is None else n)

            def loop_start(self):
                self.base = self.n

            def loop_end(self):
                self.wait()
                if self.n > self.base:
                    self.eng.sem_inc(self.own, self.base - self.n)
                    self.n = self.base

        class Phases:
            def __init__(self, eng):
                self.eng, self.n = eng, 0

            def end(self):
                self.n += 1
                self.eng.drain().then_inc(phase_end, 1)
                self.eng.wait_ge(phase_end, 4 * self.n)

        class Pieces:

            def __init__(self):
                self.n, self.slot, self.copies = 0, [0] * NRAW, 0

            def add(self, n, slots=NRAW, copies=0):
                self.n += n
                for r in range(slots):
                    self.slot[r] += n // slots
                self.copies += copies

        class Slots:

            def __init__(self):
                self.n, self.took = [0, 0], 0

            def add(self, n, took=0):
                self.n = [x + n for x in self.n]
                self.took += took

        @block.sync
        def _(sp):
            slots = Slots()

            def fill(s, i, dst, src):
                sp.wait_ge(block_done[s], slots.n[s] + i)
                sp.dma_start(dst, src).then_inc(block_in[s], 16)

            def fill_first(s, dst, src):
                if slots.n[s]:
                    sp.wait_ge(block_done[s], slots.n[s])
                sp.dma_start(dst, src).then_inc(block_in[s], 16)
                slots.n[s] += 1

            sp.dma_start(ct[:], consts).then_inc(loaded, 16)
            sp.dma_start(csil[:], cT).then_inc(loaded, 16)
            sp.dma_start(pt[:], params).then_inc(loaded, 16)
            sp.dma_start(x_res[:], xT).then_inc(loaded, 16)
            with sp.Fori(0, ADA_ROUNDS) as i:
                for n in range(ADA):
                    sp.wait_ge(ada_done[n], i + 1)
                    sp.dma_start(ada_blk[n], ada_w[i, n]).then_inc(ada_in[n], 16)

            pieces_ = Pieces()

            def load(n, r, src, cols, behind=NRAW):
                if not isinstance(n, int) or n >= behind:
                    sp.wait_ge(w_lo, n - behind + 1)
                sp.dma_start(raw_w[:, r, 0:cols], src).then_inc(piece_in[r], 16)

            def square(w, first):
                for m in range(KT):
                    load(pieces_.n + m, m % NRAW, w[m], D, 2 if first and m < NRAW else NRAW)
                pieces_.add(KT)

            def mlp(l):
                with sp.Fori(0, FT // 2) as i:
                    for r in range(NRAW):
                        load(pieces_.n + NRAW * i + r, r, ffn_up[l, i, r], D)
                pieces_.add(2 * FT)
                with sp.Fori(0, KT // 2) as i:
                    for r in range(NRAW):
                        load(pieces_.n + NRAW * i + r, r, ffn_down[l, i, r], PIECE)
                pieces_.add(2 * KT)

            fill_first(1, ring[:, 1, 0:3 * D], lora_a)
            fill_first(0, ring[:, 0, 0:26 * P], pair_w[0])
            with sp.Fori(0, KT - 1) as i:
                fill(0, i, ring[:, 0, 0:26 * P], pair_w[i + 1])
                sp.wait_ge(gate_mm, i + 1)
                sp.dma_start(gbt[:], gate_w[i]).then_inc(gate_in, 16)
            slots.n[0] += KT - 1
            sp.wait_ge(gate_mm, KT)
            sp.dma_start(gbt[:], gate_w[KT - 1]).then_inc(gate_in, 16)
            sp.wait_ge(gated, KT)
            sp.dma_start(x_res[:], xT).then_inc(x_back, 16)
            square(rw_o, False)
            mlp(0)
            for m in range(2 * KVH):
                load(pieces_.n + m, m, at_kv[m], D)
            pieces_.add(2 * KVH)
            with sp.Fori(0, QH // 2) as i:
                for s in range(2):
                    load(pieces_.n + 2 * i + s, s, at_q[i, s], D, 2)
            pieces_.add(QH, 2)
            square(at_o, True)
            mlp(1)
            sp.wait_ge(scaled_used, 8 * KT)
            sp.dma_start(yT, x_res[:]).then_inc(stored, 16)
            sp.wait_ge(stored, 16)

        @block.tensor
        def _(pe):
            mm, tp = nc.tensor.matmul, nc.tensor.transpose
            slots = Slots()
            phase = Phases(pe)
            norms = [0]

            def arrived(s, i=0):
                pe.wait_ge(block_in[s], 16 * (slots.n[s] + 1) + 16 * i)

            def product(bank, w, rhs, n=KT):
                for k in range(n):
                    last = mm(bank, w[:, k * P:(k + 1) * P], rhs[:, k], start=(k == 0), stop=(k == n - 1))
                return last

            def norm_sums():
                base = norms[0] * KT
                for k in range(KT):
                    pe.wait_ge(sq_ready, base + k + 1)
                    mm(ps[:, 0, :], ones, sq2[k % 2], start=(k == 0), stop=(k == KT - 1)).then_inc(sq_used, 1)
                norms[0] += 1

            w = Pieces()

            def piece(n, s, bank, hi, lo, tiles, first=0, total=None, fresh=False):
                pe.wait_ge(w_lo, n + 1)
                wh, wl = split_w[:, s, 0], split_w[:, s, 1]
                total = tiles if total is None else total
                for k in range(tiles):
                    if fresh:
                        pe.wait_ge(moving, moved[0] + k + 1)
                    o, t = k * P, first + k
                    mm(bank, wh[:, o:o + P], hi[:, t], start=(t == 0), stop=False)
                    mm(bank, wh[:, o:o + P], lo[:, t], start=False, stop=False)
                    last = mm(bank, wl[:, o:o + P], hi[:, t], start=False, stop=(t == total - 1))
                last.then_inc(w_used, 1)

            moved = [0]

            def square(hi, lo):
                with pe.Fori(0, 2) as i:
                    for m in range(NRAW):
                        pe.wait_ge(copied, w.copies + 4 * i + m + 1)
                        piece(w.n + NRAW * i + m, m % 2, ps[:, m, :], hi, lo, KT, fresh=(m == 0))
                w.add(KT, copies=KT)
                moved[0] += KT

            def mlp(l):
                with pe.Fori(0, FT // 2) as i:
                    for m in range(NRAW):
                        if m % 2 == 0:
                            pe.wait_ge(taken[m // 2], l * FT // 2 + i + 1)
                        piece(w.n + NRAW * i + m, m % 2, ps[:, m, :], h_hi, h_lo, KT, fresh=(m == 0))
                w.add(2 * FT)
                moved[0] += KT
                with pe.Fori(0, KT // 2) as i:
                    for s in range(2):
                        pe.wait_ge(copied, w.copies + 2 * i + s + 3)
                        for h in range(2):
                            if s == 0:
                                for x in range(2):
                                    pe.wait_ge(taken[x], l * FT // 2 + (FT // 2 + 1 if h else (FT // 2 + 1) // 2 + 1))
                            piece(w.n + NRAW * i + 2 * s + h, h, ps[:, 4 + s, :], ff_hi, ff_lo, FT // 2,
                                  h * FT // 2, FT)
                w.add(2 * KT, copies=KT)

            for n in range(ADA):
                pe.sem_inc(ada_done[n], 1)
            pe.wait_ge(loaded, 64)
            phase.end()
            def ada_columns(i, n):
                pe.wait_ge(ada_row, ADA * i + n + 1)
                pe.wait_ge(ada_taken, ADA * i + n + 1)
                pe.sem_inc(pe_tick, 1)
                for m in range(TOK // P):
                    last = tp(ps[:, 4 + n, 2 * m:2 * m + 2], ada_rows[n][:, m * P:(m + 1) * P], ident[0:NSEQ, 0:NSEQ])
                last.then_inc(ada_cols, 1)

            with pe.Fori(0, ADA_ROUNDS) as i:
                for n in range(ADA):
                    pe.wait_ge(ada_in[n], 16 * i + 16)
                    for k in range(KT):
                        last = mm(ps[0:NSEQ, n, :], csil[:, k, :], ada_blk[n][:, k, :], start=(k == 0), stop=(k == KT - 1))
                    last.then_inc(ada_done[n], 1)
                    if n > 0:
                        ada_columns(i, n - 1)
                ada_columns(i, ADA - 1)
            phase.end()
            norm_sums()
            phase.end()
            arrived(1)
            for k in range(KT):
                for n in range(3):
                    pe.wait_ge(mixed, k * 3 + n + 1)
                    last = mm(ps[:, 1 + n, :], ring[:, 1, (n * KT + k) * P:(n * KT + k + 1) * P],
                              mix4[(k * 3 + n) % 4], start=(k == 0), stop=(k == KT - 1))
                    last.then_inc(block_done[1] if k == KT - 1 and n == 2 else mixed_used, 1)
            slots.n[1] += 1
            phase.end()

            def pair(p, before, after):
                a, b = p + 1, p - 1
                w = ring[:, 0, :]

                def project(n, src, bank):
                    product(ps[:, bank, :], w[:, n * D:(n + 1) * D], src).then_inc(projected, 1)

                def next_keys(k):
                    if k == 0:
                        arrived(0, a)
                        later(bon_in, 2 * a)
                    last = mm(ps[:, 7, :], w[:, D + k * P:D + (k + 1) * P], xk[:, k], start=(k == 0), stop=(k == KT - 1))
                    if k == KT - 1:
                        last.then_inc(projected, 1)

                def next_key_squares():
                    pe.wait_ge(evac, 8 * a + 2)
                    mm(ps[:, 7, :], blk, t_sq, start=True, stop=True).then_inc(head_sum, 1)

                def next_lora(f, n):
                    lo, hi = halves[n]
                    mm(ps[:, 7, :], w[lo:hi, (24 + f) * P:(25 + f) * P], lora[lo:hi, f, :],
                       start=True, stop=True).then_inc(projected, 1)

                def next_wide(n, src, ks):
                    for k in ks:
                        last = mm(ps[:, 6, :], w[:, n * D + k * P:n * D + (k + 1) * P], src[:, k], start=(k == 0),
                                  stop=(k == KT - 1))
                    if k == KT - 1:
                        last.then_inc(projected if n == 0 else block_done[0], 1)

                def next_inputs(step):
                    if step == 0:
                        next_key_squares()
                    elif step == 1:
                        pe.wait_ge(norm_root, a + 1)
                        next_lora(1, 0)
                    elif step == 2:
                        pe.wait_ge(evac, 8 * a + 3)
                        next_lora(1, 1)
                        later(var_root, p)
                        next_wide(0, xr, range(4))
                    elif step == 3:
                        if before:
                            pe.wait_ge(gated, b + 1)
                        else:
                            pe.wait_ge(evac, 8 * a + 4)
                        next_lora(0, 0)
                        next_wide(0, xr, range(4, 8))
                    elif step == 4:
                        pe.wait_ge(evac, 8 * a + 5)
                        next_lora(0, 1)
                        pe.wait_ge(evac, 8 * a + 6)
                        next_wide(2, xv, range(3))

                def next_bonus():
                    pe.wait_ge(evac, 8 * a + 7)
                    pe.wait_ge(bon_in, 2 * a + 1)
                    mm(ps[:, 7, :], blk, t_sq, start=True, stop=True).then_inc(head_sum, 1)

                def group_norm(step):
                    if step == 0:
                        later(norm_root, p + 1)
                        mm(ps[:, 6, :], blk, o_res[:, b, :], start=True, stop=True).then_inc(mean_mm, 1)
                    elif step == 1:
                        pe.wait_ge(dev_sq, b + 1)
                        mm(ps[:, 6, :], blk, c_sq, start=True, stop=True).then_inc(var_mm, 1)
                    else:
                        if after:
                            pe.wait_ge(evac, 8 * a + 4)
                        pe.wait_ge(gate_in, 16 * b + 16)
                        mm(ps[:, 7, :], gbt[:], lora[:, 2, :], start=True, stop=True).then_inc(gate_mm, 1)

                pe.wait_ge(prep, 2 * p + 2)
                pe.wait_ge(s_ev[0], (CPS - 1) * p) if before else None
                pe.sem_inc(pe_tick, 1)
                for n in range(NDIR):
                    for c in range(NCH):
                        for lo, hi in halves:
                            last = mm(ps[lo:hi, 2 + n, c * C:(c + 1) * C], arn[lo:hi, n, c, 0:C], kbn[lo:hi, n, c, C:P],
                                      start=True, stop=True)
                    last.then_inc(sys, 1)
                for g in range(8):
                    n, h, q = g // 4, (g // 2) % 2, g % 2
                    bank = (4, 5, 0, 1)[g % 4]
                    if g == 2 and before:
                        pe.wait_ge(y_in, b + 1)
                    if g >= 4:
                        pe.wait_ge(gram_in, 8 * p + g - 3)
                    lo, hi = halves[h]
                    for c in range(4):
                        last = mm(ps[:, bank, c * P:(c + 1) * P], kbn[lo:hi, n, 4 * q + c, :], arn[lo:hi, n, 4 * q + c, :],
                                  start=True, stop=True)
                    last.then_inc(gram, 1)
                    if after:
                        next_keys(g)
                if before:
                    group_norm(0)
                for g in range(6):
                    bank = (4, 5, 0, 1)[g % 4]
                    if g < 4:
                        pe.wait_ge(gram_in, 8 * p + 5 + g)
                    else:
                        pe.wait_ge(tr_in, 6 * p + g - 3)
                        pe.sem_inc(pe_tick, 1)
                    for c in range(4):
                        if g < 4:
                            last = tp(ps[:, bank, c * P:(c + 1) * P], kbn[:, g // 2, 4 * (g % 2) + c, :], ident)
                        else:
                            cc = 4 * (g - 4) + c
                            last = tp(ps[0:C, bank, c * P:(c + 1) * P], t_v[:, cc * C:(cc + 1) * C], ident)
                    last.then_inc(tr, 1)
                pe.wait_ge(tr_in, 6 * p + 6)
                for n in range(NDIR):
                    pe.wait_ge(ident_in, 2 * p + n + 1)
                    for c in range(NCH):
                        last = tp(ps[:, 2 * n + c // 4, (c % 4) * P:(c % 4 + 1) * P], mt[:, n, c, :], ident)
                    last.then_inc(tmm[n], 1)
                for l in range(LEVELS):
                    for n in range(NDIR):
                        pe.wait_ge(mev[n], LEVELS * p + l + 1)
                        pe.sem_inc(pe_tick, 1)
                        for c in range(NCH):
                            for lo, hi in halves:
                                last = mm(ps[lo:hi, 4 + n, c * C:(c + 1) * C], nt[lo:hi, n, c, lo:hi], mc[lo:hi, n, c, :],
                                          start=True, stop=True)
                        last.then_inc(xmm[n], 1)
                    if l > 0:
                        for n in range(NDIR):
                            for c in range(NCH):
                                last = tp(ps[0:C, 2 * n + c // 4, (c % 4) * P:(c % 4 + 1) * P], mc[:, n, c, :], ident)
                            last.then_inc(tmm[n], 1)
                    if l == 1 and before:
                        group_norm(1)
                    if after:
                        next_inputs(l)
                    if l == 2 and before:
                        group_norm(2)
                    for n in range(NDIR):
                        if l > 0:
                            pe.wait_ge(tev[n], (LEVELS - 1) * p + l)
                        pe.wait_ge(xev[n], LEVELS * p + l + 1)
                        if l < LEVELS - 1:
                            pe.sem_inc(pe_tick, 1)
                            for c in range(NCH):
                                for lo, hi in halves:
                                    last = mm(ps[lo:hi, 4 + n, c * C:(c + 1) * C], mt[lo:hi, n, c, lo:hi],
                                              xc[lo:hi, n, c, :], start=True, stop=True)
                            last.then_inc(mmm[n], 1)
                        else:
                            pe.sem_inc(pe_tick, 1)
                            for c in range(NCH):
                                for h, (lo, hi) in enumerate(halves):
                                    last = mm(ps[0:C, 2 * n + h, c * C:(c + 1) * C], mt[lo:hi, n, c, lo:hi], xc[lo:hi, n, c, :],
                                              start=True, stop=True)
                            last.then_inc(fmm[n], 1)
                pe.wait_ge(carried, p + 1)
                for j in range(CPS):
                    cs = [[q * CPS + (j if n == 0 else CPS - 1 - j) for q in range(NSEQ)] for n in range(NDIR)]
                    st = sx[:, j % 2]
                    for n in range(NDIR):
                        if j == 0:
                            pe.wait_ge(fev[n], p + 1)
                        else:
                            pe.wait_ge(s_ev[n], (CPS - 1) * p + j)
                        pe.sem_inc(pe_tick, 1)
                        for q in range(NSEQ):
                            c, o = cs[n][q], q * P
                            if j > 0:
                                mm(ps[0:C, 4 + n, o:o + P], ar[:, n, c, 0:C], st[:, n, q, :], start=True, stop=False)
                            for h in range(2):
                                last = mm(ps[0:C, 4 + n, o + h * C:o + (h + 1) * C], gm[0:C, n, h, c, 0:C],
                                          wv[0:C, c, h * C:(h + 1) * C], start=(j == 0), stop=(j == 0 or h == 1))
                        last.then_inc(x0_mm[n], 1)
                    if j == 0 and after:
                        next_wide(2, xv, range(3, 6))
                    for n in range(NDIR):
                        pe.wait_ge(x0_ev[n], CPS * p + j + 1)
                        pe.sem_inc(pe_tick, 1)
                        for q in range(NSEQ):
                            for h in range(2):
                                o = 256 + q * P + h * C
                                last = mm(ps[C:P, 4 + n, o:o + C], mf[:, n, cs[n][q], h, :],
                                          x0s[:, n, q, h * C:(h + 1) * C], start=True, stop=True)
                        last.then_inc(u_mm[n], 1)
                    if j == 1 and after:
                        next_wide(2, xv, range(6, 8))
                        next_bonus()
                    if j < CPS - 1:
                        for n in range(NDIR):
                            pe.wait_ge(u_ev[n], CPS * p + j + 1)
                            for q in range(NSEQ):
                                last = mm(ps[:, 4 + n, q * P:(q + 1) * P], kb[:, n, cs[n][q], :], wv[:, cs[n][q], :],
                                          start=True, stop=True)
                            last.then_inc(s_mm[n], 1)
                    for n in range(NDIR):
                        if j == CPS - 1:
                            pe.wait_ge(u_ev[n], CPS * p + j + 1)
                        for q in range(NSEQ):
                            c = cs[n][q]
                            if j > 0:
                                mm(ps[:, n, c * C:(c + 1) * C], st[:, n, q, :], ar[:, n, c, C:P], start=True, stop=False)
                            for h, (lo, hi) in enumerate(halves):
                                last = mm(ps[lo:hi, n, c * C:(c + 1) * C], wv[:, c, lo:hi], gm[:, n, h, c, C:P],
                                          start=(j == 0), stop=True)
                        last.then_inc(y_mm, 1)

            def later(s, v):
                if not isinstance(v, int) or v > 0:
                    pe.wait_ge(s, v)

            def first_inputs():
                w = ring[:, 0, :]
                arrived(0, 0)
                def wide(bank, n, src):
                    return product(ps[:, bank, :], w[:, n * D:(n + 1) * D], src)

                def second(bank, f, n):
                    lo, hi = halves[n]
                    mm(ps[:, bank, :], w[lo:hi, (24 + f) * P:(25 + f) * P], lora[lo:hi, f, :],
                       start=True, stop=True).then_inc(projected, 1)

                wide(7, 1, xk).then_inc(projected, 1)
                second(2, 1, 0)
                second(3, 1, 1)
                second(0, 0, 0)
                wide(5, 0, xr).then_inc(projected, 1)
                second(1, 0, 1)
                wide(4, 2, xv).then_inc(block_done[0], 1)
                pe.wait_ge(evac, 2)
                mm(ps[:, 6, :], blk, t_sq, start=True, stop=True).then_inc(head_sum, 1)
                pe.wait_ge(bon_in, 1)
                mm(ps[:, 7, :], blk, t_sq, start=True, stop=True).then_inc(head_sum, 1)

            first_inputs()
            pair(0, False, True)
            with pe.Fori(1, KT - 1) as p:
                pair(p, True, True)
            pair(KT - 1, True, False)
            pe.wait_ge(y_in, KT)
            mm(ps[:, 6, :], blk, o_res[:, KT - 1, :], start=True, stop=True).then_inc(mean_mm, 1)
            pe.wait_ge(dev_sq, KT)
            mm(ps[:, 2, :], blk, c_sq, start=True, stop=True).then_inc(var_mm, 1)
            pe.wait_ge(gated, KT - 1)
            pe.wait_ge(gate_in, 16 * KT)
            mm(ps[:, 7, :], gbt[:], lora[:, 2, :], start=True, stop=True).then_inc(gate_mm, 1)
            slots.n[0] += KT
            phase.end()
            square(o_hi, o_lo)
            phase.end()
            norm_sums()
            phase.end()
            norm_sums()
            mlp(0)
            phase.end()
            norm_sums()
            phase.end()
            norm_sums()

            pe.sem_inc(a_pv, 1)
            for m, bank in enumerate((0, 1, 6, 7)):
                piece(w.n + m, m % 2, ps[:, bank, :], att_hi, h_lo, KT, fresh=(m == 0))
                if m >= KVH:
                    pe.wait_ge(a_ev, m - KVH + 1)
                    mm(ps[:, 2 + m - KVH, :], ones, asq[m - KVH], start=True, stop=True).then_inc(a_ss, 1)
            w.add(2 * KVH)
            moved[0] += KT
            for s in range(2):
                piece(w.n + s, s, ps[:, s, :], att_hi, h_lo, KT)
                pe.wait_ge(v_tr, s + 1)
                for b in range(4):
                    last = tp(ps[:, 4 + s, b * P:(b + 1) * P], qh[s][:, b * P:(b + 1) * P], ident)
                last.then_inc(a_tr, 1)

            def query_squares(h, s):
                pe.wait_ge(a_ev, KVH + h + 1)
                pe.wait_ge(a_rt, h + KVH - 1)
                mm(ps[:, 2 + s, :], ones, asq[s], start=True, stop=True).then_inc(a_ss, 1)

            for s in range(2):
                query_squares(s, s)
            pe.wait_ge(v_in, KVH)

            def heads(j, g, ahead):
                for s in range(2):
                    h = 2 * j + s
                    pe.wait_ge(a_q, KVH + 1 + h)
                    pe.wait_ge(a_ex, h + 1)
                    for q in range(NSEQ):
                        for b in range(2):
                            o = q * SEQ + b * P
                            last = mm(ps[:, 4 + q, b * SEQ:(b + 1) * SEQ], qh[s][:, o:o + P],
                                      kh[:, g, q * SEQ:(q + 1) * SEQ], start=True, stop=True)
                    last.then_inc(a_sc, 1)
                    if s == 1:
                        weighted(h - 1, 0, g, ahead)
                    if ahead:
                        pe.wait_ge(a_o, h + 1)
                        piece(w.n + h + 2, s, ps[:, s, :], att_hi, h_lo, KT)
                    pe.wait_ge(a_p, h + 1)
                    pe.wait_ge(a_te, h + 1)
                    for q in range(NSEQ):
                        for k in range(2):
                            for b in range(2):
                                o = (k * 2 + b) * P
                                last = tp(ps[:, 6 + q, o:o + P], prob[:, 2 * q + b, k * P:(k + 1) * P], ident)
                    last.then_inc(a_tr, 1)
                weighted(h, 1, g, ahead)

            def weighted(h, s, g, ahead):
                if ahead:
                    query_squares(h + 2, s)
                pe.wait_ge(a_te, h + 2)
                for q in range(NSEQ):
                    for k in range(2):
                        last = mm(ps[:, s, q * SEQ:(q + 1) * SEQ], vh[:, g, 2 * q + k, :], prT[:, q, k, :],
                                  start=(k == 0), stop=(k == 1))
                last.then_inc(a_pv, 1)

            with pe.Fori(0, 2) as j:
                heads(j, 0, True)
            heads(2, 1, True)
            heads(3, 1, False)
            w.add(QH, 2)
            phase.end()
            square(o_hi, o_lo)
            phase.end()
            norm_sums()
            phase.end()
            norm_sums()
            mlp(1)
            phase.end()
            norm_sums()
            phase.end()

        @block.scalar
        def _(act):
            A = nc.scalar.activation
            slots = Slots()
            phase = Phases(act)
            norms = [0]
            gq, gk = pt[:, C_QKG:C_QKG + 1], pt[:, C_QKG + 1:C_QKG + 2]

            def norm_squares(src):
                base = norms[0] * KT
                for k in range(KT):
                    if base + k >= 2:
                        act.wait_ge(sq_used, base + k - 1)
                    A(sq2[k % 2], src[:, k, :], ACT.Square).then_inc(sq_ready, 1)
                act.wait_ge(sq_used, base + KT)
                A(rs, ps[:, 0, :], ACT.Sqrt, bias=ct[:, K_EPS:K_EPS + 1]).then_inc(root, 1)
                norms[0] += 1

            def norm_affine(l, shift):
                base = (norms[0] - 1) * KT
                for k in range(KT):
                    act.wait_ge(scaled, base + k + 1)
                    for q in range(NSEQ):
                        last = A(h_in[:, k, q, :], tmp2[k % 2][:, q * SEQ:(q + 1) * SEQ], ACT.Identity,
                                 scale=gs[:, k, q:q + 1], bias=mod[:, (6 * l + shift) * KT + k, q:q + 1])
                    last.then_inc(scaled_used, 1)

            w = Pieces()

            def used(n):
                act.wait_ge(w_used, n + 1)

            def high(n, r, count, cols=D):
                act.wait_ge(piece_in[r], 16 * count + 16)
                if not isinstance(n, int) or n >= 2:
                    act.wait_ge(w_used, n - 1)
                A(split_w[:, r % 2, 0, 0:cols], raw_w[:, r, 0:cols], ACT.Copy).then_inc(w_hi, 1)

            def high_input():
                for k in range(KT):
                    A(o_hi[:, k, :], o_res[:, k, :], ACT.Copy).then_inc(h_high, 1)

            def square(next_cols=D):
                for m in range(KT):
                    used(w.n + m)
                    A(mix_out[:, m, :], ps[:, m % NRAW, :], ACT.Copy).then_inc(copied, 1)
                    high(w.n + m + 2, (m + 2) % NRAW, w.slot[(m + 2) % NRAW] + (m + 2) // NRAW)
                w.add(KT)

            def mlp(l, last_mlp):
                def up_round(i, cols):
                    for s in range(2):
                        n = w.n + NRAW * i + 2 * s
                        used(n)
                        r = (2 * s + 2) % NRAW
                        high(n + 2, r, w.slot[r] + i + s, cols if s else D)
                        act.wait_ge(fcols, l * FT + 2 * i + s + 1)
                        act.wait_ge(taken[s], l * FT // 2 + i + 1)
                        A(u_pad[s][:, :, 1:SEQ + 1], seqs(ps[:, 2 * s, :]), ACT.Copy)
                        A(conv[s], ps[:, 2 * s, :], ACT.Identity, scale=fcur[:, s, 1:2],
                          bias=fcur[:, s, 3:4]).then_inc(u_ready, 1)
                        high(n + 3, r + 1, w.slot[r + 1] + i + s, cols if s else D)
                        act.wait_ge(conv_ready, l * FT + 2 * i + s + 1)
                        A(conv[s], conv[s], ACT.Silu).then_inc(silu_ready, 1)

                def down_round(i, ahead):
                    for s in range(2):
                        for h in range(2):
                            n = w.n + NRAW * i + 2 * s + h
                            used(n)
                            if h == 1:
                                A(o_res[:, bass.ds(2 * i + s, 1), :], ps[:, 4 + s:5 + s, :], ACT.Copy).then_inc(copied, 1)
                            r = (2 * s + h + 2) % NRAW
                            if s == 0 or ahead:
                                high(n + 2, r, w.slot[r] + i + s, D if s == 1 and ahead == D else PIECE)

                with act.Fori(0, FT // 2 - 1) as i:
                    up_round(i, D)
                up_round(FT // 2 - 1, PIECE)
                w.add(2 * FT)
                with act.Fori(0, KT // 2 - 1) as i:
                    down_round(i, PIECE)
                down_round(KT // 2 - 1, 0 if last_mlp else D)
                w.add(2 * KT)

            act.wait_ge(loaded, 64)
            A(csil[:], csil[:], ACT.Silu)
            phase.end()
            with act.Fori(0, ADA_ROUNDS) as i:
                for n in range(ADA):
                    act.wait_ge(ada_done[n], i + 2)
                    A(ada_rows[n], ps[0:NSEQ, n, :], ACT.Copy).then_inc(ada_row, 1)
            phase.end()
            norm_squares(x_res)
            norm_affine(0, 0)
            phase.end()
            slots.n[1] += 1
            act.wait_ge(block_done[1], slots.n[1])
            A(lora[:, 0, :], ps[:, 1, :], ACT.Tanh)
            A(lora[:, 1, :], ps[:, 2, :], ACT.Copy)
            A(lora[:, 2, :], ps[:, 3, :], ACT.Sigmoid)
            phase.end()

            pairs = [ps[:, 2 * n:2 * n + 2, :].rearrange("p b (c s) -> p (b c) s", s=P) for n in range(NDIR)]

            def next_inputs(a, step, banks=(7, 6, 6, 7, 7, 7, 7, 7)):
                bk, br, bv, bw0, bw1, ba0, ba1, bn = banks

                def sigmoid(count, dst, bank, col):
                    act.wait_ge(projected, 6 * a + count)
                    A(dst, ps[:, bank, :], ACT.Sigmoid, bias=pc(col)).then_inc(evac, 1)

                if step == 0:
                    act.wait_ge(projected, 6 * a + 1)
                    act.wait_ge(pcols, a + 1)
                    if not isinstance(a, int) or a > 0:
                        act.wait_ge(carried, a)
                    A(t_k, ps[:, bk, :], ACT.Copy).then_inc(evac, 1)
                    A(t_sq, ps[:, bk, :], ACT.Square, scale=pc(4)).then_inc(evac, 1)
                elif step == 1:
                    act.wait_ge(head_sum, 2 * a + 1)
                    A(t_b1, ps[:, bn, :], ACT.Sqrt, scale=float(HEAD)).then_inc(norm_root, 1)
                elif step == 2:
                    sigmoid(2, t_a[0], ba0, 2)
                elif step == 3:
                    sigmoid(3, t_a[1], ba1, 3)
                elif step == 4:
                    sigmoid(4, s_w[0], bw0, 0)
                elif step == 5:
                    act.wait_ge(projected, 6 * a + 5)
                    A(t_r, ps[:, br, :], ACT.Copy).then_inc(evac, 1)
                    sigmoid(6, s_w[1], bw1, 1)
                elif step == 6:
                    act.wait_ge(block_done[0], slots.n[0] + a + 1)
                    A(t_v, ps[:, bv, :], ACT.Copy).then_inc(evac, 1)
                else:
                    n = step - 7
                    act.wait_ge(cum, 2 * a + n + 1)
                    A(s_e2, s_inc, ACT.Exp, scale=DECAY).then_inc(expd, 1)
                    A(s_exc, s_exc, ACT.Exp, scale=-DECAY).then_inc(expd, 1)
                    act.wait_ge(expd, 6 * a + 3 * n + 2)
                    A(s_inc, s_inc, ACT.Exp, scale=-DECAY).then_inc(expd, 1)

            def pair(p, before, after):
                a, b = p + 1, p - 1
                for g in range(6):
                    act.wait_ge(tr, 6 * p + g + 1)
                    bank = (4, 5, 0, 1)[g % 4]
                    dst = kb[:, g // 2, 4 * (g % 2):4 * (g % 2) + 4, :] if g < 4 else wv[0:C, 4 * (g - 4):4 * (g - 3), :]
                    src = ps[:, bank, :] if g < 4 else ps[0:C, bank, :]
                    A(dst, src.rearrange("p (c s) -> p c s", c=4), ACT.Copy).then_inc(tr_in, 1)
                if before:
                    act.wait_ge(centred, b + 1)
                    act.sem_inc(act_tick, 1)
                    A(c_sq, o_res[:, b, :], ACT.Square).then_inc(dev_sq, 1)
                if after:
                    next_inputs(a, 0)
                for n in range(NDIR):
                    act.wait_ge(tmm[n], LEVELS * p + 1)
                    A(mc[0:C, n, :, :], pairs[n][0:C, :, 0:C], ACT.Copy)
                    A(mc[C:P, n, :, :], pairs[n][C:P, :, C:P], ACT.Copy).then_inc(mev[n], 1)
                for l in range(LEVELS):
                    if l > 0:
                        act.wait_ge(tmm[0], LEVELS * p + l + 1)
                        A(mt[0:C, 0, :, 0:C], pairs[0][0:C, :, 0:C], ACT.Copy)
                        A(mt[C:P, 0, :, C:P], pairs[0][0:C, :, C:P], ACT.Copy).then_inc(tev[0], 1)
                    if l == 1 and before:
                        act.wait_ge(var_mm, b + 1)
                        A(c_b, ps[:, 6, :], ACT.Sqrt, bias=ct[:, K_EPS + 1:K_EPS + 2]).then_inc(var_root, 1)
                    if after:
                        next_inputs(a, l + 1)
                    if l < LEVELS - 1:
                        for n in range(NDIR):
                            act.wait_ge(mmm[n], (LEVELS - 1) * p + l + 1)
                            A(mc[:, n, :, :], chunks(ps[:, 4 + n, :]), ACT.Copy).then_inc(mev[n], 1)
                for n in range(NDIR):
                    act.wait_ge(fmm[n], p + 1)
                    for h in range(2):
                        last = A(mf[:, n, :, h, :], chunks(ps[0:C, 2 * n + h, :]), ACT.Copy)
                    last.then_inc(fev[n], 1)
                for j in range(CPS):
                    for n in range(NDIR):
                        act.wait_ge(x0_mm[n], CPS * p + j + 1)
                        A(x0s[:, n, :, :], ps[0:C, 4 + n, 0:2 * P].rearrange("p (q i) -> p q i", q=NSEQ),
                          ACT.Copy).then_inc(x0_ev[n], 1)
                    if after and j == 1:
                        next_inputs(a, 7)
                        next_inputs(a, 6)
                    if after and j == 3:
                        next_inputs(a, 8)
                act.wait_ge(y_mm, 2 * CPS * (p + 1))
                act.sem_inc(act_tick, 1)
                A(o_res[:, p, :], ps[:, 0, :], ACT.Copy).then_inc(y_cp, 1)

            for step in range(9):
                next_inputs(0, step, (7, 5, 4, 0, 1, 2, 3, 6))
            pair(0, False, True)
            with act.Fori(1, KT - 1) as p:
                pair(p, True, True)
            pair(KT - 1, True, False)
            act.wait_ge(centred, KT)
            A(c_sq, o_res[:, KT - 1, :], ACT.Square).then_inc(dev_sq, 1)
            act.wait_ge(var_mm, KT)
            A(c_b, ps[:, 2, :], ACT.Sqrt, bias=ct[:, K_EPS + 1:K_EPS + 2]).then_inc(var_root, 1)
            slots.n[0] += KT
            phase.end()
            high_input()
            for m in range(2):
                high(m, m, 0)
            square()
            phase.end()
            norm_squares(mix_out)
            phase.end()
            norm_squares(x_res)
            norm_affine(0, 3)
            mlp(0, False)
            phase.end()
            norm_squares(o_res)
            phase.end()
            norm_squares(x_res)
            norm_affine(1, 0)
            for x in range(KVH):
                used(w.n + x)
                high(w.n + x + 2, x + 2, w.slot[x + 2])
                A(raw[x], ps[:, x, :], ACT.Identity, scale=gk)
                A(asq[x], ps[:, x, :], ACT.Square).then_inc(a_ev, 1)
            for g in range(KVH):
                used(w.n + KVH + g)
                high(w.n + 2 * KVH + g, g, w.slot[g] + 1)
                A(qh[g], ps[:, 6 + g, :], ACT.Copy).then_inc(v_tr, 1)
            w.add(2 * KVH)

            def root_of(n, s):
                act.wait_ge(a_ss, n + 1)
                act.wait_ge(a_q, n - 1)
                A(ars[s], ps[:, 2 + s, :], ACT.Sqrt, scale=float(D // AH), bias=ct[:, K_EPS:K_EPS + 1]).then_inc(a_rt, 1)

            def query(h, s, n):
                used(w.n + h)
                high(w.n + h + 2, s, w.slot[s] + n)
                act.wait_ge(a_q, h + 1)
                A(raw[s], ps[:, s, :], ACT.Identity, scale=gq)
                A(asq[s], ps[:, s, :], ACT.Square).then_inc(a_ev, 1)

            for x in range(KVH):
                act.wait_ge(a_ss, x + 1)
                A(ars[x], ps[:, 2 + x, :], ACT.Sqrt, scale=float(D // AH), bias=ct[:, K_EPS:K_EPS + 1]).then_inc(a_rt, 1)
            for s in range(2):
                query(s, s, 1)
                act.wait_ge(a_tr, s + 1)
                A(vh[:, s, :, :], ps[:, 4 + s, :].rearrange("p (b d) -> p b d", b=4), ACT.Copy).then_inc(v_in, 1)
            for s in range(2):
                root_of(KVH + s, s)

            def heads(j, ahead):
                for s in range(2):
                    h = 2 * j + s
                    act.wait_ge(a_mx, h + 1)
                    act.wait_ge(a_tr, KVH + h)
                    for b in range(4):
                        last = A(prob[:, b, :], ps[:, 4 + b // 2, (b % 2) * SEQ:(b % 2 + 1) * SEQ], ACT.Exp,
                                 scale=float(AH) ** -0.5, bias=stat[:, 4 + b:5 + b], accum_out=stat[:, 8 + b:9 + b])
                    last.then_inc(a_ex, 1)
                    if s == 1 and ahead:
                        root_of(KVH + h + 1, 0)
                    if ahead:
                        query(h + 2, s, j + 2)
                    act.wait_ge(a_tr, KVH + h + 1)
                    act.wait_ge(a_pv, h + 1)
                    for q in range(NSEQ):
                        last = A(prT[:, q, :, :], ps[:, 6 + q, :].rearrange("p (k t) -> p k t", k=2), ACT.Copy)
                    last.then_inc(a_te, 1)
                if ahead:
                    root_of(KVH + h + 2, 1)

            act.sem_inc(a_ex, 1)
            act.sem_inc(a_te, 1)
            with act.Fori(0, 2) as j:
                heads(j, True)
            heads(2, True)
            heads(3, False)
            w.add(QH, 2)
            phase.end()
            high_input()
            square()
            phase.end()
            norm_squares(mix_out)
            phase.end()
            norm_squares(x_res)
            norm_affine(1, 3)
            mlp(1, True)
            phase.end()
            norm_squares(o_res)
            phase.end()

        @block.vector
        def _(dve):
            own = Own(dve, dve_own)
            phase = Phases(dve)
            V = nc.vector
            norms = [0]

            def gains(l, norm, part_, pre):
                g = pt[:, C_NORM + (4 * l + norm) * KT:C_NORM + (4 * l + norm + 1) * KT].unsqueeze(2).broadcast_to([P, KT, NSEQ])
                m = mod[:, (6 * l + part_) * KT:(6 * l + part_ + 1) * KT, :]
                own.wait()
                own(V.scalar_tensor_tensor(gs[:], m, 1.0 if pre else 0.0, g, ALU.add, ALU.mult))

            def inverse_root():
                dve.wait_ge(root, norms[0] + 1)
                return V.reciprocal(rs, rs)

            highs = [0]

            def low_input(k, src, lo, hi):
                highs[0] += 1
                dve.wait_ge(h_high, highs[0])
                V.tensor_tensor(lo, src, hi.bitcast(F32), ALU.subtract).then_inc(moving, 1)

            def pre_norm(l, norm, scale_part, hi=None):
                gains(l, norm, scale_part, True)
                own.wait()
                own(inverse_root())
                own.wait()
                base = norms[0] * KT
                for k in range(KT):
                    if base + k >= 2:
                        dve.wait_ge(scaled_used, base + k - 1)
                    own.wait()
                    V.tensor_tensor(tmp2[k % 2], x_res[:, k, :], rs, ALU.mult).then_inc(scaled, 1)
                    if hi is not None and k >= 2:
                        low_input(k - 2, h_in[:, k - 2], h_lo[:, k - 2], seqs(hi[:, k - 2, :]))
                if hi is not None:
                    for k in range(KT - 2, KT):
                        low_input(k, h_in[:, k], h_lo[:, k], seqs(hi[:, k, :]))
                norms[0] += 1

            def post_norm(l, norm, gate_part):
                gains(l, norm, gate_part, False)
                own.wait()
                inverse_root().then_inc(rstd, 1)
                base = norms[0] * KT
                for k in range(KT):
                    dve.wait_ge(scaled, base + k + 1)
                    for q in range(NSEQ):
                        xs = x_res[:, k, q * SEQ:(q + 1) * SEQ]
                        own.wait()
                        last = V.scalar_tensor_tensor(xs, tmp2[k % 2][:, q * SEQ:(q + 1) * SEQ], gs[:, k, q:q + 1], xs,
                                                      ALU.mult, ALU.add)
                    last.then_inc(scaled_used, 1)
                norms[0] += 1

            def mlp(l):
                own.loop_start()
                with dve.Fori(0, FT // 2) as i:
                    for s in range(2):
                        own.wait()
                        V.tensor_copy(fcur[:, s, :], pt[:, bass.ds(C_FFN + 4 * (l * FT + s) + 8 * i, 4)]).then_inc(fcols, 1)
                    for s in range(2):
                        dve.wait_ge(u_ready, l * FT + 2 * i + s + 1)
                        own.wait()
                        own(V.scalar_tensor_tensor(seqs(conv[s]), u_pad[s][:, :, 0:SEQ], fcur[:, s, 0:1], seqs(conv[s]),
                                                   ALU.mult, ALU.add))
                        own.wait()
                        V.scalar_tensor_tensor(seqs(conv[s]), u_pad[s][:, :, 2:SEQ + 2], fcur[:, s, 2:3], seqs(conv[s]),
                                               ALU.mult, ALU.add).then_inc(conv_ready, 1)
                        dve.wait_ge(silu_ready, l * FT + 2 * i + s + 1)
                        dve.wait_ge(w_used, mlp_base[l] + NRAW * i + 2 * s + 2)
                        own(V.tensor_tensor(conv[s], conv[s], ps[:, 2 * s + 1, :], ALU.mult))
                        own.wait()
                        own(V.tensor_copy(ff_hi[:, bass.ds(2 * i + s, 1), :].squeeze(1), conv[s]))
                        own.wait()
                        V.tensor_tensor(ff_lo[:, bass.ds(2 * i + s, 1), :].squeeze(1), conv[s],
                                        ff_hi[:, bass.ds(2 * i + s, 1), :].squeeze(1).bitcast(F32),
                                        ALU.subtract).then_inc(taken[s], 1)
                    own.loop_end()

            mlp_base = (KT, 3 * KT + 2 * FT + 2 * KVH + QH + KT)
            for s in range(2):
                dve.sem_inc(taken[s], 1)
            dve.sem_inc(copied, NRAW)
            dve.sem_inc(ada_taken, ADA)
            dve.sem_inc(a_o, 2)
            dve.wait_ge(loaded, 64)
            pair_tab = pt[:, C_PAIR:C_PAIR + KT * NPP].rearrange("p (k n) -> p k n", n=NPP)
            own.wait()
            own(V.tensor_scalar(derived[:, :, 0:1], pair_tab[:, :, 4:5], -1.0, None, ALU.mult))
            own.wait()
            own(V.tensor_scalar(derived[:, :, 1:2], pair_tab[:, :, 5:6], -1.0, 1.0, ALU.mult, ALU.add))
            phase.end()
            with dve.Fori(0, ADA_ROUNDS) as i:
                for n in range(ADA):
                    dve.wait_ge(ada_cols, ADA * i + n + 1)
                    o, m = 4 * ADA * i + 4 * n, TOK // P
                    b = pt[:, bass.ds(C_ADAB + o, m)].unsqueeze(2).broadcast_to([P, m, NSEQ])
                    V.tensor_tensor(mod[:, bass.ds(o, m), :], ps[:, 4 + n, 0:2 * m].rearrange("p (m q) -> p m q", m=m), b,
                                    ALU.add).then_inc(ada_taken, 1)
            phase.end()
            pre_norm(0, 0, 1)
            phase.end()
            n_ring = 0
            for k in range(KT):
                hk = h_pad[:, k]
                own.wait()
                own(V.tensor_tensor(seqs(hsum), hk[:, :, 0:SEQ], hk[:, :, 2:SEQ + 2], ALU.add))
                own.wait()
                own(V.scalar_tensor_tensor(seqs(xx), seqs(hsum), 0.5, h_in[:, k], ALU.mult, ALU.subtract))
                own.wait()
                mu = lambda n: pt[:, C_MU + n * KT + k:C_MU + n * KT + k + 1]
                for n in (1, 4, 5):
                    if n_ring >= 4:
                        dve.wait_ge(mixed_used, n_ring - 3)
                    own.wait()
                    V.scalar_tensor_tensor(seqs(mix4[n_ring % 4]), seqs(xx), mu(n), h_in[:, k], ALU.mult,
                                           ALU.add).then_inc(mixed, 1)
                    n_ring += 1
                for n, dst in ((0, xr), (2, xk), (3, xv)):
                    own.wait()
                    own(V.scalar_tensor_tensor(seqs(dst[:, k, :]), seqs(xx), mu(n), h_in[:, k], ALU.mult, ALU.add))
            own.wait()
            phase.end()

            pairs = [ps[:, 2 * n:2 * n + 2, :].rearrange("p b (c s) -> p (b c) s", s=P) for n in range(NDIR)]
            res = ct[:, K_RES:K_RES + TOK]

            def pair_columns(a):
                own(V.tensor_copy(pcur[:, 0:NPP], pt[:, bass.ds(C_PAIR + NPP * a, NPP)]))
                V.tensor_copy(pcur[:, NPP:NPP + 2], derived[:, bass.ds(a, 1), :].squeeze(1)).then_inc(pcols, 1)
                dve.wait_ge(pcols, a + 1)

            def key_direction(a):
                dve.wait_ge(norm_root, a + 1)
                own(V.tensor_scalar_max(t_b1, t_b1, 1e-12))
                own.wait()
                own(V.reciprocal(t_b1, t_b1))
                own.wait()
                own(V.scalar_tensor_tensor(t_nkk, t_k, pc(NPP), t_b1, ALU.mult, ALU.mult))
                own.wait()

            def rates(a):
                dve.wait_ge(evac, 8 * a + 4)
                for n in range(NDIR):
                    own(V.scalar_tensor_tensor(t_b[n], t_nkk, -1.0, t_a[n], ALU.mult, ALU.mult))
                own.wait()
                for n in range(NDIR):
                    last = V.tensor_scalar(t_a[n], t_a[n], pc(5), pc(NPP + 1), ALU.mult, ALU.add)
                last.then_inc(kdf, 1)

            def decays(a):
                dve.wait_ge(evac, 8 * a + 5)
                V.tensor_tensor_scan(s_inc, res, s_w[0], 0.0, ALU.mult, ALU.add).then_inc(scanned, 1)

            def bonus(a, step):
                if step == 0:
                    dve.wait_ge(kd_sum, a + 1)
                    dve.wait_ge(evac, 8 * a + 6)
                    V.scalar_tensor_tensor(t_sq, t_r, pc(6), t_sq, ALU.mult, ALU.mult).then_inc(bon_in, 1)
                else:
                    dve.wait_ge(head_sum, 2 * a + 2)
                    dve.wait_ge(evac, 8 * a + 8)
                    dve.wait_ge(bon_copied, a) if not isinstance(a, int) or a > 0 else None
                    V.scalar_tensor_tensor(t_bonn, ps[:, 7, :], float(HEAD), t_v, ALU.mult, ALU.mult).then_inc(bon_in, 1)

            def decays_back(a, step):
                if step == 0:
                    dve.wait_ge(cum, 2 * a + 1)
                    dve.wait_ge(evac, 8 * a + 7)
                    own(V.tensor_tensor_scan(s_l, res, s_w[1], 0.0, ALU.mult, ALU.add))
                    dve.wait_ge(expd, 6 * a + 3)
                    V.tensor_copy(pendn[:, 0, :], chunks(s_inc)[:, :, C - 1])
                    own(V.tensor_tensor(arn[:, 0, :, 0:C], chunks(t_nkk), chunks(s_exc), ALU.mult))
                    own(V.tensor_tensor(arn[:, 0, :, C:P], chunks(t_r), chunks(s_inc), ALU.mult))
                    own.wait()
                else:
                    dve.wait_ge(prod, a + 1)
                    tot = chunks(s_l)[:, :, C - 1:C].broadcast_to([P, NCH, C])
                    own(V.tensor_tensor(chunks(s_exc), tot, chunks(s_l), ALU.subtract))
                    own.wait()
                    V.tensor_tensor(s_inc, s_exc, s_w[1], ALU.add).then_inc(cum, 1)

            def last_products(a):
                dve.wait_ge(expd, 6 * a + 6)
                V.tensor_copy(pendn[:, 1, :], chunks(s_inc)[:, :, 0])
                V.tensor_tensor(arn[:, 1, :, 0:C], chunks(t_nkk), chunks(s_exc), ALU.mult)
                V.tensor_tensor(arn[:, 1, :, C:P], chunks(t_r), chunks(s_inc), ALU.mult).then_inc(prep, 1)

            def centre(b, bank):
                dve.wait_ge(mean_mm, b + 1)
                V.tensor_tensor(o_res[:, b, :], o_res[:, b, :], ps[:, bank, :], ALU.subtract).then_inc(centred, 1)

            def finish(b, step):
                o = o_res[:, b, :]
                if step == 0:
                    dve.wait_ge(var_root, b + 1)
                    own(V.reciprocal(c_b, c_b))
                    own.wait()
                    own(V.tensor_tensor(o, o, c_b, ALU.mult))
                    own.wait()
                elif step == 1:
                    own(V.tensor_scalar(o, o, pt[:, bass.ds(C_PAIR + NPP * b + 7, 1)], pt[:, bass.ds(C_PAIR + NPP * b + 8, 1)],
                                        ALU.mult, ALU.add))
                    own.wait()
                    dve.wait_ge(bon_copied, b + 1)
                    own(V.tensor_tensor(o, o, t_bon, ALU.add))
                    own.wait()
                else:
                    dve.wait_ge(gate_mm, b + 2)
                    V.tensor_tensor(o, o, ps[:, 7, :], ALU.mult).then_inc(gated, 1)

            def pair(p, before, after):
                a, b = p + 1, p - 1
                for n in range(NDIR):
                    dve.wait_ge(sys, 2 * p + n + 1)
                    msk = ct[:, K_NT + n * C:K_NT + (n + 1) * C].unsqueeze(1).broadcast_to([P, NCH, C])
                    for h, (lo, hi) in enumerate(halves):
                        last = V.tensor_tensor(nt[lo:hi, n, :, lo:hi], chunks(ps[lo:hi, 2 + n, :]), msk[lo:hi], ALU.mult)
                    last.then_inc(sys_in, 1)
                for g in range(8):
                    dve.wait_ge(gram, 8 * p + g + 1)
                    n, h, q = g // 4, (g // 2) % 2, g % 2
                    bank = (4, 5, 0, 1)[g % 4]
                    msk = ct[:, K_GM + n * P:K_GM + (n + 1) * P].unsqueeze(1).broadcast_to([P, 4, P])
                    V.tensor_tensor(gm[:, n, h, 4 * q:4 * q + 4, :], ps[:, bank, :].rearrange("p (c s) -> p c s", c=4), msk,
                                    ALU.mult).then_inc(gram_in, 1)
                if before:
                    centre(b, 6)
                if after:
                    pair_columns(a)
                for l in range(LEVELS):
                    for n in range(NDIR):
                        dve.wait_ge(xmm[n], LEVELS * p + l + 1)
                        o = K_LV + (n * LEVELS + l) * C
                        msk = ct[:, o:o + C].unsqueeze(1).broadcast_to([P, NCH, C])
                        V.tensor_tensor(xc[:, n, :, :], chunks(ps[:, 4 + n, :]), msk, ALU.mult).then_inc(xev[n], 1)
                    if l > 0:
                        dve.wait_ge(tmm[1], LEVELS * p + l + 1)
                        V.tensor_copy(mt[0:C, 1, :, 0:C], pairs[1][0:C, :, 0:C])
                        V.tensor_copy(mt[C:P, 1, :, C:P], pairs[1][0:C, :, C:P]).then_inc(tev[1], 1)
                    if before and l == 1:
                        finish(b, 0)
                    if before and l == 2:
                        finish(b, 1)
                        finish(b, 2)
                    if after and l == 3:
                        key_direction(a)
                        rates(a)
                    if after and l == 4:
                        decays(a)
                pend4 = pend[:, :, :].rearrange("p n (q c) -> p n q c", q=NSEQ)
                wv4 = wv.rearrange("p (q c) i -> p q c i", q=NSEQ)
                for j in range(CPS):
                    for n in range(NDIR):
                        dve.wait_ge(u_mm[n], CPS * p + j + 1)
                        c = j if n == 0 else CPS - 1 - j
                        V.tensor_copy(wv4[C:P, :, c, :], ps[C:P, 4 + n, 256:512].rearrange("p (q i) -> p q i", q=NSEQ)).then_inc(u_ev[n], 1)
                    if j < CPS - 1:
                        for n in range(NDIR):
                            c = j if n == 0 else CPS - 1 - j
                            dve.wait_ge(s_mm[n], (CPS - 1) * p + j + 1)
                            for h, (lo, hi) in enumerate(halves):
                                sm = ps[lo:hi, 4 + n, 0:2 * P].rearrange("p (q i) -> p q i", q=NSEQ)[:, :, lo:hi]
                                if j > 0:
                                    own(V.tensor_tensor(stmp[lo:hi, n, :, :], sm, sx[lo:hi, j % 2, n, :, lo:hi], ALU.add))
                            if j > 0:
                                own.wait()
                            for h, (lo, hi) in enumerate(halves):
                                sm = ps[lo:hi, 4 + n, 0:2 * P].rearrange("p (q i) -> p q i", q=NSEQ)[:, :, lo:hi]
                                src = stmp[lo:hi, n, :, :] if j > 0 else sm
                                last = V.tensor_tensor(sx[lo:hi, (j + 1) % 2, n, :, lo:hi], src,
                                                       pend4[lo:hi, n, :, c:c + 1].broadcast_to([C, NSEQ, C]), ALU.mult)
                            last.then_inc(s_ev[n], 1)
                    if after:
                        if j == 0:
                            bonus(a, 0)
                        elif j == 1:
                            decays_back(a, 0)
                        elif j == 2:
                            bonus(a, 1)
                            decays_back(a, 1)
                        elif j == 3:
                            last_products(a)
                dve.wait_ge(y_cp, p + 1)
                V.tensor_tensor(o_res[:, p, :], ps[:, 1, :], o_res[:, p, :], ALU.add).then_inc(y_in, 1)
                dve.wait_ge(y_in, p + 1)

            dve.sem_inc(gate_mm, 1)
            pair_columns(0)
            key_direction(0)
            rates(0)
            decays(0)
            bonus(0, 0)
            decays_back(0, 0)
            bonus(0, 1)
            decays_back(0, 1)
            last_products(0)
            pair(0, False, True)
            own.loop_start()
            with dve.Fori(1, KT - 1) as p:
                pair(p, True, True)
                own.loop_end()
            pair(KT - 1, True, False)
            centre(KT - 1, 6)
            for step in range(3):
                finish(KT - 1, step)
            phase.end()
            for k in range(KT):
                low_input(k, o_res[:, k, :], o_lo[:, k, :], o_hi[:, k, :])
            phase.end()
            dve.wait_ge(x_back, 16)
            post_norm(0, 1, 2)
            phase.end()
            pre_norm(0, 2, 4, h_hi)
            mlp(0)
            phase.end()
            post_norm(0, 3, 5)
            phase.end()
            pre_norm(1, 0, 1, att_hi)

            def rotate(x, dst, n):
                dve.wait_ge(a_ev, n + 1)
                own.wait()
                own(V.tensor_tensor(seqs(swp[x])[0:C], seqs(raw[x])[C:P], sinb[C:P], ALU.mult))
                own(V.tensor_tensor(seqs(swp[x])[C:P], seqs(raw[x])[0:C], sinb[0:C], ALU.mult))
                own(V.tensor_tensor(seqs(rot[x]), seqs(raw[x]), cosb, ALU.mult))
                own.wait()
                own(V.tensor_tensor(rot[x], rot[x], swp[x], ALU.add))
                dve.wait_ge(a_rt, n + 1)
                own(V.reciprocal(ars[x], ars[x]))
                own.wait()
                V.tensor_tensor(dst, rot[x], ars[x], ALU.mult).then_inc(a_q, 1)

            for x in range(KVH):
                rotate(x, kh[:, x, :], x)
            dve.wait_ge(v_in, KVH)
            for s in range(2):
                rotate(s, qh[s], KVH + s)

            def heads(j, ahead):
                for s in range(2):
                    h = 2 * j + s
                    dve.wait_ge(a_sc, h + 1)
                    own.wait()
                    own(V.reduce_max(stat[:, 0:4], ps[:, 4:6, :].rearrange("p q (b k) -> p (q b) k", k=SEQ), AX_X))
                    own.wait()
                    V.tensor_scalar(stat[:, 4:8], stat[:, 0:4], -float(AH) ** -0.5, None, ALU.mult).then_inc(a_mx, 1)
                    dve.wait_ge(a_ex, h + 2)
                    own.wait()
                    own(V.reciprocal(stat[:, 12:16], stat[:, 8:12]))
                    own.wait()
                    V.tensor_tensor(prob[:], prob[:], stat[:, 12:16].unsqueeze(2).broadcast_to([P, 4, SEQ]),
                                    ALU.mult).then_inc(a_p, 1)
                for s in range(2):
                    h = 2 * j + s
                    if ahead and s == 0:
                        rotate(0, qh[0], KVH + h + 2)
                    dve.wait_ge(a_pv, h + 2)
                    dve.sem_inc(dve_tick, 1)
                    V.tensor_copy(o_res[:, h, :], ps[:, s, :]).then_inc(a_o, 1)
                if ahead:
                    rotate(1, qh[1], KVH + h + 2)
                own.wait()

            own.loop_start()
            with dve.Fori(0, 2) as j:
                heads(j, True)
                own.loop_end()
            heads(2, True)
            heads(3, False)
            phase.end()
            for k in range(KT):
                low_input(k, o_res[:, k, :], o_lo[:, k, :], o_hi[:, k, :])
            phase.end()
            post_norm(1, 1, 2)
            phase.end()
            pre_norm(1, 2, 4, h_hi)
            mlp(1)
            phase.end()
            post_norm(1, 3, 5)
            phase.end()

        @block.gpsimd
        def _(pool):
            phase = Phases(pool)
            own = Own(pool, pool_own)
            G = nc.gpsimd
            norms = [0]
            posts = [0]

            def pads():
                G.memset(h_pad[:, :, :, 0:1], 0.0)
                G.memset(h_pad[:, :, :, SEQ + 1:SEQ + 2], 0.0)
                norms[0] += 1

            def u_pads():
                for s in range(2):
                    G.memset(u_pad[s][:, :, 0:1], 0.0)
                    G.memset(u_pad[s][:, :, SEQ + 1:SEQ + 2], 0.0)

            def high_input(hi):
                for k in range(KT):
                    pool.wait_ge(scaled_used, norms[0] * KT + k + 1)
                    G.tensor_copy(seqs(hi[:, k, :]), h_in[:, k]).then_inc(h_high, 1)
                norms[0] += 1

            w = Pieces()

            def low(n, r, cols=D):
                pool.wait_ge(w_hi, n + 1)
                G.tensor_tensor(split_w[:, r % 2, 1, 0:cols], raw_w[:, r, 0:cols], split_w[:, r % 2, 0, 0:cols].bitcast(F32),
                                ALU.subtract).then_inc(w_lo, 1)

            def square():
                for m in range(KT):
                    low(w.n + m + 2, (m + 2) % NRAW)
                w.add(KT)

            def mlp(last_mlp):
                with pool.Fori(0, FT // 2 - 1) as i:
                    for m in range(NRAW):
                        low(w.n + NRAW * i + m + 2, (m + 2) % NRAW)
                for m in range(NRAW):
                    low(w.n + 2 * FT - NRAW + m + 2, (m + 2) % NRAW, D if m < 2 else PIECE)
                w.add(2 * FT)
                with pool.Fori(0, KT // 2 - 1) as i:
                    for m in range(NRAW):
                        low(w.n + NRAW * i + m + 2, (m + 2) % NRAW, PIECE)
                for m in range(2 if last_mlp else NRAW):
                    low(w.n + 2 * KT - NRAW + m + 2, (m + 2) % NRAW, PIECE if m < 2 else D)
                w.add(2 * KT)

            def post_norm(src):
                posts[0] += 1
                pool.wait_ge(rstd, posts[0])
                base = norms[0] * KT
                for k in range(KT):
                    if base + k >= 2:
                        pool.wait_ge(scaled_used, base + k - 1)
                    G.tensor_tensor(tmp2[k % 2], src[:, k, :], rs, ALU.mult).then_inc(scaled, 1)
                norms[0] += 1

            G.memset(scan[:, 15 * 1024 - 6144:15 * 1024], 0.0)
            G.memset(sx[:], 0.0)
            phase.end()
            phase.end()
            pads()
            phase.end()
            phase.end()
            def next_keys(a):
                pool.wait_ge(kdf, a + 1)
                own(G.tensor_tensor(t_a[0], t_a[0], t_k, ALU.mult))
                own.wait()
                own(G.tensor_tensor(t_a[1], t_a[1], t_k, ALU.mult))
                own.wait()
                G.tensor_tensor(t_sq, t_a[0], t_a[1], ALU.add).then_inc(kd_sum, 1)
                pool.wait_ge(kd_sum, a + 1)
                pool.wait_ge(scanned, a + 1)
                G.tensor_tensor(s_exc, s_inc, s_w[0], ALU.subtract).then_inc(cum, 1)
                pool.wait_ge(cum, 2 * a + 1)

            def products(a, n):
                if n == 0:
                    pool.wait_ge(head_sum, 2 * a + 2)
                pool.wait_ge(expd, 6 * a + 3 * n + 1)
                own(G.tensor_tensor(kbn[:, n, :, 0:C], chunks(t_a[n]), chunks(s_e2), ALU.mult))
                own.wait()
                last = G.tensor_tensor(kbn[:, n, :, C:P], chunks(t_b[n]), chunks(s_e2), ALU.mult)
                if n == 0:
                    last.then_inc(prod, 1)
                    pool.wait_ge(prod, a + 1)
                else:
                    last.then_inc(prep, 1)

            def carry(p, first=False):
                pool.wait_ge(prep, 2 * p + 2)
                if not first:
                    pool.wait_ge(y_in, p)
                pool.sem_inc(pool_tick, 1)
                own(G.tensor_copy(pend[:], pendn[:]))
                own.wait()
                G.tensor_copy(ar, arn).then_inc(carried, 1)

            def keep_bonus(p):
                pool.wait_ge(bon_in, 2 * p + 2)
                pool.sem_inc(pool_tick, 1)
                G.tensor_copy(t_bon, t_bonn).then_inc(bon_copied, 1)

            def pair(p, before, after):
                a = p + 1
                carry(p, not before)
                pool.wait_ge(carried, p + 1)
                for n in range(NDIR):
                    pool.wait_ge(sys_in, 2 * p + n + 1)
                    one = ct[:, K_ID:K_ID + P].unsqueeze(1).broadcast_to([P, NCH, P])
                    own(G.tensor_tensor(nt[:, n], nt[:, n], one, ALU.add))
                    own.wait()
                    m1 = ct[:, K_M1 + n * C:K_M1 + (n + 1) * C].unsqueeze(1).broadcast_to([P, NCH, C])
                    own(G.tensor_tensor(mt[0:C, n, :, 0:C], nt[0:C, n, :, 0:C], m1[0:C], ALU.mult))
                    own.wait()
                    G.tensor_tensor(mt[C:P, n, :, C:P], nt[C:P, n, :, C:P], m1[C:P], ALU.mult).then_inc(ident_in, 1)
                    pool.wait_ge(ident_in, 2 * p + n + 1)
                if before:
                    pool.wait_ge(gated, p)
                keep_bonus(p)
                pool.wait_ge(bon_copied, p + 1)
                if after:
                    next_keys(a)
                    products(a, 0)
                    products(a, 1)

            next_keys(0)
            products(0, 0)
            products(0, 1)
            pair(0, False, True)
            own.loop_start()
            with pool.Fori(1, KT - 1) as p:
                pair(p, True, True)
                own.loop_end()
            pair(KT - 1, True, False)
            phase.end()
            for m in range(2):
                low(m, m)
            square()
            phase.end()
            post_norm(mix_out)
            u_pads()
            phase.end()
            high_input(h_hi)
            mlp(False)
            phase.end()
            post_norm(o_res)
            phase.end()
            high_input(att_hi)
            for m in range(2 * KVH):
                low(w.n + m + 2, (m + 2) % NRAW)
            w.add(2 * KVH)
            for g in range(KVH):
                with pool.Fori(0, 2) as i:
                    for s in range(2):
                        low(w.n + 2 * i + s + 2, s)
                w.add(4, 2)
            phase.end()
            square()
            phase.end()
            post_norm(mix_out)
            u_pads()
            phase.end()
            high_input(h_hi)
            mlp(True)
            phase.end()
            post_norm(o_res)
            phase.end()


def tiles(w):
    k, m = w.shape
    return w.reshape(k // P, P, m // P, P).transpose(2, 1, 0, 3)


def columns(v):
    return v.reshape(-1, P).T


def kernel(x_prompt, x_sample, c_prompt, c_sample, ada_w, ada_b, norm_g, rw_mu, rw_rkv, rw_w0, rw_wA, rw_wB,
           rw_a0, rw_aA, rw_aB, rw_gA, rw_gB, rw_kk, rw_ka, rw_rk, rw_lnx, rw_o, rw_v0, rw_vA, rw_vB,
           at_qkv, at_qk_g, at_o, ffn_up, ffn_conv_w, ffn_conv_b, ffn_down):
    import concourse.bacc as bacc
    from concourse.bass_utils import run_bass_kernel_spmd

    arr = lambda a: np.asarray(a)
    x = np.concatenate([arr(x_prompt), arr(x_sample)], 0)
    xT = x.transpose(2, 0, 1).reshape(KT, P, TOK).transpose(1, 0, 2)
    c = np.concatenate([arr(c_prompt), arr(c_sample)], 0)
    cT = c.T.reshape(KT, P, NSEQ).transpose(1, 0, 2)

    halfway = np.concatenate([np.arange(0, AH, 2), np.arange(1, AH, 2)])
    pair = np.stack([columns(a) for a in (arr(rw_w0)[0, 0], arr(rw_w0)[0, 1], arr(rw_a0)[0, 0], arr(rw_a0)[0, 1],
                                          arr(rw_kk)[0], arr(rw_ka)[0], arr(rw_rk)[0], arr(rw_lnx)[0, 0],
                                          arr(rw_lnx)[0, 1])], -1)
    cw, cb = arr(ffn_conv_w), arr(ffn_conv_b)
    ffc = np.concatenate([np.stack([columns(a) for a in (cw[l, 0], cw[l, 1], cw[l, 2], cb[l])], -1)
                          for l in range(DEPTH)], 1)
    params = np.concatenate([columns(arr(ada_b)), columns(arr(norm_g)), columns(arr(rw_mu)[0]),
                             pair.reshape(P, -1), arr(at_qk_g)[0][:, halfway].T, ffc.reshape(P, -1)], 1)

    aw = arr(ada_w).reshape(DEPTH, KT, P, 12, TOK).transpose(0, 3, 2, 1, 4).reshape(DEPTH * 4, 3, P, KT * TOK)
    rkv = [tiles(arr(rw_rkv)[0, n]).reshape(KT, P, D) for n in range(3)]
    second = [arr(w)[0].reshape(P, KT, P).transpose(1, 0, 2) for w in (rw_wB, rw_aB, rw_gB)]
    pair_w = np.concatenate(rkv + second[0:2], -1)
    first = [tiles(arr(w)[0].transpose(1, 0, 2).reshape(D, P))[0].reshape(P, D) for w in (rw_wA, rw_aA)]
    lora_a = np.concatenate(first + [tiles(arr(rw_gA)[0])[0].reshape(P, D)], -1)
    wo = tiles(arr(rw_o)[0]).reshape(KT, P, D)
    qkv = tiles(arr(at_qkv)[0]).reshape(12, P, D)
    swap = lambda w: w.reshape(w.shape[0], P, KT, P)[..., halfway].reshape(w.shape[0], P, D)
    at_kv = np.concatenate([swap(qkv[8:10]), qkv[10:12]])
    at_q = swap(qkv[0:8]).reshape(4, 2, P, D)
    ao = tiles(arr(at_o)[0]).reshape(KT, P, D)
    up = np.stack([tiles(arr(ffn_up)[l]).reshape(2, FT, P, D).transpose(1, 0, 2, 3).reshape(FT // 2, 4, P, D)
                   for l in range(DEPTH)])
    down = np.stack([tiles(arr(ffn_down)[l]).reshape(KT, P, 2, D_FF // 2).transpose(0, 2, 1, 3)
                     .reshape(KT // 2, 4, P, D_FF // 2) for l in range(DEPTH)])

    ins = dict(xT=xT, cT=cT, params=params, consts=constants(), ada_w=aw, lora_a=lora_a, pair_w=pair_w, gate_w=second[2], rw_o=wo,
               at_kv=at_kv, at_q=at_q, at_o=ao, ffn_up=up, ffn_down=down)
    nc = bacc.Bacc("TRN2", target_bir_lowering=False, num_devices=1)
    arrays, args = {}, {}
    for name, a in ins.items():
        a = np.ascontiguousarray(a)
        arrays[f"in_{name}"] = a
        args[name] = nc.dram_tensor(f"in_{name}", a.shape, mybir.dt.from_np(a.dtype), kind="ExternalInput").ap()
    yT = nc.dram_tensor("out_y", (P, KT, TOK), F32, kind="ExternalOutput").ap()
    encoder_trunk(nc, yT=yT, **args)
    r = run_bass_kernel_spmd(nc, [arrays], core_ids=[0])
    y = r.results[0]["out_y"].reshape(P, KT, NSEQ, SEQ).transpose(2, 3, 1, 0).reshape(NSEQ, SEQ, D)
    return y[0:1], y[1:2]
```

```python
from contextlib import ExitStack

import numpy as np

import concourse.bass as bass
from concourse import mybir

F32 = mybir.dt.float32
F32R = mybir.dt.float32r
ALU = mybir.AluOpType
ACT = mybir.ActivationFunctionType
AX_X = mybir.AxisListType.X

P = 128
D = 1024
KT = D // P
NSEQ = 2
SEQ = 256
TOK = NSEQ * SEQ
DEPTH = 2
D_FF = 2816
FT = D_FF // P
HEAD = 64
NDIR = 2
C = 64
NCH = TOK // C
CPS = SEQ // C
LEVELS = 5
QH, KVH, AH = 8, 2, 128
GRID_W = 64
ROPE_THETA = 10000.0
NORM_EPS = 1e-6
GN_EPS = 64e-5
DECAY = float(np.exp(-0.5))

C_ADAB = 0
C_NORM = C_ADAB + DEPTH * 48
C_MU = C_NORM + DEPTH * 4 * KT
C_PAIR = C_MU + 6 * KT
NPP = 9
C_QKG = C_PAIR + KT * NPP
C_FFN = C_QKG + 2
NPARAM = C_FFN + DEPTH * FT * 4

K_ONES = 0
K_BLK = K_ONES + P
K_ID = K_BLK + P
K_GM = K_ID + P
K_NT = K_GM + NDIR * P
K_M1 = K_NT + NDIR * C
K_LV = K_M1 + NDIR * C
K_RES = K_LV + NDIR * LEVELS * C
K_COS = K_RES + TOK
K_SIN = K_COS + SEQ
K_EPS = K_SIN + SEQ
NCONST = K_EPS + 2


def constants():
    t = np.zeros((P, NCONST), np.float32)
    t[:, K_ONES:K_ONES + P] = 1.0 / D
    head = np.arange(P) // HEAD
    t[:, K_BLK:K_BLK + P] = (head[:, None] == head[None, :]) / HEAD
    t[:, K_ID:K_ID + P] = np.eye(P)
    i = np.arange(C)
    for n in range(NDIR):
        before = (i[:, None] < i[None, :]) if n == 0 else (i[:, None] > i[None, :])
        upto = before | (i[:, None] == i[None, :])
        gm = np.concatenate([before, upto], 1)
        t[:, K_GM + n * P:K_GM + (n + 1) * P] = np.concatenate([gm, gm], 0)
        t[:, K_NT + n * C:K_NT + (n + 1) * C] = np.tile(before.T, (2, 1))
        same = lambda b: (i[:, None] // b) == (i[None, :] // b)
        t[:, K_M1 + n * C:K_M1 + (n + 1) * C] = np.tile((before.T & same(2)) | np.eye(C, dtype=bool), (2, 1))
        for l in range(LEVELS):
            b = 2 ** (l + 1)
            m = (before & same(2 * b) & ~same(b)) | np.eye(C, dtype=bool)
            o = K_LV + (n * LEVELS + l) * C
            t[:, o:o + C] = np.tile(m, (2, 1))
    t[:, K_RES:K_RES + TOK] = (np.arange(TOK) % C != 0)
    tok = np.arange(SEQ)
    npair = AH // 4
    inv = ROPE_THETA ** (-np.arange(npair, dtype=np.float32) / npair)
    ang = np.concatenate([(tok // GRID_W)[:, None] * inv, (tok % GRID_W)[:, None] * inv], -1).astype(np.float32)
    t[:, K_COS:K_COS + SEQ] = np.tile(np.cos(ang).T, (2, 1))
    t[:, K_SIN:K_SIN + SEQ] = np.concatenate([np.sin(ang).T, -np.sin(ang).T], 0)
    t[:, K_EPS] = NORM_EPS
    t[:, K_EPS + 1] = GN_EPS
    return t


def encoder_trunk(nc, xT, cT, params, consts, ada_w, lora_a, pair_w, gate_w, rw_o, at_kv, at_q, at_o,
                  ffn_up, ffn_down, yT):
    ctx = ExitStack()
    ADA = 3
    ADA_FIRST = 2
    ADA_ROUNDS = DEPTH * 6 * D // TOK // ADA
    with ctx:
        sb = lambda name, shape: ctx.enter_context(nc.sbuf_tensor(name, shape, F32))
        sem = lambda name: ctx.enter_context(nc.semaphore(name))

        x_res = sb("x_res", [P, KT, TOK])
        pt = sb("pt", [P, NPARAM])
        ct = sb("ct", [P, NCONST])
        mod = sb("mod", [P, DEPTH * 6 * KT, NSEQ])
        gs = sb("gs", [P, KT, NSEQ])
        csil = sb("csil", [P, KT, NSEQ])
        derived = sb("derived", [P, KT, 2])
        pcur = sb("pcur", [P, NPP + 2])
        fcur = sb("fcur", [P, 2, 4])
        sx = sb("sx", [P, 2, NDIR, NSEQ, P])
        pend = sb("pend", [P, NDIR, NCH])
        pendn = sb("pendn", [P, NDIR, NCH])
        gbt = sb("gbt", [P, P])
        SLOT, PIECE, NRAW = 27 * P, D_FF // 2, 4
        BIG, SCAN = 3 * KT * TOK, 15 * 1024
        AREA = BIG + SCAN + 2 * SLOT + 3 * TOK

        def view(*tensors):
            with ExitStack() as here:
                return [here.enter_context(nc.sbuf_tensor(name, shape, kind)) for name, shape, kind in tensors]

        h_pad, o_res, area = view(
            ("h_pad", [P, KT, NSEQ, SEQ + 2], F32),
            ("o_res", [P, KT, TOK], F32),
            ("area", [P, AREA], F32))
        h_lo_pad, h_hi, ff_hi, ff_lo, ffs, split_w, raw_w = view(
            ("h_lo_pad", [P, KT, NSEQ, SEQ + 2], F32R),
            ("h_hi", [P, KT, TOK], F32R),
            ("ff_hi", [P, FT, TOK], F32R),
            ("ff_lo", [P, FT, TOK], F32R),
            ("ffs", [P, AREA - 2 * FT * TOK - (NRAW + 4) * PIECE], F32),
            ("split_w", [P, 2, 2, PIECE], F32R),
            ("raw_w", [P, NRAW, PIECE], F32))
        o_hi, _, o_lo = view(
            ("o_hi", [P, KT, TOK], F32R),
            ("o_gap", [P, KT * NSEQ * 2], F32),
            ("o_lo", [P, KT, TOK], F32R))

        big = area[:, 0:BIG]
        scan = area[:, BIG:BIG + SCAN]
        ring = area[:, BIG + SCAN:BIG + SCAN + 2 * SLOT].rearrange("p (s k) -> p s k", s=2)
        lora = area[:, BIG + SCAN + 2 * SLOT:].rearrange("p (n t) -> p n t", n=3)
        ps = ctx.enter_context(nc.psum_tensor("ps", [P, 8, 512], F32))

        xr, xk, xv = (big[:, n * KT * TOK:(n + 1) * KT * TOK].rearrange("p (k t) -> p k t", k=KT) for n in range(3))
        mix_out = xr
        h_in = h_pad[:, :, :, 1:SEQ + 1]

        off = [0]

        def part(n):
            off[0] += n
            return scan[:, off[0] - n:off[0]]

        kb = part(2048).rearrange("p (n c s) -> p n c s", n=NDIR, c=NCH)
        ar = part(2048).rearrange("p (n c s) -> p n c s", n=NDIR, c=NCH)
        gm_flat = part(4096)
        gm = gm_flat.rearrange("p (n h c s) -> p n h c s", n=NDIR, h=2, c=NCH)
        wv = part(1024).rearrange("p (c i) -> p c i", c=NCH)
        nt = part(2048).rearrange("p (n c s) -> p n c s", n=NDIR, c=NCH)
        mt = part(2048).rearrange("p (n c s) -> p n c s", n=NDIR, c=NCH)
        mc_flat = part(1024)
        mc = mc_flat.rearrange("p (n c s) -> p n c s", n=NDIR, c=NCH)
        xc_flat = part(1024)
        xc = xc_flat.rearrange("p (n c s) -> p n c s", n=NDIR, c=NCH)
        x0s = xc_flat[0:C, 0:2 * NSEQ * P].rearrange("p (n q i) -> p n q i", n=NDIR, q=NSEQ)
        stmp = mc_flat[:, 0:2 * NSEQ * C].rearrange("p (n q i) -> p n q i", n=NDIR, q=NSEQ)
        ht = h_pad[:, :, :, :].rearrange("p k q t -> p (k q t)")
        xt = x_res[:, :, :].rearrange("p k t -> p (k t)")
        tile = lambda area, n: area[:, n * TOK:(n + 1) * TOK]
        mf = ht[0:C, 0:4 * TOK].rearrange("p (n c h t) -> p n c h t", n=NDIR, c=NCH, h=2)
        c_sq, c_b = tile(ht, 0), tile(ht, 1)
        c_b_last = tile(xt, 0)
        t_r, t_v, t_nkk, s_e2 = (tile(ht, n) for n in range(4, 8))
        t_a1, t_b1, s_exc, s_inc, t_bonn, t_bon = (tile(ring[:, 1, :], n) for n in range(6))
        kbn = xt[:, 0:2048].rearrange("p (n c s) -> p n c s", n=NDIR, c=NCH)
        arn = xt[:, 2048:4096].rearrange("p (n c s) -> p n c s", n=NDIR, c=NCH)
        t_k, t_sq = tile(xt, 0), tile(xt, 1)
        s_w0, t_a0, t_b0, s_w1 = tile(xt, 2), tile(xt, 3), tile(xt, 6), tile(xt, 7)
        s_l = s_w0
        t_a, t_b, s_w = (t_a0, t_a1), (t_b0, t_b1), (s_w0, s_w1)
        sq2 = (gm_flat[:, 0:TOK], gm_flat[:, TOK:2 * TOK])
        NTMP = 4
        tmp4 = tuple(gm_flat[:, n * TOK:(n + 1) * TOK] for n in (2, 3, 5, 7))
        rs = gm_flat[:, 4 * TOK:5 * TOK]
        hsum = gm_flat[:, 6 * TOK:7 * TOK]
        mixb = kb.rearrange("p n c s -> p (n c s)")
        mix4 = tuple(mixb[:, n * TOK:(n + 1) * TOK] for n in range(4))
        arf = ar.rearrange("p n c s -> p (n c s)")
        h_lo = h_lo_pad[:, :, :, 1:SEQ + 1]
        att_hi = ff_hi[:, 0:KT, :]
        FU = NSEQ * (SEQ + 2)
        u_pad = tuple(ffs[:, n * FU:(n + 1) * FU].rearrange("p (q t) -> p q t", q=NSEQ) for n in range(2))
        conv = tuple(ffs[:, 2 * FU + n * TOK:2 * FU + (n + 1) * TOK] for n in range(2))
        out_sq = conv
        out_sum = sx[:, 0, :, :, :].rearrange("p n q i -> p (n q i)")
        boff = [KT * TOK]

        def bpart(n):
            boff[0] += n
            return big[:, boff[0] - n:boff[0]]

        kh = bpart(KVH * TOK).rearrange("p (g t) -> p g t", g=KVH)
        vh = bpart(KVH * TOK).rearrange("p (g b d) -> p g b d", g=KVH, b=4)
        qh = tuple(bpart(TOK) for _ in range(2))
        raw = tuple(bpart(TOK) for _ in range(2))
        rot = tuple(bpart(TOK) for _ in range(2))
        swp = tuple(bpart(TOK) for _ in range(2))
        asq = tuple(bpart(TOK) for _ in range(2))
        ars = tuple(bpart(TOK) for _ in range(2))
        prob = mixb[:, 0:4 * SEQ].rearrange("p (b k) -> p b k", b=4)
        prT = mixb[:, 4 * SEQ:8 * SEQ].rearrange("p (q b t) -> p q b t", q=2, b=2)
        stat = arf[:, 0:16]
        cosb = ct[:, K_COS:K_COS + SEQ].unsqueeze(1).broadcast_to([P, NSEQ, SEQ])
        sinb = ct[:, K_SIN:K_SIN + SEQ].unsqueeze(1).broadcast_to([P, NSEQ, SEQ])

        ones = ct[:, K_ONES:K_ONES + P]
        blk = ct[:, K_BLK:K_BLK + P]
        ident = ct[:, K_ID:K_ID + P]
        seqs = lambda ap: ap.rearrange("p (q t) -> p q t", q=NSEQ)
        ada_area = area[:, BIG + 8 * 1024:BIG + 8 * 1024 + ADA * KT * TOK]
        ada_blk = tuple(ada_area[:, n * KT * TOK:(n + 1) * KT * TOK].rearrange("p (k m) -> p k m", k=KT) for n in range(ADA))
        ada_rows = tuple(scan[0:NSEQ, (4 + n) * TOK:(5 + n) * TOK] for n in range(ADA))
        lora_w = o_res[:, :, :].rearrange("p k t -> p (k t)")[:, 0:3 * D]
        chunks = lambda ap: ap.rearrange("p (c t) -> p c t", c=NCH)
        pc = lambda n: pcur[:, n:n + 1]
        halves = ((0, C), (C, P))
        OWN_PRODUCTS = (0, 3, 6)

        pair_of = lambda name: [sem(f"{name}{n}") for n in range(2)]
        c_in, ct_in, x_in, pt_in = sem("c_in"), sem("ct_in"), sem("x_in"), sem("pt_in")
        c_ready, pads_in = sem("c_ready"), sem("pads_in")
        all_done = sem("all_done")
        dve_own, pool_own = sem("dve_own"), sem("pool_own")
        pe_tick, act_tick, dve_tick, pool_tick = sem("pe_tick"), sem("act_tick"), sem("dve_tick"), sem("pool_tick")
        ada_in = [sem(f"ada_in{n}") for n in range(ADA)]
        ada_done = [sem(f"ada_done{n}") for n in range(ADA)]
        ada_row, ada_cols, ada_taken = sem("ada_row"), sem("ada_cols"), sem("ada_taken")
        sq_ready, sq_used = sem("sq_ready"), sem("sq_used")
        out_sq_in, out_sq_added = sem("out_sq_in"), sem("out_sq_added")
        out_sum_mm = sem("out_sum_mm")
        root, rstd = sem("root"), sem("rstd")
        scaled, out_scaled = sem("scaled"), sem("out_scaled")
        scaled_used = sem("scaled_used")
        h_high, h_high_odd, moving = sem("h_high"), sem("h_high_odd"), sem("moving")
        piece_in = [sem(f"piece_in{r}") for r in range(NRAW)]
        w_hi, w_lo, w_used = sem("w_hi"), sem("w_lo"), sem("w_used")
        copied = sem("copied")
        taken = pair_of("taken")
        fcols, u_ready, conv_ready, silu_ready = sem("fcols"), sem("u_ready"), sem("conv_ready"), sem("silu_ready")
        mixed, mixed_used = sem("mixed"), sem("mixed_used")
        lora_in, lora_mm = sem("lora_in"), sem("lora_mm")
        pair_in, pair_used = sem("pair_in"), sem("pair_used")
        pcols = sem("pcols")
        projected, evac = sem("projected"), sem("evac")
        head_sum, norm_root = sem("head_sum"), sem("norm_root")
        kdf, kd_sum, bon_in = sem("kdf"), sem("kd_sum"), sem("bon_in")
        scanned, cum, expd = sem("scanned"), sem("cum"), sem("expd")
        prod, prep = sem("prod"), sem("prep")
        carried, bon_copied = sem("carried"), sem("bon_copied")
        sys, sys_in, gram, gram_in = sem("sys"), sem("sys_in"), sem("gram"), sem("gram_in")
        tr, tr_in, ident_in = sem("tr"), sem("tr_in"), sem("ident_in")
        xmm, xev, mmm, mev = (pair_of(n) for n in ("xmm", "xev", "mmm", "mev"))
        tmm, tev, fmm, fev = (pair_of(n) for n in ("tmm", "tev", "fmm", "fev"))
        x0_mm, x0_ev, u_mm, u_ev = (pair_of(n) for n in ("x0_mm", "x0_ev", "u_mm", "u_ev"))
        s_mm, s_ev = pair_of("s_mm"), pair_of("s_ev")
        y_mm, y_cp, y_in = sem("y_mm"), sem("y_cp"), sem("y_in")
        mean_mm, centred, dev_sq, var_mm, var_root = (sem(n) for n in (
            "mean_mm", "centred", "dev_sq", "var_mm", "var_root"))
        gate_in, gate_mm, gated = sem("gate_in"), sem("gate_mm"), sem("gated")
        x_back = sem("x_back")
        a_ev, a_ss, a_rt, a_q = sem("a_ev"), sem("a_ss"), sem("a_rt"), sem("a_q")
        v_tr, v_in = sem("v_tr"), sem("v_in")
        a_sc, a_mx, a_ex, a_p = sem("a_sc"), sem("a_mx"), sem("a_ex"), sem("a_p")
        a_tr, a_te, a_pv, a_o = sem("a_tr"), sem("a_te"), sem("a_pv"), sem("a_o")
        stored = sem("stored")

        block = ctx.enter_context(nc.Block())

        class Own:

            def __init__(self, eng, own):
                self.eng, self.own, self.n = eng, own, 0

            def __call__(self, ins):
                ins.then_inc(self.own, 1)
                self.n += 1
                return self.n

            def wait(self, n=None):
                if self.n:
                    self.eng.wait_ge(self.own, self.n if n is None else n)

            def loop_start(self):
                self.base = self.n

            def loop_end(self):
                self.wait()
                if self.n > self.base:
                    self.eng.sem_inc(self.own, self.base - self.n)
                    self.n = self.base

        def barrier(eng):
            eng.drain().then_inc(all_done, 1)
            eng.wait_ge(all_done, 4)

        class Pieces:

            def __init__(self):
                self.n, self.slot, self.copies = 0, [0] * NRAW, 0

            def add(self, n, slots=NRAW, copies=0):
                self.n += n
                for r in range(slots):
                    self.slot[r] += n // slots
                self.copies += copies

        @block.sync
        def _(sp):
            sp.dma_start(csil[:], cT).then_inc(c_in, 16)
            sp.dma_start(ada_blk[0], ada_w[0, 0]).then_inc(ada_in[0], 16)
            sp.dma_start(ct[:], consts).then_inc(ct_in, 16)
            for n in range(1, ADA):
                sp.dma_start(ada_blk[n], ada_w[0, n]).then_inc(ada_in[n], 16)
            sp.dma_start(x_res[:], xT).then_inc(x_in, 16)
            sp.dma_start(pt[:], params).then_inc(pt_in, 16)
            with sp.Fori(1, ADA_ROUNDS) as i:
                for n in range(ADA):
                    sp.wait_ge(ada_done[n], i)
                    sp.dma_start(ada_blk[n], ada_w[i, n]).then_inc(ada_in[n], 16)

            pieces_ = Pieces()

            def load(n, r, src, cols, behind=NRAW):
                if not isinstance(n, int) or n >= behind:
                    sp.wait_ge(w_lo, n - behind + 1)
                sp.dma_start(raw_w[:, r, 0:cols], src).then_inc(piece_in[r], 16)

            def square(w, first):
                for m in range(KT):
                    if pieces_.n == 0 and m == 0:
                        sp.wait_ge(pair_used, KT)
                        sp.wait_ge(bon_copied, KT)
                    if pieces_.n == 0 and m == 2:
                        sp.wait_ge(gated, KT)
                    load(pieces_.n + m, m % NRAW, w[m], D, 2 if first and m < NRAW else NRAW)
                pieces_.add(KT)

            def mlp(l):
                with sp.Fori(0, FT // 2) as i:
                    for r in range(NRAW):
                        load(pieces_.n + NRAW * i + r, r, ffn_up[l, i, r], D)
                pieces_.add(2 * FT)
                with sp.Fori(0, KT // 2) as i:
                    for r in range(NRAW):
                        load(pieces_.n + NRAW * i + r, r, ffn_down[l, i, r], PIECE)
                pieces_.add(2 * KT)

            sp.dma_start(lora_w, lora_a).then_inc(lora_in, 16)
            for n in range(ADA):
                sp.wait_ge(ada_done[n], ADA_ROUNDS)
            sp.dma_start(ring[:, 0, 0:26 * P], pair_w[0]).then_inc(pair_in, 16)
            with sp.Fori(0, KT - 1) as i:
                sp.wait_ge(pair_used, i + 1)
                sp.dma_start(ring[:, 0, 0:26 * P], pair_w[i + 1]).then_inc(pair_in, 16)
                sp.wait_ge(gate_mm, i + 1)
                sp.dma_start(gbt[:], gate_w[i]).then_inc(gate_in, 16)
            sp.wait_ge(gate_mm, KT)
            sp.dma_start(gbt[:], gate_w[KT - 1]).then_inc(gate_in, 16)
            square(rw_o, False)
            sp.dma_start(x_res[:], xT).then_inc(x_back, 16)
            mlp(0)
            for m in range(2 * KVH):
                load(pieces_.n + m, m, at_kv[m], D)
            pieces_.add(2 * KVH)
            with sp.Fori(0, QH // 2) as i:
                for s in range(2):
                    load(pieces_.n + 2 * i + s, s, at_q[i, s], D, 2)
            pieces_.add(QH, 2)
            square(at_o, True)
            mlp(1)
            for k in range(0, KT, 2):
                sp.wait_ge(scaled_used, 7 * KT + k + 2)
                sp.dma_start(yT[:, k:k + 2], x_res[:, k:k + 2]).then_inc(stored, 16)
            sp.wait_ge(stored, 16 * KT // 2)

        @block.tensor
        def _(pe):
            mm, tp = nc.tensor.matmul, nc.tensor.transpose
            norms = [0]

            def product(bank, w, rhs, n=KT):
                for k in range(n):
                    last = mm(bank, w[:, k * P:(k + 1) * P], rhs[:, k], start=(k == 0), stop=(k == n - 1))
                return last

            def norm_sums():
                base = norms[0] * KT
                for k in range(KT):
                    pe.wait_ge(sq_ready, base + k + 1)
                    mm(ps[:, 0, :], ones, sq2[k % 2], start=(k == 0), stop=(k == KT - 1)).then_inc(sq_used, 1)
                norms[0] += 1

            w = Pieces()

            def piece(n, s, bank, hi, lo, tiles, first=0, total=None, fresh=False):
                pe.wait_ge(w_lo, n + 1)
                wh, wl = split_w[:, s, 0], split_w[:, s, 1]
                total = tiles if total is None else total
                for k in range(tiles):
                    if fresh:
                        pe.wait_ge(moving, moved[0] + k + 1)
                    o, t = k * P, first + k
                    mm(bank, wh[:, o:o + P], hi[:, t], start=(t == 0), stop=False)
                    mm(bank, wh[:, o:o + P], lo[:, t], start=False, stop=False)
                    last = mm(bank, wl[:, o:o + P], hi[:, t], start=False, stop=(t == total - 1))
                last.then_inc(w_used, 1)

            moved = [0]

            sums = [0]

            def output_sum():
                sums[0] += 1
                pe.wait_ge(out_sq_added, 2 + sums[0] * KT)
                mm(ps[:, 7, :], ones, out_sum, start=True, stop=True).then_inc(out_sum_mm, 1)

            def square(hi, lo):
                with pe.Fori(0, 2) as i:
                    for m in range(NRAW):
                        pe.wait_ge(copied, w.copies + 4 * i + m + 1)
                        piece(w.n + NRAW * i + m, m % 2, ps[:, m, :], hi, lo, KT, fresh=(m == 0))
                w.add(KT, copies=KT)
                moved[0] += KT

            def mlp(l):
                with pe.Fori(0, FT // 2) as i:
                    for m in range(NRAW):
                        if m % 2 == 0:
                            pe.wait_ge(taken[m // 2], l * FT // 2 + i + 1)
                        piece(w.n + NRAW * i + m, m % 2, ps[:, m, :], h_hi, h_lo, KT, fresh=(m == 0))
                w.add(2 * FT)
                moved[0] += KT
                with pe.Fori(0, KT // 2) as i:
                    for s in range(2):
                        pe.wait_ge(copied, w.copies + 2 * i + s + 3)
                        for h in range(2):
                            if s == 0:
                                for x in range(2):
                                    pe.wait_ge(taken[x], l * FT // 2 + (FT // 2 + 1 if h else (FT // 2 + 1) // 2 + 1))
                            piece(w.n + NRAW * i + 2 * s + h, h, ps[:, 4 + s, :], ff_hi, ff_lo, FT // 2,
                                  h * FT // 2, FT)
                w.add(2 * KT, copies=KT)

            pe.wait_ge(c_ready, 1)
            def ada_columns(i, n):
                pe.wait_ge(ada_row, ADA * i + n + 1)
                pe.wait_ge(ada_taken, ADA * i + n + 1)
                pe.sem_inc(pe_tick, 1)
                for m in range(TOK // P):
                    last = tp(ps[:, 4 + n, 2 * m:2 * m + 2], ada_rows[n][:, m * P:(m + 1) * P], ident[0:NSEQ, 0:NSEQ])
                last.then_inc(ada_cols, 1)

            def ada(i):
                for n in range(ADA):
                    pe.wait_ge(ada_in[n], 16 * i + 16)
                    for k in range(KT):
                        last = mm(ps[0:NSEQ, n, :], csil[:, k, :], ada_blk[n][:, k, :], start=(k == 0), stop=(k == KT - 1))
                    last.then_inc(ada_done[n], 1)
                    if n == 0:
                        pe.wait_ge(ct_in, 16)
                    else:
                        ada_columns(i, n - 1)
                ada_columns(i, ADA - 1)

            with pe.Fori(0, ADA_FIRST) as i:
                ada(i)
            norm_sums()
            pe.wait_ge(root, 1)
            with pe.Fori(ADA_FIRST, ADA_ROUNDS) as i:
                ada(i)
            pe.wait_ge(lora_in, 16)
            for k in range(KT):
                for n in range(3):
                    pe.wait_ge(mixed, k * 3 + n + 1)
                    last = mm(ps[:, 1 + n, :], lora_w[:, (n * KT + k) * P:(n * KT + k + 1) * P],
                              mix4[(k * 3 + n) % 4], start=(k == 0), stop=(k == KT - 1))
                    last.then_inc(lora_mm if k == KT - 1 and n == 2 else mixed_used, 1)
            barrier(pe)

            def pair(p, before, after):
                a, b = p + 1, p - 1
                w = ring[:, 0, :]

                def next_keys(k):
                    if k == 0:
                        pe.wait_ge(pair_in, 16 * a + 16)
                        later(bon_in, 2 * a)
                    last = mm(ps[:, 7, :], w[:, D + k * P:D + (k + 1) * P], xk[:, k], start=(k == 0), stop=(k == KT - 1))
                    if k == KT - 1:
                        last.then_inc(projected, 1)

                def next_key_squares():
                    pe.wait_ge(evac, 8 * a + 2)
                    mm(ps[:, 7, :], blk, t_sq, start=True, stop=True).then_inc(head_sum, 1)

                def next_lora(f, n):
                    lo, hi = halves[n]
                    mm(ps[:, 7, :], w[lo:hi, (24 + f) * P:(25 + f) * P], lora[lo:hi, f, :],
                       start=True, stop=True).then_inc(projected, 1)

                def next_wide(n, src, ks):
                    for k in ks:
                        last = mm(ps[:, 6, :], w[:, n * D + k * P:n * D + (k + 1) * P], src[:, k], start=(k == 0),
                                  stop=(k == KT - 1))
                    if k == KT - 1:
                        last.then_inc(projected if n == 0 else pair_used, 1)

                def next_inputs(step):
                    if step == 0:
                        next_key_squares()
                    elif step == 1:
                        pe.wait_ge(norm_root, a + 1)
                        next_lora(1, 0)
                    elif step == 2:
                        pe.wait_ge(evac, 8 * a + 3)
                        next_lora(1, 1)
                        later(var_root, p)
                        next_wide(0, xr, range(4))
                    elif step == 3:
                        if before:
                            pe.wait_ge(gated, b + 1)
                        else:
                            pe.wait_ge(evac, 8 * a + 4)
                        next_lora(0, 0)
                        next_wide(0, xr, range(4, 8))
                    elif step == 4:
                        pe.wait_ge(evac, 8 * a + 5)
                        next_lora(0, 1)
                        pe.wait_ge(evac, 8 * a + 6)
                        next_wide(2, xv, range(4))

                def next_bonus():
                    pe.wait_ge(evac, 8 * a + 7)
                    pe.wait_ge(bon_in, 2 * a + 1)
                    mm(ps[:, 7, :], blk, t_sq, start=True, stop=True).then_inc(head_sum, 1)

                def group_norm(step):
                    if step == 0:
                        later(norm_root, p + 1)
                        mm(ps[:, 6, :], blk, o_res[:, b, :], start=True, stop=True).then_inc(mean_mm, 1)
                    elif step == 1:
                        pe.wait_ge(dev_sq, b + 1)
                        mm(ps[:, 6, :], blk, c_sq, start=True, stop=True).then_inc(var_mm, 1)
                    else:
                        if after:
                            pe.wait_ge(evac, 8 * a + 4)
                        pe.wait_ge(gate_in, 16 * b + 16)
                        mm(ps[:, 7, :], gbt[:], lora[:, 2, :], start=True, stop=True).then_inc(gate_mm, 1)

                pe.wait_ge(prep, 2 * p + 2)
                if before:
                    pe.wait_ge(s_ev[0], (CPS - 1) * p)
                pe.sem_inc(pe_tick, 1)
                for n in range(NDIR):
                    for c in range(NCH):
                        for lo, hi in halves:
                            last = mm(ps[lo:hi, 2 + n, c * C:(c + 1) * C], arn[lo:hi, n, c, 0:C], kbn[lo:hi, n, c, C:P],
                                      start=True, stop=True)
                    last.then_inc(sys, 1)
                for g in range(8):
                    n, h, q = g // 4, (g // 2) % 2, g % 2
                    bank = (4, 5, 0, 1)[g % 4]
                    if g == 2 and before:
                        pe.wait_ge(y_in, b + 1)
                    if g >= 4:
                        pe.wait_ge(gram_in, 8 * p + g - 3)
                    lo, hi = halves[h]
                    for c in range(4):
                        last = mm(ps[:, bank, c * P:(c + 1) * P], kbn[lo:hi, n, 4 * q + c, :], arn[lo:hi, n, 4 * q + c, :],
                                  start=True, stop=True)
                    last.then_inc(gram, 1)
                    if after:
                        next_keys(g)
                if before:
                    group_norm(0)
                for g in range(6):
                    bank = (4, 5, 0, 1)[g % 4]
                    if g < 4:
                        pe.wait_ge(gram_in, 8 * p + 5 + g)
                    else:
                        pe.wait_ge(tr_in, 6 * p + g - 3)
                        pe.sem_inc(pe_tick, 1)
                    for c in range(4):
                        if g < 4:
                            last = tp(ps[:, bank, c * P:(c + 1) * P], kbn[:, g // 2, 4 * (g % 2) + c, :], ident)
                        else:
                            cc = 4 * (g - 4) + c
                            last = tp(ps[0:C, bank, c * P:(c + 1) * P], t_v[:, cc * C:(cc + 1) * C], ident)
                    last.then_inc(tr, 1)
                pe.wait_ge(tr_in, 6 * p + 6)
                for n in range(NDIR):
                    pe.wait_ge(ident_in, 2 * p + n + 1)
                    for c in range(NCH):
                        last = tp(ps[:, 2 * n + c // 4, (c % 4) * P:(c % 4 + 1) * P], mt[:, n, c, :], ident)
                    last.then_inc(tmm[n], 1)
                for l in range(LEVELS):
                    for n in range(NDIR):
                        pe.wait_ge(mev[n], LEVELS * p + l + 1)
                        pe.sem_inc(pe_tick, 1)
                        for c in range(NCH):
                            for lo, hi in halves:
                                last = mm(ps[lo:hi, 4 + n, c * C:(c + 1) * C], nt[lo:hi, n, c, lo:hi], mc[lo:hi, n, c, :],
                                          start=True, stop=True)
                        last.then_inc(xmm[n], 1)
                    if l > 0:
                        for n in range(NDIR):
                            for c in range(NCH):
                                last = tp(ps[0:C, 2 * n + c // 4, (c % 4) * P:(c % 4 + 1) * P], mc[:, n, c, :], ident)
                            last.then_inc(tmm[n], 1)
                    if l == 1 and before:
                        group_norm(1)
                    if after:
                        next_inputs(l)
                    if l == 2 and before:
                        group_norm(2)
                    for n in range(NDIR):
                        if l > 0:
                            pe.wait_ge(tev[n], (LEVELS - 1) * p + l)
                        pe.wait_ge(xev[n], LEVELS * p + l + 1)
                        if l < LEVELS - 1:
                            pe.sem_inc(pe_tick, 1)
                            for c in range(NCH):
                                for lo, hi in halves:
                                    last = mm(ps[lo:hi, 4 + n, c * C:(c + 1) * C], mt[lo:hi, n, c, lo:hi],
                                              xc[lo:hi, n, c, :], start=True, stop=True)
                            last.then_inc(mmm[n], 1)
                        else:
                            pe.sem_inc(pe_tick, 1)
                            for c in range(NCH):
                                for h, (lo, hi) in enumerate(halves):
                                    last = mm(ps[0:C, 2 * n + h, c * C:(c + 1) * C], mt[lo:hi, n, c, lo:hi], xc[lo:hi, n, c, :],
                                              start=True, stop=True)
                            last.then_inc(fmm[n], 1)
                pe.wait_ge(carried, p + 1)
                for j in range(CPS):
                    cs = [[q * CPS + (j if n == 0 else CPS - 1 - j) for q in range(NSEQ)] for n in range(NDIR)]
                    st = sx[:, j % 2]
                    for n in range(NDIR):
                        if j == 0:
                            pe.wait_ge(fev[n], p + 1)
                        else:
                            pe.wait_ge(s_ev[n], (CPS - 1) * p + j)
                        pe.sem_inc(pe_tick, 1)
                        for q in range(NSEQ):
                            c, o = cs[n][q], q * P
                            if j > 0:
                                mm(ps[0:C, 4 + n, o:o + P], ar[:, n, c, 0:C], st[:, n, q, :], start=True, stop=False)
                            for h in range(2):
                                last = mm(ps[0:C, 4 + n, o + h * C:o + (h + 1) * C], gm[0:C, n, h, c, 0:C],
                                          wv[0:C, c, h * C:(h + 1) * C], start=(j == 0), stop=(j == 0 or h == 1))
                        last.then_inc(x0_mm[n], 1)
                    if j == 0 and after:
                        next_wide(2, xv, range(4, 8))
                    for n in range(NDIR):
                        pe.wait_ge(x0_ev[n], CPS * p + j + 1)
                        pe.sem_inc(pe_tick, 1)
                        for q in range(NSEQ):
                            for h in range(2):
                                o = 256 + q * P + h * C
                                last = mm(ps[C:P, 4 + n, o:o + C], mf[:, n, cs[n][q], h, :],
                                          x0s[:, n, q, h * C:(h + 1) * C], start=True, stop=True)
                        last.then_inc(u_mm[n], 1)
                    if j == 1 and after:
                        next_bonus()
                    if j < CPS - 1:
                        for n in range(NDIR):
                            pe.wait_ge(u_ev[n], CPS * p + j + 1)
                            for q in range(NSEQ):
                                last = mm(ps[:, 4 + n, q * P:(q + 1) * P], kb[:, n, cs[n][q], :], wv[:, cs[n][q], :],
                                          start=True, stop=True)
                            last.then_inc(s_mm[n], 1)
                    for n in range(NDIR):
                        if j == CPS - 1:
                            pe.wait_ge(u_ev[n], CPS * p + j + 1)
                        for q in range(NSEQ):
                            c = cs[n][q]
                            if j > 0:
                                mm(ps[:, n, c * C:(c + 1) * C], st[:, n, q, :], ar[:, n, c, C:P], start=True, stop=False)
                            for h, (lo, hi) in enumerate(halves):
                                last = mm(ps[lo:hi, n, c * C:(c + 1) * C], wv[:, c, lo:hi], gm[:, n, h, c, C:P],
                                          start=(j == 0), stop=True)
                        last.then_inc(y_mm, 1)

            def later(s, v):
                if not isinstance(v, int) or v > 0:
                    pe.wait_ge(s, v)

            def first_inputs():
                w = ring[:, 0, :]
                pe.wait_ge(pair_in, 16)
                def wide(bank, n, src):
                    return product(ps[:, bank, :], w[:, n * D:(n + 1) * D], src)

                def second(bank, f, n):
                    lo, hi = halves[n]
                    mm(ps[:, bank, :], w[lo:hi, (24 + f) * P:(25 + f) * P], lora[lo:hi, f, :],
                       start=True, stop=True).then_inc(projected, 1)

                wide(7, 1, xk).then_inc(projected, 1)
                second(2, 1, 0)
                second(3, 1, 1)
                second(0, 0, 0)
                pe.wait_ge(evac, 2)
                mm(ps[:, 6, :], blk, t_sq, start=True, stop=True).then_inc(head_sum, 1)
                wide(5, 0, xr).then_inc(projected, 1)
                second(1, 0, 1)
                wide(4, 2, xv).then_inc(pair_used, 1)
                pe.wait_ge(bon_in, 1)
                mm(ps[:, 7, :], blk, t_sq, start=True, stop=True).then_inc(head_sum, 1)

            first_inputs()
            pair(0, False, True)
            with pe.Fori(1, KT - 1) as p:
                pair(p, True, True)
            pair(KT - 1, True, False)
            pe.wait_ge(y_in, KT)
            mm(ps[:, 6, :], blk, o_res[:, KT - 1, :], start=True, stop=True).then_inc(mean_mm, 1)
            pe.wait_ge(dev_sq, KT)
            mm(ps[:, 2, :], blk, c_sq, start=True, stop=True).then_inc(var_mm, 1)
            pe.wait_ge(gated, KT - 1)
            pe.wait_ge(gate_in, 16 * KT)
            mm(ps[:, 7, :], gbt[:], lora[:, 2, :], start=True, stop=True).then_inc(gate_mm, 1)
            square(o_hi, o_lo)
            output_sum()
            norm_sums()
            mlp(0)
            output_sum()
            norm_sums()

            pe.sem_inc(a_pv, 1)
            for m, bank in enumerate((0, 1, 6, 7)):
                piece(w.n + m, m % 2, ps[:, bank, :], att_hi, h_lo, KT, fresh=(m == 0))
                if m >= KVH:
                    pe.wait_ge(a_ev, m - KVH + 1)
                    mm(ps[:, 2 + m - KVH, :], ones, asq[m - KVH], start=True, stop=True).then_inc(a_ss, 1)
            w.add(2 * KVH)
            moved[0] += KT
            for s in range(2):
                piece(w.n + s, s, ps[:, s, :], att_hi, h_lo, KT)
                pe.wait_ge(v_tr, s + 1)
                for b in range(4):
                    last = tp(ps[:, 4 + s, b * P:(b + 1) * P], qh[s][:, b * P:(b + 1) * P], ident)
                last.then_inc(a_tr, 1)

            def query_squares(h, s):
                pe.wait_ge(a_ev, KVH + h + 1)
                pe.wait_ge(a_rt, h + KVH - 1)
                mm(ps[:, 2 + s, :], ones, asq[s], start=True, stop=True).then_inc(a_ss, 1)

            for s in range(2):
                query_squares(s, s)
            pe.wait_ge(v_in, KVH)

            def heads(j, g, ahead):
                for s in range(2):
                    h = 2 * j + s
                    pe.wait_ge(a_q, KVH + 1 + h)
                    pe.wait_ge(a_ex, h + 1)
                    for q in range(NSEQ):
                        for b in range(2):
                            o = q * SEQ + b * P
                            last = mm(ps[:, 4 + q, b * SEQ:(b + 1) * SEQ], qh[s][:, o:o + P],
                                      kh[:, g, q * SEQ:(q + 1) * SEQ], start=True, stop=True)
                    last.then_inc(a_sc, 1)
                    if s == 1:
                        weighted(h - 1, 0, g, ahead)
                    if ahead:
                        pe.wait_ge(a_o, h + 1)
                        piece(w.n + h + 2, s, ps[:, s, :], att_hi, h_lo, KT)
                    pe.wait_ge(a_p, h + 1)
                    pe.wait_ge(a_te, h + 1)
                    for q in range(NSEQ):
                        for k in range(2):
                            for b in range(2):
                                o = (k * 2 + b) * P
                                last = tp(ps[:, 6 + q, o:o + P], prob[:, 2 * q + b, k * P:(k + 1) * P], ident)
                    last.then_inc(a_tr, 1)
                weighted(h, 1, g, ahead)

            def weighted(h, s, g, ahead):
                if ahead and s == 0:
                    query_squares(h + 2, s)
                pe.wait_ge(a_te, h + 2)
                for q in range(NSEQ):
                    for k in range(2):
                        last = mm(ps[:, s, q * SEQ:(q + 1) * SEQ], vh[:, g, 2 * q + k, :], prT[:, q, k, :],
                                  start=(k == 0), stop=(k == 1))
                last.then_inc(a_pv, 1)
                if ahead and s == 1:
                    query_squares(h + 2, s)

            with pe.Fori(0, 2) as j:
                heads(j, 0, True)
            heads(2, 1, True)
            heads(3, 1, False)
            w.add(QH, 2)
            square(o_hi, o_lo)
            output_sum()
            norm_sums()
            mlp(1)
            output_sum()

        @block.scalar
        def _(act):
            A = nc.scalar.activation
            norms = [0]
            gq, gk = pt[:, C_QKG:C_QKG + 1], pt[:, C_QKG + 1:C_QKG + 2]

            pres, outs = [0], [0]

            def norm_squares():
                base = pres[0] * KT
                for k in range(KT):
                    if base + k >= 2:
                        act.wait_ge(sq_used, base + k - 1)
                    if norms[0]:
                        act.wait_ge(scaled_used, (norms[0] - 1) * KT + k + 1)
                    A(sq2[k % 2], x_res[:, k, :], ACT.Square).then_inc(sq_ready, 1)
                act.wait_ge(sq_used, base + KT)
                A(rs, ps[:, 0, :], ACT.Sqrt, bias=ct[:, K_EPS:K_EPS + 1]).then_inc(root, 1)
                norms[0] += 1
                pres[0] += 1

            def output_squares(k, slot, bank):
                act.wait_ge(out_sq_added, outs[0] * KT + k + 1)
                A(out_sq[slot], bank, ACT.Square).then_inc(out_sq_in, 1)

            def output_root():
                outs[0] += 1
                act.wait_ge(out_sum_mm, outs[0])
                A(rs, ps[:, 7, :], ACT.Sqrt, bias=ct[:, K_EPS:K_EPS + 1]).then_inc(root, 1)
                norms[0] += 1

            def norm_affine(l, shift, split=None):
                base = (pres[0] - 1) * KT
                for k in range(KT):
                    act.wait_ge(scaled, base + k + 1)
                    for q in range(NSEQ):
                        last = A(h_in[:, k, q, :], tmp4[k % NTMP][:, q * SEQ:(q + 1) * SEQ], ACT.Identity,
                                 scale=gs[:, k, q:q + 1], bias=mod[:, (6 * l + shift) * KT + k, q:q + 1])
                    last.then_inc(scaled_used, 1)
                    if split is not None and k % 2:
                        act.wait_ge(scaled_used, (norms[0] - 1) * KT + k + 1)
                        A(seqs(split[:, k, :]), h_in[:, k], ACT.Copy).then_inc(h_high_odd, 1)

            w = Pieces()

            def used(n):
                act.wait_ge(w_used, n + 1)

            def high(n, r, count, cols=D):
                act.wait_ge(piece_in[r], 16 * count + 16)
                if not isinstance(n, int) or n >= 2:
                    act.wait_ge(w_used, n - 1)
                A(split_w[:, r % 2, 0, 0:cols], raw_w[:, r, 0:cols], ACT.Copy).then_inc(w_hi, 1)

            def high_input(finished, before):
                for k in range(KT):
                    act.wait_ge(finished, before + k + 1)
                    A(o_hi[:, k, :], o_res[:, k, :], ACT.Copy).then_inc(h_high, 1)

            def square():
                for m in range(KT):
                    used(w.n + m)
                    output_squares(m, m % 2, ps[:, m % NRAW, :])
                    A(mix_out[:, m, :], ps[:, m % NRAW, :], ACT.Copy).then_inc(copied, 1)
                    high(w.n + m + 2, (m + 2) % NRAW, w.slot[(m + 2) % NRAW] + (m + 2) // NRAW)
                w.add(KT)

            def mlp(l, last_mlp):
                def up_round(i, cols):
                    for s in range(2):
                        n = w.n + NRAW * i + 2 * s
                        used(n)
                        r = (2 * s + 2) % NRAW
                        high(n + 2, r, w.slot[r] + i + s, cols if s else D)
                        act.wait_ge(fcols, l * FT + 2 * i + s + 1)
                        act.wait_ge(taken[s], l * FT // 2 + i + 1)
                        A(u_pad[s][:, :, 1:SEQ + 1], seqs(ps[:, 2 * s, :]), ACT.Copy)
                        A(conv[s], ps[:, 2 * s, :], ACT.Identity, scale=fcur[:, s, 1:2],
                          bias=fcur[:, s, 3:4]).then_inc(u_ready, 1)
                        high(n + 3, r + 1, w.slot[r + 1] + i + s, cols if s else D)
                        act.wait_ge(conv_ready, l * FT + 2 * i + s + 1)
                        A(conv[s], conv[s], ACT.Silu).then_inc(silu_ready, 1)

                def down_round(i, ahead):
                    for s in range(2):
                        for h in range(2):
                            n = w.n + NRAW * i + 2 * s + h
                            used(n)
                            if h == 1:
                                output_squares(2 * i + s, s, ps[:, 4 + s, :])
                                A(o_res[:, bass.ds(2 * i + s, 1), :], ps[:, 4 + s:5 + s, :], ACT.Copy).then_inc(copied, 1)
                            r = (2 * s + h + 2) % NRAW
                            if s == 0 or ahead:
                                high(n + 2, r, w.slot[r] + i + s, D if s == 1 and ahead == D else PIECE)

                with act.Fori(0, FT // 2 - 1) as i:
                    up_round(i, D)
                up_round(FT // 2 - 1, PIECE)
                w.add(2 * FT)
                with act.Fori(0, KT // 2 - 1) as i:
                    down_round(i, PIECE)
                down_round(KT // 2 - 1, 0 if last_mlp else D)
                w.add(2 * KT)

            act.wait_ge(c_in, 16)
            A(csil[:], csil[:], ACT.Silu).then_inc(c_ready, 1)

            def ada(i):
                def columns_out(n):
                    act.wait_ge(ada_cols, ADA * i + n + 1)
                    m = TOK // P
                    A(mod[:, bass.ds(2 * 6 * i + m * n, m), :], ps[:, 4 + n, 0:2 * m].rearrange("p (m q) -> p m q", m=m),
                      ACT.Copy).then_inc(ada_taken, 1)

                for n in range(ADA):
                    act.wait_ge(ada_done[n], i + 1)
                    A(ada_rows[n], ps[0:NSEQ, n, :], ACT.Copy).then_inc(ada_row, 1)
                    if n > 0:
                        columns_out(n - 1)
                columns_out(ADA - 1)

            with act.Fori(0, ADA_FIRST) as i:
                ada(i)
            act.wait_ge(x_in, 16)
            act.wait_ge(ct_in, 16)
            norm_squares()
            norm_affine(0, 0)
            with act.Fori(ADA_FIRST, ADA_ROUNDS) as i:
                ada(i)
            act.wait_ge(lora_mm, 1)
            A(lora[:, 0, :], ps[:, 1, :], ACT.Tanh)
            A(lora[:, 1, :], ps[:, 2, :], ACT.Copy)
            A(lora[:, 2, :], ps[:, 3, :], ACT.Sigmoid)
            barrier(act)

            pairs = [ps[:, 2 * n:2 * n + 2, :].rearrange("p b (c s) -> p (b c) s", s=P) for n in range(NDIR)]

            def next_inputs(a, step, banks=(7, 6, 6, 7, 7, 7, 7, 7)):
                bk, br, bv, bw0, bw1, ba0, ba1, bn = banks

                def sigmoid(count, dst, bank, col):
                    act.wait_ge(projected, 6 * a + count)
                    A(dst, ps[:, bank, :], ACT.Sigmoid, bias=pc(col)).then_inc(evac, 1)

                if step == 0:
                    act.wait_ge(projected, 6 * a + 1)
                    act.wait_ge(pcols, a + 1)
                    if not isinstance(a, int) or a > 0:
                        act.wait_ge(carried, a)
                    A(t_k, ps[:, bk, :], ACT.Copy).then_inc(evac, 1)
                    A(t_sq, ps[:, bk, :], ACT.Square, scale=pc(4)).then_inc(evac, 1)
                elif step == 1:
                    act.wait_ge(head_sum, 2 * a + 1)
                    A(t_b1, ps[:, bn, :], ACT.Sqrt, scale=float(HEAD)).then_inc(norm_root, 1)
                elif step == 2:
                    sigmoid(2, t_a[0], ba0, 2)
                elif step == 3:
                    sigmoid(3, t_a[1], ba1, 3)
                elif step == 4:
                    sigmoid(4, s_w[0], bw0, 0)
                elif step == 5:
                    act.wait_ge(projected, 6 * a + 5)
                    A(t_r, ps[:, br, :], ACT.Copy).then_inc(evac, 1)
                    sigmoid(6, s_w[1], bw1, 1)
                elif step == 6:
                    act.wait_ge(pair_used, a + 1)
                    A(t_v, ps[:, bv, :], ACT.Copy).then_inc(evac, 1)
                else:
                    n = step - 7
                    act.wait_ge(cum, 2 * a + n + 1)
                    A(s_e2, s_inc, ACT.Exp, scale=DECAY).then_inc(expd, 1)
                    A(s_exc, s_exc, ACT.Exp, scale=-DECAY).then_inc(expd, 1)
                    act.wait_ge(expd, 6 * a + 3 * n + 2)
                    A(s_inc, s_inc, ACT.Exp, scale=-DECAY).then_inc(expd, 1)

            def pair(p, before, after):
                a, b = p + 1, p - 1
                for g in range(6):
                    act.wait_ge(tr, 6 * p + g + 1)
                    bank = (4, 5, 0, 1)[g % 4]
                    dst = kb[:, g // 2, 4 * (g % 2):4 * (g % 2) + 4, :] if g < 4 else wv[0:C, 4 * (g - 4):4 * (g - 3), :]
                    src = ps[:, bank, :] if g < 4 else ps[0:C, bank, :]
                    A(dst, src.rearrange("p (c s) -> p c s", c=4), ACT.Copy).then_inc(tr_in, 1)
                if before:
                    act.wait_ge(centred, b + 1)
                    act.sem_inc(act_tick, 1)
                    A(c_sq, o_res[:, b, :], ACT.Square).then_inc(dev_sq, 1)
                if after:
                    next_inputs(a, 0)
                for n in range(NDIR):
                    act.wait_ge(tmm[n], LEVELS * p + 1)
                    A(mc[0:C, n, :, :], pairs[n][0:C, :, 0:C], ACT.Copy)
                    A(mc[C:P, n, :, :], pairs[n][C:P, :, C:P], ACT.Copy).then_inc(mev[n], 1)
                for l in range(LEVELS):
                    if l > 0:
                        act.wait_ge(tmm[0], LEVELS * p + l + 1)
                        A(mt[0:C, 0, :, 0:C], pairs[0][0:C, :, 0:C], ACT.Copy)
                        A(mt[C:P, 0, :, C:P], pairs[0][0:C, :, C:P], ACT.Copy).then_inc(tev[0], 1)
                    if l == 1 and before:
                        act.wait_ge(var_mm, b + 1)
                        A(c_b, ps[:, 6, :], ACT.Sqrt, bias=ct[:, K_EPS + 1:K_EPS + 2]).then_inc(var_root, 1)
                    if after:
                        next_inputs(a, l + 1)
                    if l < LEVELS - 1:
                        for n in range(NDIR):
                            act.wait_ge(mmm[n], (LEVELS - 1) * p + l + 1)
                            A(mc[:, n, :, :], chunks(ps[:, 4 + n, :]), ACT.Copy).then_inc(mev[n], 1)
                for n in range(NDIR):
                    act.wait_ge(fmm[n], p + 1)
                    for h in range(2):
                        last = A(mf[:, n, :, h, :], chunks(ps[0:C, 2 * n + h, :]), ACT.Copy)
                    last.then_inc(fev[n], 1)
                for j in range(CPS):
                    for n in range(NDIR):
                        act.wait_ge(x0_mm[n], CPS * p + j + 1)
                        A(x0s[:, n, :, :], ps[0:C, 4 + n, 0:2 * P].rearrange("p (q i) -> p q i", q=NSEQ),
                          ACT.Copy).then_inc(x0_ev[n], 1)
                    if after and j == 1:
                        next_inputs(a, 7)
                        next_inputs(a, 6)
                    if after and j == 3:
                        next_inputs(a, 8)
                act.wait_ge(y_mm, 2 * CPS * (p + 1))
                act.sem_inc(act_tick, 1)
                A(o_res[:, p, :], ps[:, 0, :], ACT.Copy).then_inc(y_cp, 1)

            for step in range(9):
                next_inputs(0, step, (7, 5, 4, 0, 1, 2, 3, 6))
            pair(0, False, True)
            with act.Fori(1, KT - 1) as p:
                pair(p, True, True)
            pair(KT - 1, True, False)
            act.wait_ge(centred, KT)
            A(c_sq, o_res[:, KT - 1, :], ACT.Square).then_inc(dev_sq, 1)
            high(0, 0, 0)
            act.wait_ge(var_mm, KT)
            A(c_b_last, ps[:, 2, :], ACT.Sqrt, bias=ct[:, K_EPS + 1:K_EPS + 2]).then_inc(var_root, 1)
            high_input(gated, 0)
            high(1, 1, 0)
            square()
            output_root()
            norm_squares()
            norm_affine(0, 3, h_hi)
            mlp(0, False)
            output_root()
            norm_squares()
            norm_affine(1, 0, att_hi)
            for x in range(KVH):
                used(w.n + x)
                high(w.n + x + 2, x + 2, w.slot[x + 2])
                A(raw[x], ps[:, x, :], ACT.Identity, scale=gk)
                A(asq[x], ps[:, x, :], ACT.Square).then_inc(a_ev, 1)
            for g in range(KVH):
                used(w.n + KVH + g)
                high(w.n + 2 * KVH + g, g, w.slot[g] + 1)
                A(qh[g], ps[:, 6 + g, :], ACT.Copy).then_inc(v_tr, 1)
            w.add(2 * KVH)

            def root_of(n, s):
                act.wait_ge(a_ss, n + 1)
                act.wait_ge(a_q, n - 1)
                A(ars[s], ps[:, 2 + s, :], ACT.Sqrt, scale=float(D // AH), bias=ct[:, K_EPS:K_EPS + 1]).then_inc(a_rt, 1)

            def query(h, s, n):
                used(w.n + h)
                high(w.n + h + 2, s, w.slot[s] + n)
                act.wait_ge(a_q, h + 1)
                A(raw[s], ps[:, s, :], ACT.Identity, scale=gq)
                A(asq[s], ps[:, s, :], ACT.Square).then_inc(a_ev, 1)

            for x in range(KVH):
                act.wait_ge(a_ss, x + 1)
                A(ars[x], ps[:, 2 + x, :], ACT.Sqrt, scale=float(D // AH), bias=ct[:, K_EPS:K_EPS + 1]).then_inc(a_rt, 1)
            for s in range(2):
                query(s, s, 1)
                act.wait_ge(a_tr, s + 1)
                A(vh[:, s, :, :], ps[:, 4 + s, :].rearrange("p (b d) -> p b d", b=4), ACT.Copy).then_inc(v_in, 1)
            for s in range(2):
                root_of(KVH + s, s)

            def heads(j, ahead):
                for s in range(2):
                    h = 2 * j + s
                    act.wait_ge(a_mx, h + 1)
                    act.wait_ge(a_tr, KVH + h)
                    for b in range(4):
                        last = A(prob[:, b, :], ps[:, 4 + b // 2, (b % 2) * SEQ:(b % 2 + 1) * SEQ], ACT.Exp,
                                 scale=float(AH) ** -0.5, bias=stat[:, 4 + b:5 + b], accum_out=stat[:, 8 + b:9 + b])
                    last.then_inc(a_ex, 1)
                    if s == 1 and ahead:
                        root_of(KVH + h + 1, 0)
                    if ahead:
                        query(h + 2, s, j + 2)
                    act.wait_ge(a_tr, KVH + h + 1)
                    act.wait_ge(a_pv, h + 1)
                    for q in range(NSEQ):
                        last = A(prT[:, q, :, :], ps[:, 6 + q, :].rearrange("p (k t) -> p k t", k=2), ACT.Copy)
                    last.then_inc(a_te, 1)
                if ahead:
                    root_of(KVH + h + 2, 1)

            act.sem_inc(a_ex, 1)
            act.sem_inc(a_te, 1)
            with act.Fori(0, 2) as j:
                heads(j, True)
            heads(2, True)
            heads(3, False)
            w.add(QH, 2)
            high_input(a_o, 2)
            square()
            output_root()
            norm_squares()
            norm_affine(1, 3, h_hi)
            mlp(1, True)
            output_root()

        @block.vector
        def _(dve):
            own = Own(dve, dve_own)
            V = nc.vector
            norms, posts, others = [0], [0], [0]

            def gains(l, norm, part_, pre):
                g = pt[:, C_NORM + (4 * l + norm) * KT:C_NORM + (4 * l + norm + 1) * KT].unsqueeze(2).broadcast_to([P, KT, NSEQ])
                m = mod[:, (6 * l + part_) * KT:(6 * l + part_ + 1) * KT, :]
                own.wait()
                own(V.scalar_tensor_tensor(gs[:], m, 1.0 if pre else 0.0, g, ALU.add, ALU.mult))

            def inverse_root():
                dve.wait_ge(root, norms[0] + 1)
                return V.reciprocal(rs, rs)

            highs = [0, 0]

            def low_input(src, lo, hi, odd=0):
                s = h_high_odd if odd else h_high
                highs[odd] += 1
                dve.wait_ge(s, highs[odd])
                V.tensor_tensor(lo, src, hi.bitcast(F32), ALU.subtract).then_inc(moving, 1)

            def biases(lo, hi):
                b = pt[:, C_ADAB + lo:C_ADAB + hi].unsqueeze(2).broadcast_to([P, hi - lo, NSEQ])
                dve.wait_ge(ada_taken, ADA + hi * P // TOK)
                own(V.tensor_tensor(mod[:, lo:hi, :], mod[:, lo:hi, :], b, ALU.add))

            def pre_norm(l, norm, scale_part, hi=None):
                own.wait()
                own(inverse_root())
                if norms[0] == 0:
                    biases(0, ADA_FIRST * ADA * TOK // P)
                gains(l, norm, scale_part, True)
                own.wait()
                base = norms[0] * KT
                for k in range(KT):
                    if base + k >= NTMP:
                        dve.wait_ge(scaled_used, base + k - NTMP + 1)
                    own.wait()
                    V.tensor_tensor(tmp4[k % NTMP], x_res[:, k, :], rs, ALU.mult).then_inc(scaled, 1)
                    if hi is not None and k >= 2:
                        low_input(h_in[:, k - 2], h_lo[:, k - 2], seqs(hi[:, k - 2, :]), k % 2)
                if hi is not None:
                    for k in range(KT - 2, KT):
                        low_input(h_in[:, k], h_lo[:, k], seqs(hi[:, k, :]), k % 2)
                norms[0] += 1

            outs = [0]

            def add_output_squares():
                own.wait()
                own(V.memset(out_sum, 0.0))
                for k in range(KT):
                    dve.wait_ge(out_sq_in, outs[0] * KT + k + 1)
                    own.wait()
                    if k:
                        dve.wait_ge(out_sq_added, 2 + outs[0] * KT + k)
                    V.tensor_tensor(out_sum, out_sum, out_sq[k % 2], ALU.add).then_inc(out_sq_added, 1)
                outs[0] += 1

            def post_norm(l, norm, gate_part, src):
                gains(l, norm, gate_part, False)
                own.wait()
                inverse_root().then_inc(rstd, 1)
                posts[0] += 1
                dve.wait_ge(rstd, posts[0])
                base = norms[0] * KT
                for k in range(KT):
                    if k in OWN_PRODUCTS:
                        dve.wait_ge(scaled_used, base + k - NTMP + 1)
                        own(V.tensor_tensor(tmp4[k % NTMP], src[:, k, :], rs, ALU.mult))
                    else:
                        others[0] += 1
                        dve.wait_ge(out_scaled, others[0])
                    for q in range(NSEQ):
                        xs = x_res[:, k, q * SEQ:(q + 1) * SEQ]
                        own.wait()
                        last = V.scalar_tensor_tensor(xs, tmp4[k % NTMP][:, q * SEQ:(q + 1) * SEQ], gs[:, k, q:q + 1], xs,
                                                      ALU.mult, ALU.add)
                    last.then_inc(scaled_used, 1)
                norms[0] += 1

            def mlp(l):
                own.loop_start()
                with dve.Fori(0, FT // 2) as i:
                    for s in range(2):
                        own.wait()
                        V.tensor_copy(fcur[:, s, :], pt[:, bass.ds(C_FFN + 4 * (l * FT + s) + 8 * i, 4)]).then_inc(fcols, 1)
                    for s in range(2):
                        dve.wait_ge(u_ready, l * FT + 2 * i + s + 1)
                        own.wait()
                        own(V.scalar_tensor_tensor(seqs(conv[s]), u_pad[s][:, :, 0:SEQ], fcur[:, s, 0:1], seqs(conv[s]),
                                                   ALU.mult, ALU.add))
                        own.wait()
                        V.scalar_tensor_tensor(seqs(conv[s]), u_pad[s][:, :, 2:SEQ + 2], fcur[:, s, 2:3], seqs(conv[s]),
                                               ALU.mult, ALU.add).then_inc(conv_ready, 1)
                        dve.wait_ge(silu_ready, l * FT + 2 * i + s + 1)
                        dve.wait_ge(w_used, mlp_base[l] + NRAW * i + 2 * s + 2)
                        own(V.tensor_tensor(conv[s], conv[s], ps[:, 2 * s + 1, :], ALU.mult))
                        own.wait()
                        own(V.tensor_copy(ff_hi[:, bass.ds(2 * i + s, 1), :].squeeze(1), conv[s]))
                        own.wait()
                        V.tensor_tensor(ff_lo[:, bass.ds(2 * i + s, 1), :].squeeze(1), conv[s],
                                        ff_hi[:, bass.ds(2 * i + s, 1), :].squeeze(1).bitcast(F32),
                                        ALU.subtract).then_inc(taken[s], 1)
                    own.loop_end()

            mlp_base = (KT, 3 * KT + 2 * FT + 2 * KVH + QH + KT)
            for s in range(2):
                dve.sem_inc(taken[s], 1)
            dve.sem_inc(copied, NRAW)
            dve.sem_inc(ada_taken, ADA)
            dve.sem_inc(out_sq_added, 2)
            dve.sem_inc(a_o, 2)
            dve.wait_ge(pt_in, 16)
            dve.wait_ge(x_in, 16)
            pair_tab = pt[:, C_PAIR:C_PAIR + KT * NPP].rearrange("p (k n) -> p k n", n=NPP)
            own.wait()
            own(V.tensor_scalar(derived[:, :, 0:1], pair_tab[:, :, 4:5], -1.0, None, ALU.mult))
            own.wait()
            own(V.tensor_scalar(derived[:, :, 1:2], pair_tab[:, :, 5:6], -1.0, 1.0, ALU.mult, ALU.add))
            pre_norm(0, 0, 1)
            mu = lambda n, k: pt[:, C_MU + n * KT + k:C_MU + n * KT + k + 1]
            dve.wait_ge(scaled_used, KT)
            dve.wait_ge(pads_in, 1)
            for k in range(KT):
                hk = h_pad[:, k]
                own.wait()
                own(V.tensor_tensor(seqs(hsum), hk[:, :, 0:SEQ], hk[:, :, 2:SEQ + 2], ALU.add))
                own.wait()
                own(V.scalar_tensor_tensor(seqs(x_res[:, k, :]), seqs(hsum), 0.5, h_in[:, k], ALU.mult, ALU.subtract))
                own.wait()
                for n, dst in ((0, xr), (2, xk), (3, xv)):
                    own(V.scalar_tensor_tensor(seqs(dst[:, k, :]), seqs(x_res[:, k, :]), mu(n, k), h_in[:, k],
                                               ALU.mult, ALU.add))
            n_ring = 0
            own.wait()
            for k in range(KT):
                for n in (1, 4, 5):
                    if n_ring >= 4:
                        dve.wait_ge(mixed_used, n_ring - 3)
                    V.scalar_tensor_tensor(seqs(mix4[n_ring % 4]), seqs(x_res[:, k, :]), mu(n, k), h_in[:, k], ALU.mult,
                                           ALU.add).then_inc(mixed, 1)
                    n_ring += 1
            biases(ADA_FIRST * ADA * TOK // P, DEPTH * 6 * KT)
            own.wait()
            barrier(dve)

            pairs = [ps[:, 2 * n:2 * n + 2, :].rearrange("p b (c s) -> p (b c) s", s=P) for n in range(NDIR)]
            res = ct[:, K_RES:K_RES + TOK]

            def pair_columns(a):
                own(V.tensor_copy(pcur[:, 0:NPP], pt[:, bass.ds(C_PAIR + NPP * a, NPP)]))
                V.tensor_copy(pcur[:, NPP:NPP + 2], derived[:, bass.ds(a, 1), :].squeeze(1)).then_inc(pcols, 1)
                dve.wait_ge(pcols, a + 1)

            def key_direction(a):
                dve.wait_ge(norm_root, a + 1)
                own(V.tensor_scalar_max(t_b1, t_b1, 1e-12))
                own.wait()
                own(V.reciprocal(t_b1, t_b1))
                own.wait()
                own(V.scalar_tensor_tensor(t_nkk, t_k, pc(NPP), t_b1, ALU.mult, ALU.mult))
                own.wait()

            def rates(a):
                dve.wait_ge(evac, 8 * a + 4)
                for n in range(NDIR):
                    own(V.scalar_tensor_tensor(t_b[n], t_nkk, -1.0, t_a[n], ALU.mult, ALU.mult))
                own.wait()
                for n in range(NDIR):
                    last = V.tensor_scalar(t_a[n], t_a[n], pc(5), pc(NPP + 1), ALU.mult, ALU.add)
                last.then_inc(kdf, 1)

            def decays(a):
                dve.wait_ge(evac, 8 * a + 5)
                V.tensor_tensor_scan(s_inc, res, s_w[0], 0.0, ALU.mult, ALU.add).then_inc(scanned, 1)

            def bonus(a, step):
                if step == 0:
                    dve.wait_ge(kd_sum, a + 1)
                    dve.wait_ge(evac, 8 * a + 6)
                    V.scalar_tensor_tensor(t_sq, t_r, pc(6), t_sq, ALU.mult, ALU.mult).then_inc(bon_in, 1)
                else:
                    dve.wait_ge(head_sum, 2 * a + 2)
                    dve.wait_ge(evac, 8 * a + 8)
                    if not isinstance(a, int) or a > 0:
                        dve.wait_ge(bon_copied, a)
                    V.scalar_tensor_tensor(t_bonn, ps[:, 7, :], float(HEAD), t_v, ALU.mult, ALU.mult).then_inc(bon_in, 1)

            def decays_back(a, step):
                if step == 0:
                    dve.wait_ge(cum, 2 * a + 1)
                    dve.wait_ge(evac, 8 * a + 7)
                    own(V.tensor_tensor_scan(s_l, res, s_w[1], 0.0, ALU.mult, ALU.add))
                    dve.wait_ge(expd, 6 * a + 3)
                    V.tensor_copy(pendn[:, 0, :], chunks(s_inc)[:, :, C - 1])
                    own(V.tensor_tensor(arn[:, 0, :, 0:C], chunks(t_nkk), chunks(s_exc), ALU.mult))
                    own(V.tensor_tensor(arn[:, 0, :, C:P], chunks(t_r), chunks(s_inc), ALU.mult))
                    own.wait()
                else:
                    dve.wait_ge(prod, a + 1)
                    tot = chunks(s_l)[:, :, C - 1:C].broadcast_to([P, NCH, C])
                    own(V.tensor_tensor(chunks(s_exc), tot, chunks(s_l), ALU.subtract))
                    own.wait()
                    V.tensor_tensor(s_inc, s_exc, s_w[1], ALU.add).then_inc(cum, 1)

            def last_products(a):
                dve.wait_ge(expd, 6 * a + 6)
                V.tensor_copy(pendn[:, 1, :], chunks(s_inc)[:, :, 0])
                V.tensor_tensor(arn[:, 1, :, 0:C], chunks(t_nkk), chunks(s_exc), ALU.mult)
                V.tensor_tensor(arn[:, 1, :, C:P], chunks(t_r), chunks(s_inc), ALU.mult).then_inc(prep, 1)

            def centre(b, bank):
                dve.wait_ge(mean_mm, b + 1)
                V.tensor_tensor(o_res[:, b, :], o_res[:, b, :], ps[:, bank, :], ALU.subtract).then_inc(centred, 1)

            def finish(b, step, c_b=c_b):
                o = o_res[:, b, :]
                if step == 0:
                    dve.wait_ge(var_root, b + 1)
                    own(V.reciprocal(c_b, c_b))
                    own.wait()
                    own(V.tensor_tensor(o, o, c_b, ALU.mult))
                    own.wait()
                elif step == 1:
                    own(V.tensor_scalar(o, o, pt[:, bass.ds(C_PAIR + NPP * b + 7, 1)], pt[:, bass.ds(C_PAIR + NPP * b + 8, 1)],
                                        ALU.mult, ALU.add))
                    own.wait()
                    dve.wait_ge(bon_copied, b + 1)
                    own(V.tensor_tensor(o, o, t_bon, ALU.add))
                    own.wait()
                else:
                    dve.wait_ge(gate_mm, b + 2)
                    V.tensor_tensor(o, o, ps[:, 7, :], ALU.mult).then_inc(gated, 1)

            def pair(p, before, after):
                a, b = p + 1, p - 1
                for n in range(NDIR):
                    dve.wait_ge(sys, 2 * p + n + 1)
                    msk = ct[:, K_NT + n * C:K_NT + (n + 1) * C].unsqueeze(1).broadcast_to([P, NCH, C])
                    for h, (lo, hi) in enumerate(halves):
                        last = V.tensor_tensor(nt[lo:hi, n, :, lo:hi], chunks(ps[lo:hi, 2 + n, :]), msk[lo:hi], ALU.mult)
                    last.then_inc(sys_in, 1)
                for g in range(8):
                    dve.wait_ge(gram, 8 * p + g + 1)
                    n, h, q = g // 4, (g // 2) % 2, g % 2
                    bank = (4, 5, 0, 1)[g % 4]
                    msk = ct[:, K_GM + n * P:K_GM + (n + 1) * P].unsqueeze(1).broadcast_to([P, 4, P])
                    V.tensor_tensor(gm[:, n, h, 4 * q:4 * q + 4, :], ps[:, bank, :].rearrange("p (c s) -> p c s", c=4), msk,
                                    ALU.mult).then_inc(gram_in, 1)
                if before:
                    centre(b, 6)
                if after:
                    pair_columns(a)
                for l in range(LEVELS):
                    for n in range(NDIR):
                        dve.wait_ge(xmm[n], LEVELS * p + l + 1)
                        o = K_LV + (n * LEVELS + l) * C
                        msk = ct[:, o:o + C].unsqueeze(1).broadcast_to([P, NCH, C])
                        V.tensor_tensor(xc[:, n, :, :], chunks(ps[:, 4 + n, :]), msk, ALU.mult).then_inc(xev[n], 1)
                    if l > 0:
                        dve.wait_ge(tmm[1], LEVELS * p + l + 1)
                        V.tensor_copy(mt[0:C, 1, :, 0:C], pairs[1][0:C, :, 0:C])
                        V.tensor_copy(mt[C:P, 1, :, C:P], pairs[1][0:C, :, C:P]).then_inc(tev[1], 1)
                    if before and l == 1:
                        finish(b, 0)
                    if before and l == 2:
                        finish(b, 1)
                        finish(b, 2)
                    if after and l == 3:
                        key_direction(a)
                        rates(a)
                    if after and l == 4:
                        decays(a)
                pend4 = pend[:, :, :].rearrange("p n (q c) -> p n q c", q=NSEQ)
                wv4 = wv.rearrange("p (q c) i -> p q c i", q=NSEQ)
                for j in range(CPS):
                    for n in range(NDIR):
                        dve.wait_ge(u_mm[n], CPS * p + j + 1)
                        c = j if n == 0 else CPS - 1 - j
                        V.tensor_copy(wv4[C:P, :, c, :], ps[C:P, 4 + n, 256:512].rearrange("p (q i) -> p q i", q=NSEQ)).then_inc(u_ev[n], 1)
                    if j < CPS - 1:
                        for n in range(NDIR):
                            c = j if n == 0 else CPS - 1 - j
                            dve.wait_ge(s_mm[n], (CPS - 1) * p + j + 1)
                            for h, (lo, hi) in enumerate(halves):
                                sm = ps[lo:hi, 4 + n, 0:2 * P].rearrange("p (q i) -> p q i", q=NSEQ)[:, :, lo:hi]
                                if j > 0:
                                    own(V.tensor_tensor(stmp[lo:hi, n, :, :], sm, sx[lo:hi, j % 2, n, :, lo:hi], ALU.add))
                            if j > 0:
                                own.wait()
                            for h, (lo, hi) in enumerate(halves):
                                sm = ps[lo:hi, 4 + n, 0:2 * P].rearrange("p (q i) -> p q i", q=NSEQ)[:, :, lo:hi]
                                src = stmp[lo:hi, n, :, :] if j > 0 else sm
                                last = V.tensor_tensor(sx[lo:hi, (j + 1) % 2, n, :, lo:hi], src,
                                                       pend4[lo:hi, n, :, c:c + 1].broadcast_to([C, NSEQ, C]), ALU.mult)
                            last.then_inc(s_ev[n], 1)
                    if after:
                        if j == 0:
                            bonus(a, 0)
                        elif j == 1:
                            decays_back(a, 0)
                        elif j == 2:
                            bonus(a, 1)
                            decays_back(a, 1)
                        elif j == 3:
                            last_products(a)
                dve.wait_ge(y_cp, p + 1)
                V.tensor_tensor(o_res[:, p, :], ps[:, 1, :], o_res[:, p, :], ALU.add).then_inc(y_in, 1)
                dve.wait_ge(y_in, p + 1)

            dve.sem_inc(gate_mm, 1)
            pair_columns(0)
            key_direction(0)
            rates(0)
            decays(0)
            bonus(0, 0)
            decays_back(0, 0)
            bonus(0, 1)
            decays_back(0, 1)
            last_products(0)
            pair(0, False, True)
            own.loop_start()
            with dve.Fori(1, KT - 1) as p:
                pair(p, True, True)
                own.loop_end()
            pair(KT - 1, True, False)
            centre(KT - 1, 6)
            for step in range(3):
                finish(KT - 1, step, c_b_last)
            for k in range(KT):
                low_input(o_res[:, k, :], o_lo[:, k, :], o_hi[:, k, :])
            add_output_squares()
            dve.wait_ge(x_back, 16)
            post_norm(0, 1, 2, mix_out)
            pre_norm(0, 2, 4, h_hi)
            mlp(0)
            add_output_squares()
            post_norm(0, 3, 5, o_res)
            pre_norm(1, 0, 1, att_hi)

            def rotate(x, n):
                dve.wait_ge(a_ev, n + 1)
                own.wait()
                own(V.tensor_tensor(seqs(swp[x])[0:C], seqs(raw[x])[C:P], sinb[C:P], ALU.mult))
                own(V.tensor_tensor(seqs(swp[x])[C:P], seqs(raw[x])[0:C], sinb[0:C], ALU.mult))
                own(V.tensor_tensor(seqs(rot[x]), seqs(raw[x]), cosb, ALU.mult))
                own.wait()
                own(V.tensor_tensor(rot[x], rot[x], swp[x], ALU.add))

            def normalise(x, dst, n):
                dve.wait_ge(a_rt, n + 1)
                own(V.reciprocal(ars[x], ars[x]))
                own.wait()
                V.tensor_tensor(dst, rot[x], ars[x], ALU.mult).then_inc(a_q, 1)

            for x in range(KVH):
                rotate(x, x)
                normalise(x, kh[:, x, :], x)
            dve.wait_ge(v_in, KVH)
            rotate(0, KVH)
            normalise(0, qh[0], KVH)

            def heads(j, ahead):
                for s in range(2):
                    h = 2 * j + s
                    dve.wait_ge(a_sc, h + 1)
                    own.wait()
                    own(V.reduce_max(stat[:, 0:4], ps[:, 4:6, :].rearrange("p q (b k) -> p (q b) k", k=SEQ), AX_X))
                    own.wait()
                    V.tensor_scalar(stat[:, 4:8], stat[:, 0:4], -float(AH) ** -0.5, None, ALU.mult).then_inc(a_mx, 1)
                    more = s == 0 or ahead
                    if more:
                        rotate(1 - s, KVH + h + 1)
                    dve.wait_ge(a_ex, h + 2)
                    own.wait()
                    own(V.reciprocal(stat[:, 12:16], stat[:, 8:12]))
                    own.wait()
                    V.tensor_tensor(prob[:], prob[:], stat[:, 12:16].unsqueeze(2).broadcast_to([P, 4, SEQ]),
                                    ALU.mult).then_inc(a_p, 1)
                    if more:
                        normalise(1 - s, qh[1 - s], KVH + h + 1)
                for s in range(2):
                    h = 2 * j + s
                    dve.wait_ge(a_pv, h + 2)
                    dve.sem_inc(dve_tick, 1)
                    V.tensor_copy(o_res[:, h, :], ps[:, s, :]).then_inc(a_o, 1)
                own.wait()

            own.loop_start()
            with dve.Fori(0, 2) as j:
                heads(j, True)
                own.loop_end()
            heads(2, True)
            heads(3, False)
            for k in range(KT):
                low_input(o_res[:, k, :], o_lo[:, k, :], o_hi[:, k, :])
            add_output_squares()
            post_norm(1, 1, 2, mix_out)
            pre_norm(1, 2, 4, h_hi)
            mlp(1)
            add_output_squares()
            post_norm(1, 3, 5, o_res)

        @block.gpsimd
        def _(pool):
            own = Own(pool, pool_own)
            G = nc.gpsimd
            norms = [0]
            posts = [0]

            def u_pads():
                for s in range(2):
                    G.memset(u_pad[s][:, :, 0:1], 0.0)
                    G.memset(u_pad[s][:, :, SEQ + 1:SEQ + 2], 0.0)

            def high_input(hi):
                for k in range(0, KT, 2):
                    pool.wait_ge(scaled_used, norms[0] * KT + k + 1)
                    G.tensor_copy(seqs(hi[:, k, :]), h_in[:, k]).then_inc(h_high, 1)
                norms[0] += 1

            w = Pieces()

            def low(n, r, cols=D):
                pool.wait_ge(w_hi, n + 1)
                G.tensor_tensor(split_w[:, r % 2, 1, 0:cols], raw_w[:, r, 0:cols], split_w[:, r % 2, 0, 0:cols].bitcast(F32),
                                ALU.subtract).then_inc(w_lo, 1)

            def square():
                for m in range(KT):
                    low(w.n + m + 2, (m + 2) % NRAW)
                w.add(KT)

            def mlp(last_mlp):
                with pool.Fori(0, FT // 2 - 1) as i:
                    for m in range(NRAW):
                        low(w.n + NRAW * i + m + 2, (m + 2) % NRAW)
                for m in range(NRAW):
                    low(w.n + 2 * FT - NRAW + m + 2, (m + 2) % NRAW, D if m < 2 else PIECE)
                w.add(2 * FT)
                with pool.Fori(0, KT // 2 - 1) as i:
                    for m in range(NRAW):
                        low(w.n + NRAW * i + m + 2, (m + 2) % NRAW, PIECE)
                for m in range(2 if last_mlp else NRAW):
                    low(w.n + 2 * KT - NRAW + m + 2, (m + 2) % NRAW, PIECE if m < 2 else D)
                w.add(2 * KT)

            def post_norm(src):
                posts[0] += 1
                pool.wait_ge(rstd, posts[0])
                base = norms[0] * KT
                for k in range(KT):
                    if k in OWN_PRODUCTS:
                        continue
                    if base + k >= NTMP:
                        pool.wait_ge(scaled_used, base + k - NTMP + 1)
                    G.tensor_tensor(tmp4[k % NTMP], src[:, k, :], rs, ALU.mult).then_inc(out_scaled, 1)
                norms[0] += 1

            G.memset(sx[:], 0.0)
            G.memset(h_pad[:, :, :, 0:1], 0.0)
            G.memset(h_pad[:, :, :, SEQ + 1:SEQ + 2], 0.0).then_inc(pads_in, 1)
            norms[0] += 1
            barrier(pool)
            own(G.memset(nt, 0.0))
            own(G.memset(mt, 0.0))
            own.wait()
            def next_keys(a):
                pool.wait_ge(kdf, a + 1)
                own(G.tensor_tensor(t_a[0], t_a[0], t_k, ALU.mult))
                own.wait()
                own(G.tensor_tensor(t_a[1], t_a[1], t_k, ALU.mult))
                own.wait()
                G.tensor_tensor(t_sq, t_a[0], t_a[1], ALU.add).then_inc(kd_sum, 1)
                pool.wait_ge(kd_sum, a + 1)
                pool.wait_ge(scanned, a + 1)
                G.tensor_tensor(s_exc, s_inc, s_w[0], ALU.subtract).then_inc(cum, 1)
                pool.wait_ge(cum, 2 * a + 1)

            def products(a, n):
                if n == 0:
                    pool.wait_ge(head_sum, 2 * a + 2)
                pool.wait_ge(expd, 6 * a + 3 * n + 1)
                own(G.tensor_tensor(kbn[:, n, :, 0:C], chunks(t_a[n]), chunks(s_e2), ALU.mult))
                own.wait()
                last = G.tensor_tensor(kbn[:, n, :, C:P], chunks(t_b[n]), chunks(s_e2), ALU.mult)
                if n == 0:
                    last.then_inc(prod, 1)
                    pool.wait_ge(prod, a + 1)
                else:
                    last.then_inc(prep, 1)

            def carry(p, first=False):
                pool.wait_ge(prep, 2 * p + 2)
                if not first:
                    pool.wait_ge(y_in, p)
                pool.sem_inc(pool_tick, 1)
                own(G.tensor_copy(pend[:], pendn[:]))
                own.wait()
                G.tensor_copy(ar, arn).then_inc(carried, 1)

            def keep_bonus(p):
                pool.wait_ge(bon_in, 2 * p + 2)
                pool.sem_inc(pool_tick, 1)
                G.tensor_copy(t_bon, t_bonn).then_inc(bon_copied, 1)

            def pair(p, before, after):
                a = p + 1
                carry(p, not before)
                pool.wait_ge(carried, p + 1)
                for n in range(NDIR):
                    pool.wait_ge(sys_in, 2 * p + n + 1)
                    one = ct[:, K_ID:K_ID + P].unsqueeze(1).broadcast_to([P, NCH, P])
                    own(G.tensor_tensor(nt[:, n], nt[:, n], one, ALU.add))
                    own.wait()
                    m1 = ct[:, K_M1 + n * C:K_M1 + (n + 1) * C].unsqueeze(1).broadcast_to([P, NCH, C])
                    own(G.tensor_tensor(mt[0:C, n, :, 0:C], nt[0:C, n, :, 0:C], m1[0:C], ALU.mult))
                    own.wait()
                    G.tensor_tensor(mt[C:P, n, :, C:P], nt[C:P, n, :, C:P], m1[C:P], ALU.mult).then_inc(ident_in, 1)
                    pool.wait_ge(ident_in, 2 * p + n + 1)
                if before:
                    pool.wait_ge(gated, p)
                keep_bonus(p)
                pool.wait_ge(bon_copied, p + 1)
                if after:
                    next_keys(a)
                    products(a, 0)
                    products(a, 1)

            next_keys(0)
            products(0, 0)
            products(0, 1)
            pair(0, False, True)
            own.loop_start()
            with pool.Fori(1, KT - 1) as p:
                pair(p, True, True)
                own.loop_end()
            pair(KT - 1, True, False)
            for m in range(2):
                low(m, m)
            square()
            post_norm(mix_out)
            u_pads()
            high_input(h_hi)
            mlp(False)
            post_norm(o_res)
            high_input(att_hi)
            for m in range(2 * KVH):
                low(w.n + m + 2, (m + 2) % NRAW)
            w.add(2 * KVH)
            for g in range(KVH):
                with pool.Fori(0, 2) as i:
                    for s in range(2):
                        low(w.n + 2 * i + s + 2, s)
                w.add(4, 2)
            square()
            post_norm(mix_out)
            u_pads()
            high_input(h_hi)
            mlp(True)
            post_norm(o_res)


def tiles(w):
    k, m = w.shape
    return w.reshape(k // P, P, m // P, P).transpose(2, 1, 0, 3)


def columns(v):
    return v.reshape(-1, P).T


def kernel(x_prompt, x_sample, c_prompt, c_sample, ada_w, ada_b, norm_g, rw_mu, rw_rkv, rw_w0, rw_wA, rw_wB,
           rw_a0, rw_aA, rw_aB, rw_gA, rw_gB, rw_kk, rw_ka, rw_rk, rw_lnx, rw_o, rw_v0, rw_vA, rw_vB,
           at_qkv, at_qk_g, at_o, ffn_up, ffn_conv_w, ffn_conv_b, ffn_down):
    import concourse.bacc as bacc
    from concourse.bass_utils import run_bass_kernel_spmd

    arr = lambda a: np.asarray(a)
    x = np.concatenate([arr(x_prompt), arr(x_sample)], 0)
    xT = x.transpose(2, 0, 1).reshape(KT, P, TOK).transpose(1, 0, 2)
    c = np.concatenate([arr(c_prompt), arr(c_sample)], 0)
    cT = c.T.reshape(KT, P, NSEQ).transpose(1, 0, 2)

    halfway = np.concatenate([np.arange(0, AH, 2), np.arange(1, AH, 2)])
    pair = np.stack([columns(a) for a in (arr(rw_w0)[0, 0], arr(rw_w0)[0, 1], arr(rw_a0)[0, 0], arr(rw_a0)[0, 1],
                                          arr(rw_kk)[0], arr(rw_ka)[0], arr(rw_rk)[0], arr(rw_lnx)[0, 0],
                                          arr(rw_lnx)[0, 1])], -1)
    cw, cb = arr(ffn_conv_w), arr(ffn_conv_b)
    ffc = np.concatenate([np.stack([columns(a) for a in (cw[l, 0], cw[l, 1], cw[l, 2], cb[l])], -1)
                          for l in range(DEPTH)], 1)
    params = np.concatenate([columns(arr(ada_b)), columns(arr(norm_g)), columns(arr(rw_mu)[0]),
                             pair.reshape(P, -1), arr(at_qk_g)[0][:, halfway].T, ffc.reshape(P, -1)], 1)

    aw = arr(ada_w).reshape(DEPTH, KT, P, 12, TOK).transpose(0, 3, 2, 1, 4).reshape(DEPTH * 4, 3, P, KT * TOK)
    rkv = [tiles(arr(rw_rkv)[0, n]).reshape(KT, P, D) for n in range(3)]
    second = [arr(w)[0].reshape(P, KT, P).transpose(1, 0, 2) for w in (rw_wB, rw_aB, rw_gB)]
    pair_w = np.concatenate(rkv + second[0:2], -1)
    first = [tiles(arr(w)[0].transpose(1, 0, 2).reshape(D, P))[0].reshape(P, D) for w in (rw_wA, rw_aA)]
    lora_a = np.concatenate(first + [tiles(arr(rw_gA)[0])[0].reshape(P, D)], -1)
    wo = tiles(arr(rw_o)[0]).reshape(KT, P, D)
    qkv = tiles(arr(at_qkv)[0]).reshape(12, P, D)
    swap = lambda w: w.reshape(w.shape[0], P, KT, P)[..., halfway].reshape(w.shape[0], P, D)
    at_kv = np.concatenate([swap(qkv[8:10]), qkv[10:12]])
    at_q = swap(qkv[0:8]).reshape(4, 2, P, D)
    ao = tiles(arr(at_o)[0]).reshape(KT, P, D)
    up = np.stack([tiles(arr(ffn_up)[l]).reshape(2, FT, P, D).transpose(1, 0, 2, 3).reshape(FT // 2, 4, P, D)
                   for l in range(DEPTH)])
    down = np.stack([tiles(arr(ffn_down)[l]).reshape(KT, P, 2, D_FF // 2).transpose(0, 2, 1, 3)
                     .reshape(KT // 2, 4, P, D_FF // 2) for l in range(DEPTH)])

    ins = dict(xT=xT, cT=cT, params=params, consts=constants(), ada_w=aw, lora_a=lora_a, pair_w=pair_w, gate_w=second[2], rw_o=wo,
               at_kv=at_kv, at_q=at_q, at_o=ao, ffn_up=up, ffn_down=down)
    nc = bacc.Bacc("TRN2", target_bir_lowering=False, num_devices=1)
    arrays, args = {}, {}
    for name, a in ins.items():
        a = np.ascontiguousarray(a)
        arrays[f"in_{name}"] = a
        args[name] = nc.dram_tensor(f"in_{name}", a.shape, mybir.dt.from_np(a.dtype), kind="ExternalInput").ap()
    yT = nc.dram_tensor("out_y", (P, KT, TOK), F32, kind="ExternalOutput").ap()
    encoder_trunk(nc, yT=yT, **args)
    r = run_bass_kernel_spmd(nc, [arrays], core_ids=[0])
    y = r.results[0]["out_y"].reshape(P, KT, NSEQ, SEQ).transpose(2, 3, 1, 0).reshape(NSEQ, SEQ, D)
    return y[0:1], y[1:2]
```
